# Optimizing a Trainium2 kernel written in Bass

```python
import math
import jax, jax.numpy as jnp
from jax import lax
import numpy as np

D_MODEL = 1024
BATCH = 1
SEQ = 512
DEPTH = 2

CONV_DIM = 1024
CONV_KERNEL = 31
D_INNER = 2 * D_MODEL
HEAD_DIM = 64
N_SSM_HEADS = D_INNER // HEAD_DIM
N_GROUPS = 8
D_STATE = 128
SSM_CONV = 5
CHUNK = 128
XBC_DIM = D_INNER + 2 * N_GROUPS * D_STATE
FFN_DIM = int(math.ceil(D_MODEL * 8 / 3 / 256) * 256)
PLE_DIM = 256
N_IN = 2 * CONV_DIM + 2 * D_MODEL + D_INNER + XBC_DIM + 2 * N_SSM_HEADS
DEEPNORM_ALPHA = (2 * DEPTH) ** 0.25
DEEPNORM_BETA = (8 * DEPTH) ** -0.25
LN_EPS = 1e-5
RMS_EPS = 1e-6

kernel_name = "hybrid_conformer_ssd_encoder"

def layer_norm(x, g, b):
    xf = x.astype(jnp.float32)
    mu = jnp.mean(xf, axis=-1, keepdims=True)
    var = jnp.mean(jnp.square(xf - mu), axis=-1, keepdims=True)
    return ((xf - mu) * lax.rsqrt(var + LN_EPS) * g + b).astype(x.dtype)

def rms_norm(x, g):
    xf = x.astype(jnp.float32)
    return (xf * lax.rsqrt(jnp.mean(jnp.square(xf), axis=-1, keepdims=True) + RMS_EPS) * g).astype(x.dtype)

def depthwise_conv_centred(u, w, b):
    pad = (w.shape[0] - 1) // 2
    out = lax.conv_general_dilated(
        u, w[:, None, :].astype(u.dtype), window_strides=(1,), padding=[(pad, pad)],
        dimension_numbers=("NWC", "WIO", "NWC"), feature_group_count=u.shape[-1])
    return out + b

def ssd_chunked(x, dt, A, Bm, Cm):
    b, s, h, p = x.shape
    g, n = Bm.shape[-2:]
    r = h // g
    c, l = s // CHUNK, CHUNK
    x = x.astype(jnp.float32)
    dt = dt.astype(jnp.float32)
    X = (x * dt[..., None]).reshape(b, c, l, g, r, p)
    Ad = (dt * A).reshape(b, c, l, g, r).transpose(0, 1, 3, 4, 2)
    Bc = Bm.astype(jnp.float32).reshape(b, c, l, g, n)
    Cc = Cm.astype(jnp.float32).reshape(b, c, l, g, n)
    A_cs = jnp.cumsum(Ad, axis=-1)
    idx = jnp.arange(l)
    lower = idx[:, None] >= idx[None, :]
    seg = A_cs[..., :, None] - A_cs[..., None, :]
    Lmat = jnp.exp(jnp.where(lower, seg, -jnp.inf))
    CB = jnp.einsum("bclgn,bcsgn->bcgls", Cc, Bc)
    y_diag = jnp.einsum("bcgrls,bcsgrp->bclgrp", CB[:, :, :, None] * Lmat, X)
    decay_states = jnp.exp(A_cs[..., -1:] - A_cs).transpose(0, 1, 4, 2, 3)
    states = jnp.einsum("bclgn,bclgrp->bcgrpn", Bc, X * decay_states[..., None])
    chunk_decay = jnp.exp(A_cs[..., -1])

    def step(carry, inp):
        st, dec = inp
        return carry * dec[..., None, None] + st, carry

    h0 = jnp.zeros((b, g, r, p, n), jnp.float32)
    _, prev = lax.scan(step, h0, (jnp.moveaxis(states, 1, 0), jnp.moveaxis(chunk_decay, 1, 0)))
    prev = jnp.moveaxis(prev, 0, 1)
    decay_out = jnp.exp(A_cs).transpose(0, 1, 4, 2, 3)
    y_off = jnp.einsum("bclgn,bcgrpn->bclgrp", Cc, prev) * decay_out[..., None]
    return (y_diag + y_off).reshape(b, s, h, p)

def conformer_branch(glu_in, conv_w, conv_b, ln_g, ln_b, w_out):
    a, gt = jnp.split(glu_in, 2, axis=-1)
    u = a * jax.nn.sigmoid(gt)
    u = depthwise_conv_centred(u, conv_w, conv_b)
    u = jax.nn.silu(layer_norm(u, ln_g, ln_b))
    return u @ w_out

def mamba2_bidir_branch(z, xbc, dt_raw, conv_w, conv_b, a_log, dt_bias, d_skip, norm_g, w_out):
    b, s, _ = z.shape
    xbc = jax.nn.silu(depthwise_conv_centred(xbc, conv_w, conv_b))
    xs, Bm, Cm = jnp.split(xbc, [D_INNER, D_INNER + N_GROUPS * D_STATE], axis=-1)
    xs = xs.reshape(b, s, N_SSM_HEADS, HEAD_DIM)
    Bm = Bm.reshape(b, s, N_GROUPS, D_STATE)
    Cm = Cm.reshape(b, s, N_GROUPS, D_STATE)
    dt_raw = dt_raw.astype(jnp.float32)
    dt_f = jax.nn.softplus(dt_raw[..., :N_SSM_HEADS] + dt_bias[0])
    dt_b = jax.nn.softplus(dt_raw[..., N_SSM_HEADS:] + dt_bias[1])
    A = -jnp.exp(a_log.astype(jnp.float32))
    y_f = ssd_chunked(xs, dt_f, A[0], Bm, Cm)
    flip = lambda t: jnp.flip(t, axis=1)
    y_b = flip(ssd_chunked(flip(xs), flip(dt_b), A[1], flip(Bm), flip(Cm)))
    y = y_f + y_b + xs.astype(jnp.float32) * d_skip[:, None]
    y = y.reshape(b, s, D_INNER) * jax.nn.silu(z.astype(jnp.float32))
    yg = y.reshape(b, s, N_GROUPS, D_INNER // N_GROUPS)
    yg = yg * lax.rsqrt(jnp.mean(jnp.square(yg), axis=-1, keepdims=True) + RMS_EPS)
    y = (yg.reshape(b, s, D_INNER) * norm_g).astype(z.dtype)
    return y @ w_out

def setup_inputs(seed: int = 0) -> dict:
    key = jax.random.key(seed)
    ks = iter(jax.random.split(key, 32))

    def nrm(shape, scale):
        return jax.random.normal(next(ks), shape, jnp.float32) * scale

    L = DEPTH
    dt0 = jnp.exp(jax.random.uniform(next(ks), (L, 2, N_SSM_HEADS)) * (math.log(0.1) - math.log(1e-3)) + math.log(1e-3))
    dt_bias = dt0 + jnp.log(-jnp.expm1(-dt0))
    a_log = jnp.log(jax.random.uniform(next(ks), (L, 2, N_SSM_HEADS), minval=1.0, maxval=16.0))
    return {
        "x": nrm((BATCH, SEQ, D_MODEL), 1.0),
        "p": nrm((DEPTH, BATCH, SEQ, PLE_DIM), 1.0),
        "w_in": nrm((L, D_MODEL, N_IN), D_MODEL ** -0.5),
        "conv_a_w": nrm((L, CONV_KERNEL, CONV_DIM), CONV_KERNEL ** -0.5),
        "conv_a_b": nrm((L, CONV_DIM), 0.02),
        "ln_a_g": 1.0 + nrm((L, CONV_DIM), 0.02),
        "ln_a_b": nrm((L, CONV_DIM), 0.02),
        "w_a_out": nrm((L, CONV_DIM, D_MODEL), CONV_DIM ** -0.5 * DEEPNORM_BETA),
        "ssm_conv_w": nrm((L, SSM_CONV, XBC_DIM), SSM_CONV ** -0.5),
        "ssm_conv_b": nrm((L, XBC_DIM), 0.02),
        "a_log": a_log,
        "dt_bias": dt_bias,
        "d_skip": 1.0 + nrm((L, N_SSM_HEADS), 0.02),
        "ssm_norm_g": 1.0 + nrm((L, D_INNER), 0.02),
        "w_b_out": nrm((L, D_INNER, D_MODEL), D_INNER ** -0.5 * DEEPNORM_BETA),
        "w_o": nrm((L, D_MODEL, D_MODEL), D_MODEL ** -0.5 * DEEPNORM_BETA),
        "ln1_g": 1.0 + nrm((L, D_MODEL), 0.02),
        "ln1_b": nrm((L, D_MODEL), 0.02),
        "w_gate_up": nrm((L, D_MODEL, 2 * FFN_DIM), D_MODEL ** -0.5),
        "w_down": nrm((L, FFN_DIM, D_MODEL), FFN_DIM ** -0.5 * DEEPNORM_BETA),
        "ln2_g": 1.0 + nrm((L, D_MODEL), 0.02),
        "ln2_b": nrm((L, D_MODEL), 0.02),
        "w_ple": nrm((L, PLE_DIM, D_MODEL), PLE_DIM ** -0.5 * DEEPNORM_BETA),
        "ple_norm_g": 1.0 + nrm((L, D_MODEL), 0.02),
        "w_ple_gate": nrm((L, D_MODEL, D_MODEL), D_MODEL ** -0.5),
    }

def reference(x, p, w_in, conv_a_w, conv_a_b, ln_a_g, ln_a_b, w_a_out, ssm_conv_w, ssm_conv_b,
              a_log, dt_bias, d_skip, ssm_norm_g, w_b_out, w_o, ln1_g, ln1_b, w_gate_up, w_down,
              ln2_g, ln2_b, w_ple, ple_norm_g, w_ple_gate):
    cuts = [2 * CONV_DIM, 2 * CONV_DIM + 2 * D_MODEL, 2 * CONV_DIM + 2 * D_MODEL + D_INNER,
            2 * CONV_DIM + 2 * D_MODEL + D_INNER + XBC_DIM]
    for i in range(DEPTH):
        proj = x @ w_in[i]
        glu_in, gates, z, xbc, dt_raw = jnp.split(proj, cuts, axis=-1)
        gate_a, gate_b = jnp.split(gates, 2, axis=-1)
        y_a = conformer_branch(glu_in, conv_a_w[i], conv_a_b[i], ln_a_g[i], ln_a_b[i], w_a_out[i])
        y_b = mamba2_bidir_branch(z, xbc, dt_raw, ssm_conv_w[i], ssm_conv_b[i], a_log[i],
                                  dt_bias[i], d_skip[i], ssm_norm_g[i], w_b_out[i])
        merged = jax.nn.sigmoid(gate_a) * y_a + jax.nn.sigmoid(gate_b) * y_b
        h = layer_norm(DEEPNORM_ALPHA * x + merged @ w_o[i], ln1_g[i], ln1_b[i])
        g_, u_ = jnp.split(h @ w_gate_up[i], 2, axis=-1)
        h2 = layer_norm(DEEPNORM_ALPHA * h + (jax.nn.silu(g_) * u_) @ w_down[i], ln2_g[i], ln2_b[i])
        e = rms_norm(p[i] @ w_ple[i], ple_norm_g[i])
        x = h2 + e * jax.nn.sigmoid(h2 @ w_ple_gate[i])
    return x


_drawn_inputs = setup_inputs


def setup_inputs(seed=0):
    import zlib

    import numpy as np

    out = dict(_drawn_inputs(seed))
    spreads = {}
    factors = {'conv_a_b': 8.0,
     'ln_a_g': 64.0,
     'ln_a_b': 64.0,
     'ssm_conv_b': 8.0,
     'd_skip': 64.0,
     'ssm_norm_g': 64.0,
     'ple_norm_g': 11.851,
     'ln1_g': 4.615,
     'ln1_b': 4.337,
     'ln2_g': 4.629,
     'ln2_b': 4.435}
    for name, (base, spread) in spreads.items():
        noise = np.random.default_rng([zlib.crc32(name.encode()), seed]).standard_normal(out[name].shape)
        drawn = base * np.exp(spread * noise) if base else spread * noise
        out[name] = __import__('jax').numpy.asarray(drawn.astype(out[name].dtype))
    for name, factor in factors.items():
        out[name] = (out[name] * factor).astype(out[name].dtype)
    return out
```

```python
import concourse.bass as bass
from concourse import mybir
from contextlib import ExitStack
import math

F32 = mybir.dt.float32
F32R = mybir.dt.float32r
ALU = mybir.AluOpType
ACT = mybir.ActivationFunctionType

D, T, LAYERS, CONV_A, HEADS, GROUPS, STATE, HEAD = 1024, 512, 2, 31, 32, 8, 128, 64
INNER, FFN, PLE, TAPS = 2048, 2816, 256, 5
P = 128
KT = D // P
CH = T // P
HG = HEADS // GROUPS
GW = INNER // GROUPS
ALPHA = (2 * LAYERS) ** 0.25
LN_EPS, RMS_EPS = 1e-5, 1e-6
SLOTS = 4
WT = KT * P

PAIRS = GROUPS // 2
PAIR_CYCLES = 6
C_GATE_A = PAIRS * PAIR_CYCLES
C_GATE_B = C_GATE_A + KT // SLOTS
C_A_OUT = C_GATE_B + KT // SLOTS
C_O = C_A_OUT + KT // SLOTS
C_UP0 = C_O + KT // SLOTS
C_UP1 = C_UP0 + 2 * KT // SLOTS
C_DOWN0 = C_UP1 + 2 * KT // SLOTS
FT = FFN // P
LAST = FT - 2 * KT
C_UP2 = C_DOWN0 + KT // SLOTS
C_DOWN1 = C_UP2 + 2 * LAST // SLOTS
C_DOWN2 = C_DOWN1 + KT // SLOTS
C_PLE = C_DOWN2 + KT // SLOTS
CYCLES = C_PLE + KT // SLOTS
ALL_CYCLES = LAYERS * CYCLES + 1

O_CAW = 0
CP = CONV_A + 1
GP = 4 * TAPS + 4 + 2
O_GRP = O_CAW + KT * CP
O_LNA = O_GRP + GROUPS * GP
O_LN1 = O_LNA + 2 * KT
O_LN2 = O_LN1 + 2 * KT
O_PLE = O_LN2 + 2 * KT
O_DTB = O_PLE + KT
O_ALOG = O_DTB + 2 * HEADS
O_DSK = O_ALOG + 2 * HEADS
NPAR = O_DSK + HEADS
DTK, ADT, WDEC, DOUT, TOT = range(5)
BWD, FWD = 0, 1
LN_A, LN_1, LN_2 = range(3)
NORMS = 3
CONSTS = 15
LOG_TERMS = 8


def build(nc, x_in, p_in, w_stream, w_dt, w_ple, par_in, out):
    ctx = ExitStack()
    with ctx:
        def sb(name, shape, dtype=F32, where=None):
            return (where or ctx).enter_context(nc.sbuf_tensor(name, shape, dtype))

        def sem(name):
            return ctx.enter_context(nc.semaphore(name))

        xh = sb("x_hi", [P, KT, T], F32R)
        xl = sb("x_lo", [P, KT, T], F32R)
        raw = sb("w_raw", [P, 2, WT])
        whi = sb("w_hi", [P, SLOTS, WT], F32R)
        wlo = sb("w_lo", [P, SLOTS, WT], F32R)
        u = sb("glu_out", [P, 2, T])
        za = sb("z_a", [P, KT, T])
        zb = sb("z_b", [P, KT, T])
        sg = sb("sigmoids", [P, T])
        par = sb("params", [P, NPAR])
        steps = sb("steps", [P, 5, 2, CH, HEADS])
        gtab = sb("group_steps", [P, 2, 5 * 2 * CH, HG])
        gpar = sb("group_params", [P, 2, GP])
        gdsk = sb("group_skip", [P, 2, HG])
        nega = sb("neg_a", [P, 2 * HEADS])
        U = sb("tri_le", [P, P])
        LW = sb("tri_ge", [P, P])
        SL = sb("tri_gt", [P, P])
        SU = sb("tri_lt", [P, P])
        ones = sb("ones", [P, P])
        mean1 = sb("ones_over_d", [P, P])
        ident = sb("ident", [P, P])
        neghalf = sb("neg_half", [P, CH])
        ms = sb("mean_squares", [P, CH])
        mse = sb("mean_squares_eps", [P, CH])
        rst = sb("group_rstd", [P, CH])

        caw = sb("conv_a_params", [P, 2, CP])
        eps = sb("eps", [P, 2])

        with ExitStack() as r:
            cin = sb("conv_in", [P, 4, T], F32, r)
            acc = sb("conv_acc", [P, 2, T], F32, r)
            feat = sb("xs_b_c", [P, 4, T], F32, r)
            xtok = sb("x_tok", [P, CH, GW], F32, r)
            btok = sb("b_tok", [P, CH, STATE], F32, r)
            ztok = sb("z_tok", [P, 2, T], F32, r)
            E = sb("decay", [P, CH, HG, P], F32, r)
            rhs = sb("seg_rhs", [P, 2, HG, P], F32, r)
            cb = sb("cb_masked", [P, 2, CH, P], F32, r)
            xw = sb("x_weighted", [P, 2, 2, GW], F32, r)
            H = sb("states", [P, CH * 2, GW], F32, r)
            y = sb("y_tok", [P, CH, GW], F32, r)
            tm = sb("tmp_m", [P, HG, P], F32, r)
            ty = sb("tmp_y", [P, 2, GW], F32, r)
            junk = sb("squares", [P, GW], F32, r)
        with ExitStack() as r:
            aah = sb("act_a_hi", [P, KT, T], F32R, r)
            aal = sb("act_a_lo", [P, KT, T], F32R, r)
            with ExitStack() as r_b:
                abh = sb("act_b_hi", [P, KT, T], F32R, r_b)
                abl = sb("act_b_lo", [P, KT, T], F32R, r_b)
            with ExitStack() as r_b:
                pin = sb("ple_p", [P, 2, T], F32, r_b)
                wpl = sb("w_ple_in", [P, 2, D], F32, r_b)
            sb("act_b_place", [P, 2 * KT, T], F32, r)
            rstd = sb("rstd", [P, T], F32, r)
        sb("region_1", [P, 33 * T + GW])
        with ExitStack() as r:
            yh = sb("y_hi", [P, 4, T], F32R, r)
            yl = sb("y_lo", [P, 4, T], F32R, r)
        ge = sb("gate_or_e", [P, KT, T])
        stepf = steps[:, :, :, :, :].rearrange("p k d c h -> p k (d c h)")
        tmf = tm[:, :, :].rearrange("p a b -> p (a b)")
        tyf = ty[:, :, :].rearrange("p a b -> p (a b)")

        bank = [ctx.enter_context(nc.psum_tensor(f"bank{b}", [P, T], F32)) for b in range(8)]

        def halves(b):
            return b[:, :].rearrange("p (c e) -> p c e", c=2)

        def quarters(b):
            return b[:, :].rearrange("p (c e) -> p c e", c=4)

        raw_ready = [sem(f"raw_ready{s}") for s in range(SLOTS)]
        hi_done = [sem(f"hi_done{s}") for s in range(SLOTS)]
        lo_done = [sem(f"lo_done{s}") for s in range(SLOTS)]
        used = [sem(f"used{s}") for s in range(SLOTS)]
        evac = [sem(f"evac{s}") for s in range(SLOTS)]
        consts = sem("consts")
        x_loaded = sem("x_loaded")
        par_loaded = sem("par_loaded")
        p_loaded = sem("p_loaded")
        ple_loaded = sem("ple_loaded")
        dtw_loaded = sem("dtw_loaded")
        out_stored = sem("out_stored")
        xh_done = sem("xh_done")
        xl_done = sem("xl_done")
        zb_zero = sem("zb_zero")
        dtw_hi = sem("dtw_hi")
        dtw_lo = sem("dtw_lo")
        dt_done = sem("dt_done")
        dt_v = sem("dt_v")
        dt_e = sem("dt_e")
        ad_ready = sem("ad_ready")
        cum_done = sem("cum_done")
        cum_exp = sem("cum_exp")
        nega_e = sem("nega_e")
        grp_ready = sem("grp_ready")
        conv_done = sem("conv_done")
        silu_done = sem("silu_done")
        tr_done = sem("tr_done")
        tok_evac = sem("tok_evac")
        cb_done = sem("cb_done")
        xw_ready = sem("xw_ready")
        seg_done = sem("seg_done")
        rhs_ready = sem("rhs_ready")
        exp_done = sem("exp_done")
        st_done = sem("st_done")
        st_evac = sem("st_evac")
        h_ready = sem("h_ready")
        m_ready = sem("m_ready")
        yo_done = sem("yo_done")
        xd_ready = sem("xd_ready")
        yp_read = sem("yp_read")
        yg_ready = sem("yg_ready")
        ss_done = sem("ss_done")
        rms_done = sem("rms_done")
        yn_ready = sem("yn_ready")
        yt_done = sem("yt_done")
        yh_done = sem("yh_done")
        yl_done = sem("yl_done")
        ua_ready = sem("ua_ready")
        mean_done = sem("mean_done")
        xc_ready = sem("xc_ready")
        sq_ready = sem("sq_ready")
        sq_used = sem("sq_used")
        std_ready = sem("std_ready")
        zn_ready = sem("zn_ready")
        zf_ready = sem("zf_ready")
        zh_ready = sem("zh_ready")
        al_done = sem("al_done")
        bh_done = sem("bh_done")
        bl_done = sem("bl_done")
        gb_ready = sem("gb_ready")
        mg_ready = sem("mg_ready")
        z1_ready = sem("z1_ready")
        fh_done = sem("fh_done")
        fl_done = sem("fl_done")
        e_done = sem("e_done")
        e_evac = sem("e_evac")
        esq_ready = sem("esq_ready")
        esq_used = sem("esq_used")
        estd_ready = sem("estd_ready")
        en_ready = sem("en_ready")
        ef_ready = sem("ef_ready")
        pg_used = sem("pg_used")
        xn_ready = sem("xn_ready")
        dve_order = sem("dve_order")
        settled = sem("settled")
        EARLY = 2

        def seen(n):
            return n + EARLY

        def settle(e):
            e.sem_inc(settled, 1)

        def open_(e, *ss):
            for s in ss:
                e.sem_inc(s, EARLY)

        block = ctx.enter_context(nc.Block())

        @block.sync
        def _(sp):
            def tile(cyc, s):
                sp.wait_ge(lo_done[(s + 2) % SLOTS], seen(cyc + (1 if s >= 2 else 0)))
                sp.dma_start(raw[:, s % 2, :], w_stream[cyc, s]).then_inc(raw_ready[s], 16)

            sp.dma_start(zb[:, :, :], x_in).then_inc(x_loaded, 16)
            sp.dma_start(raw[:, 0, :], w_stream[0, 0]).then_inc(raw_ready[0], 16)
            sp.dma_start(raw[:, 1, :], w_stream[0, 1]).then_inc(raw_ready[1], 16)
            tile(0, 2)
            tile(0, 3)
            with sp.Fori(1, ALL_CYCLES) as cyc:
                for s in range(SLOTS):
                    tile(cyc, s)
            sp.wait_ge(xn_ready, seen(LAYERS * KT))
            sp.dma_start(out, zb[:, :, :]).then_inc(out_stored, 16)
            sp.wait_ge(out_stored, 16)

        @block.gpsimd
        def _(gp):
            open_(gp, rhs_ready, xd_ready, rms_done, zb_zero, *lo_done)

            def lo(cyc, *slots):
                for s in slots:
                    gp.wait_ge(hi_done[s], seen(cyc + 1))
                    gp.tensor_tensor(wlo[:, s, :], raw[:, s % 2, :], whi[:, s, :].bitcast(F32),
                                     ALU.subtract).then_inc(lo_done[s], 1)

            def masked_steps(q, G, c):
                gp.wait_ge(seg_done, seen(CH * G + c))
                g = gtab[:, q, :, :].rearrange("p (k d c) h -> p k d c h", k=5, d=2)
                for d, m in ((FWD, U), (BWD, LW)):
                    ad = g[:, ADT, d, c, :].unsqueeze(2).broadcast_to([P, HG, P])
                    i = gp.tensor_tensor(rhs[:, d], ad, m[:, :].unsqueeze(1).broadcast_to([P, HG, P]), ALU.mult)
                i.then_inc(rhs_ready, 1)

            def skip(q, G):
                gp.wait_ge(tok_evac, seen(3 * G + 2))
                gp.wait_ge(yt_done, seen(2 * G))
                d = gdsk[:, q, :].unsqueeze(1).unsqueeze(3).broadcast_to([P, CH, HG, HEAD])
                v = "p c (h e) -> p c h e"
                gp.tensor_tensor(y[:, :, :].rearrange(v, h=HG), xtok[:, :, :].rearrange(v, h=HG), d,
                                 ALU.mult).then_inc(xd_ready, 1)

            def group_rms(G):
                gp.wait_ge(ss_done, seen(CH * (G + 1)))
                gp.wait_ge(yn_ready, seen(G))
                settle(gp)
                gp.tensor_scalar(mse[:, :], ms[:, :], RMS_EPS, None, ALU.add).then_inc(rms_done, 1)
                gp.wait_ge(rms_done, seen(2 * G + 1))
                gp.tensor_tensor(rst[:, :], mse[:, :], neghalf[:, :], ALU.pow).then_inc(rms_done, 1)

            n = [0]

            def fill(dst, pattern=None, value=1.0):
                gp.memset(dst, value).then_inc(consts, 1)
                n[0] += 1
                if pattern:
                    gp.wait_ge(consts, n[0])
                    base, mult, step, op = pattern
                    gp.affine_select(out=dst, in_=dst, compare_op=op, fill=0.0, base=base,
                                     pattern=[[step, P]], channel_multiplier=mult).then_inc(consts, 1)
                    n[0] += 1

            fill(ones[:, :])
            fill(eps[:, 0:1], value=LN_EPS)
            fill(eps[:, 1:2], value=RMS_EPS)
            fill(mean1[:, :], value=1.0 / D)
            fill(neghalf[:, :], value=-0.5)
            fill(U[:, :], (0, -1, 1, ALU.is_ge))
            fill(LW[:, :], (0, 1, -1, ALU.is_ge))
            fill(SL[:, :], (0, 1, -1, ALU.is_gt))
            fill(SU[:, :], (0, -1, 1, ALU.is_gt))
            fill(ident[:, :], (0, 1, -1, ALU.is_equal))
            assert n[0] == CONSTS
            lo(0, 0, 1, 2, 3)
            with gp.Fori(0, LAYERS) as L:
                base = L * CYCLES
                gp.wait_ge(xl_done, seen(NORMS * KT * L + KT))
                settle(gp)
                gp.memset(zb[:, :, :], 0.0).then_inc(zb_zero, 1)
                with gp.Fori(0, PAIRS) as j:
                    c0 = base + j * PAIR_CYCLES
                    G0 = L * GROUPS + j * 2
                    lo(c0 + 1, 0, 1, 2, 3)
                    gp.wait_ge(grp_ready, seen(G0 + 1))
                    masked_steps(0, G0, 0)
                    lo(c0 + 2, 0)
                    masked_steps(0, G0, 1)
                    lo(c0 + 2, 1)
                    masked_steps(0, G0, 2)
                    masked_steps(0, G0, 3)
                    skip(0, G0)
                    lo(c0 + 2, 2, 3)
                    group_rms(G0)
                    lo(c0 + 3, 0, 1)
                    gp.wait_ge(grp_ready, seen(G0 + 2))
                    masked_steps(1, G0 + 1, 0)
                    lo(c0 + 3, 2)
                    masked_steps(1, G0 + 1, 1)
                    lo(c0 + 3, 3)
                    masked_steps(1, G0 + 1, 2)
                    masked_steps(1, G0 + 1, 3)
                    skip(1, G0 + 1)
                    lo(c0 + 4, 0, 1)
                    group_rms(G0 + 1)
                    lo(c0 + 4, 2, 3)
                    lo(c0 + 5, 0, 1, 2, 3)
                    lo(c0 + 6, 0, 1, 2, 3)
                with gp.Fori(C_GATE_A, CYCLES) as c:
                    lo(base + c + 1, 0, 1, 2, 3)

        @block.scalar
        def _(act):
            open_(act, xh_done, silu_done, tok_evac, exp_done, st_evac, ss_done, yh_done,
                  sq_ready, std_ready, zf_ready, zh_ready, bh_done, fh_done,
                  e_evac, esq_ready, estd_ready, ef_ready, dt_e, cum_exp, nega_e,
                  dtw_hi, *hi_done)

            def hi(cyc, *slots):
                for s in slots:
                    act.wait_ge(raw_ready[s], (cyc + 1) * 16)
                    act.wait_ge(used[s], seen(cyc))
                    act.activation(whi[:, s, :], raw[:, s % 2, :], ACT.Copy).then_inc(hi_done[s], 1)

            def take(cyc, s, dst, func=ACT.Copy):
                act.wait_ge(used[s], seen(cyc + 1))
                act.activation(dst, bank[s][:, :], func).then_inc(evac[s], 1)

            def conv_inputs(q, G, tiles):
                act.wait_ge(conv_done, seen(4 * G))
                for c, (cyc, s) in enumerate(tiles):
                    take(cyc, s, cin[:, c, :])
                    hi(cyc + 1, s)

            def z_gates(G, cyc, slots):
                act.wait_ge(yg_ready, seen(CH * G))
                for i, s in enumerate(slots):
                    take(cyc, s, ztok[:, i, :], ACT.Silu)
                    hi(cyc + 1, s)

            def silus(G):
                act.wait_ge(yo_done, seen(CH * G))
                for c in range(4):
                    act.wait_ge(conv_done, seen(4 * G + c + 1))
                    act.activation(feat[:, c, :], acc[:, c % 2, :], ACT.Silu).then_inc(silu_done, 1)

            def scan_a(G):
                act.wait_ge(xd_ready, seen(G))
                for i in range(2):
                    act.wait_ge(tr_done, seen(4 * G + i + 1))
                    act.activation(xtok[:, 2 * i:2 * i + 2, :], halves(bank[6 + i]), ACT.Copy).then_inc(tok_evac, 1)
                act.wait_ge(tr_done, seen(4 * G + 3))
                act.activation(btok[:, :, :], quarters(bank[6]), ACT.Copy).then_inc(tok_evac, 1)

                def decay(c):
                    act.wait_ge(seg_done, seen(CH * G + c + 1))
                    act.activation(E[:, c], quarters(bank[4 + c % 2]), ACT.Exp).then_inc(exp_done, 1)

                def state(n):
                    act.wait_ge(st_done, seen(3 * G + n + 1))
                    dst = (H[:, 3:5, :], H[:, 0:6:5, :], H[:, 2:8:5, :])[n]
                    act.activation(dst, halves(bank[6]), ACT.Copy).then_inc(st_evac, 1)

                decay(0)
                decay(1)
                state(0)
                decay(2)
                state(1)
                decay(3)
                state(2)

            def scan_b(q, G):
                for c in range(CH):
                    act.wait_ge(yg_ready, seen(CH * G + c + 1))
                    act.activation(junk[:, :], y[:, c, :], ACT.Square, scale=GW ** -0.5,
                                   accum_out=ms[:, c:c + 1]).then_inc(ss_done, 1)
                    act.wait_ge(ss_done, seen(CH * G + c + 1))
                for i in range(2):
                    act.wait_ge(yt_done, seen(2 * G + i + 1))
                    act.activation(yh[:, 2 * q + i, :], bank[4 + i][:, :], ACT.Copy,
                                   scale=gpar[:, q, 24 + i:25 + i]).then_inc(yh_done, 1)

            def norm(L, kind, z, hi_dst, off, func):
                k = NORMS * L + kind
                for m in range(KT):
                    act.wait_ge(xc_ready, seen(k * KT + m + 1))
                    if m >= 2:
                        act.wait_ge(sq_used, seen(k * KT + m - 1))
                    act.activation(u[:, m % 2, :], z[:, m, :], ACT.Square).then_inc(sq_ready, 1)
                act.wait_ge(sq_used, seen(KT * (k + 1)))
                act.activation(rstd[:, :], bank[5][:, :], ACT.Sqrt, bias=eps[:, 0:1]).then_inc(std_ready, 1)
                for m in range(KT + 1):
                    if m < KT:
                        act.wait_ge(zn_ready, seen(k * KT + m + 1))
                        act.activation(z[:, m, :], z[:, m, :], func, scale=par[:, off + m:off + m + 1],
                                       bias=par[:, off + KT + m:off + KT + m + 1]).then_inc(zf_ready, 1)
                    if m >= 1:
                        act.wait_ge(zf_ready, seen(k * KT + m))
                        act.activation(hi_dst[:, m - 1, :], z[:, m - 1, :], ACT.Copy).then_inc(zh_ready, 1)

            act.wait_ge(consts, CONSTS)
            hi(0, 0, 1, 2, 3)
            with act.Fori(0, LAYERS) as L:
                base = L * CYCLES
                act.wait_ge(xn_ready, seen(KT * L))
                act.dma_start(par[:, :], par_in[L]).then_inc(par_loaded, 16)
                act.dma_start(tmf, w_dt[L]).then_inc(dtw_loaded, 16)
                act.wait_ge(x_loaded, 16)
                for m in range(KT):
                    act.activation(xh[:, m, :], zb[:, m, :], ACT.Copy).then_inc(xh_done, 1)
                act.wait_ge(dtw_loaded, 16 * (L + 1))
                act.activation(yh[:, 0, :], tmf, ACT.Copy).then_inc(dtw_hi, 1)
                act.wait_ge(par_loaded, 16 * (L + 1))
                act.activation(nega[:, :], par[:, O_ALOG:O_ALOG + 2 * HEADS], ACT.Exp).then_inc(nega_e, 1)
                act.wait_ge(dt_v, seen(L + 1))
                act.activation(ty[:, 1, :], ty[:, 0, :], ACT.Abs).then_inc(dt_e, 1)
                act.wait_ge(dt_e, seen(2 * L + 1))
                act.activation(ty[:, 1, :], ty[:, 1, :], ACT.Exp, scale=-1.0).then_inc(dt_e, 1)
                act.wait_ge(cum_done, seen(L + 1))
                act.activation(stepf[:, WDEC:DOUT + 1, :], halves(bank[5]), ACT.Exp).then_inc(cum_exp, 1)
                act.activation(stepf[:, TOT, :], bank[6][:, 0:GW], ACT.Exp).then_inc(cum_exp, 1)
                with act.Fori(0, PAIRS) as j:
                    c0 = base + j * PAIR_CYCLES
                    G0 = L * GROUPS + j * 2
                    conv_inputs(0, G0, [(c0, 0), (c0, 1), (c0, 2), (c0, 3)])
                    z_gates(G0, c0 + 1, (0, 1))
                    silus(G0)
                    scan_a(G0)
                    conv_inputs(1, G0 + 1, [(c0 + 1, 2), (c0 + 1, 3), (c0 + 2, 0), (c0 + 2, 1)])
                    scan_b(0, G0)
                    z_gates(G0 + 1, c0 + 2, (2, 3))
                    silus(G0 + 1)
                    scan_a(G0 + 1)
                    take(c0 + 3, 1, sg[:, :], ACT.Sigmoid)
                    hi(c0 + 4, 0, 1)
                    scan_b(1, G0 + 1)
                    act.wait_ge(evac[0], seen(c0 + 4))
                    take(c0 + 3, 3, sg[:, :], ACT.Sigmoid)
                    hi(c0 + 4, 2, 3)
                    hi(c0 + 5, 0, 1, 2, 3)
                    hi(c0 + 6, 0, 1, 2, 3)
                act.wait_ge(yl_done, seen(2 * GROUPS * (L + 1)))
                settle(act)
                with act.Fori(0, KT // SLOTS) as i:
                    for s in range(SLOTS):
                        take(base + C_GATE_A + i, s, ge[:, SLOTS * i + s, :], ACT.Sigmoid)
                        hi(base + C_GATE_A + i + 1, s)
                norm(L, LN_A, za, aah, O_LNA, ACT.Silu)
                with act.Fori(0, KT // SLOTS) as i:
                    for s in range(SLOTS):
                        act.wait_ge(gb_ready, seen(KT * L + SLOTS * i + s))
                        take(base + C_GATE_B + i, s, sg[:, :], ACT.Sigmoid)
                        hi(base + C_GATE_B + i + 1, s)
                with act.Fori(0, KT // SLOTS) as i:
                    for s in range(SLOTS):
                        act.wait_ge(mg_ready, seen(KT * L + SLOTS * i + s + 1))
                        act.activation(abh[:, SLOTS * i + s, :], zb[:, SLOTS * i + s, :], ACT.Copy).then_inc(bh_done, 1)
                        hi(base + C_A_OUT + i + 1, s)
                with act.Fori(C_O, C_UP0) as c:
                    hi(base + c + 1, 0, 1, 2, 3)
                norm(L, LN_1, za, xh, O_LN1, ACT.Identity)

                def swiglu(c0, count, dst):
                    with act.Fori(0, count // 2) as i:
                        for r in range(2):
                            take(c0 + i, 2 * r, sg[:, :], ACT.Silu)
                            hi(c0 + i + 1, 2 * r)
                            act.wait_ge(evac[2 * r + 1], seen(c0 + i + 1))
                            act.activation(dst[:, 2 * i + r, :], u[:, r, :], ACT.Copy).then_inc(fh_done, 1)
                            hi(c0 + i + 1, 2 * r + 1)

                swiglu(base + C_UP0, KT, aah)
                swiglu(base + C_UP1, KT, abh)
                with act.Fori(C_DOWN0, C_UP2) as c:
                    hi(base + c + 1, 0, 1, 2, 3)
                swiglu(base + C_UP2, LAST, aah)
                with act.Fori(C_DOWN1, C_DOWN2) as c:
                    hi(base + c + 1, 0, 1, 2, 3)
                act.wait_ge(used[3], seen(base + C_DOWN2))
                act.dma_start(pin[:, :, :], p_in[L]).then_inc(p_loaded, 16)
                act.dma_start(wpl[:, :, :], w_ple[L]).then_inc(ple_loaded, 16)
                with act.Fori(C_DOWN2, C_PLE) as c:
                    hi(base + c + 1, 0, 1, 2, 3)
                for m in range(KT):
                    act.wait_ge(e_done, seen(KT * L + m + 1))
                    act.activation(ge[:, m, :], bank[4 + m % 4][:, :], ACT.Copy).then_inc(e_evac, 1)
                norm(L, LN_2, zb, xh, O_LN2, ACT.Identity)
                for m in range(KT):
                    act.wait_ge(e_evac, seen(KT * L + m + 1))
                    if m >= 2:
                        act.wait_ge(esq_used, seen(KT * L + m - 1))
                    act.activation(u[:, m % 2, :], ge[:, m, :], ACT.Square).then_inc(esq_ready, 1)
                act.wait_ge(esq_used, seen(KT * (L + 1)))
                act.activation(rstd[:, :], bank[6][:, :], ACT.Sqrt, bias=eps[:, 1:2]).then_inc(estd_ready, 1)
                for m in range(KT):
                    act.wait_ge(en_ready, seen(KT * L + m + 1))
                    act.activation(ge[:, m, :], ge[:, m, :], ACT.Copy,
                                   scale=par[:, O_PLE + m:O_PLE + m + 1]).then_inc(ef_ready, 1)
                with act.Fori(0, KT // SLOTS) as i:
                    for s in range(SLOTS):
                        act.wait_ge(pg_used, seen(KT * L + SLOTS * i + s))
                        take(base + C_PLE + i, s, sg[:, :], ACT.Sigmoid)
                        hi(base + C_PLE + i + 1, s)

        @block.tensor
        def _(pe):
            open_(pe, dt_done, cum_done, tr_done, seg_done, st_done, yo_done, yt_done,
                  mean_done, sq_used, e_done, esq_used, *used)

            def three(dst, wh, wl, mh, ml, first, last):
                pe.matmul(dst, wh, mh, start=first, stop=False)
                pe.matmul(dst, wh, ml, start=False, stop=False)
                return pe.matmul(dst, wl, mh, start=False, stop=last)

            def slot_ready(cyc, s):
                pe.wait_ge(lo_done[s], seen(cyc + 1))
                pe.wait_ge(evac[s], seen(cyc))

            def dense(cyc, s, mh, ml, nk=KT):
                slot_ready(cyc, s)
                for k in range(nk):
                    w = slice(k * P, (k + 1) * P)
                    i = three(bank[s][:, :], whi[:, s, w], wlo[:, s, w], mh[:, k, :], ml[:, k, :],
                              k == 0, k == nk - 1)
                i.then_inc(used[s], 1)

            def z_tiles(cyc, s):
                slot_ready(cyc, s)
                slot_ready(cyc, s + 1)
                for c in range(CH):
                    dst = halves(bank[s + c // 2])[:, c % 2, :].rearrange("p (b e) -> p b e", b=2)
                    for k in range(KT):
                        t, w = slice(c * P, (c + 1) * P), slice(k * P, (k + 1) * P)
                        h, l, end = whi[:, s:s + 2, w], wlo[:, s:s + 2, w], k == KT - 1
                        pe.matmul(dst, xh[:, k, t], h, start=k == 0, stop=False)
                        pe.matmul(dst, xh[:, k, t], l, start=False, stop=False)
                        if c < CH - 1 or not end:
                            pe.matmul(dst, xl[:, k, t], h, start=False, stop=end)
                        else:
                            pe.matmul(dst[:, 0], xl[:, k, t], h[:, 0], start=False, stop=False).then_inc(used[s], 1)
                            pe.matmul(dst[:, 1], xl[:, k, t], h[:, 1], start=False, stop=end).then_inc(used[s + 1], 1)

            def scan_a(G):
                for i in range(2):
                    pe.wait_ge(silu_done, seen(4 * G + 2))
                    pe.wait_ge(yp_read, seen(CH * G))
                    for n in range(4):
                        c, t = 2 * i + n // 2, n % 2
                        q = pe.transpose(bank[6 + i][:, n * P:(n + 1) * P], feat[:, t, c * P:(c + 1) * P], ident[:, :])
                    q.then_inc(tr_done, 1)
                pe.wait_ge(silu_done, seen(4 * G + 3))
                pe.wait_ge(tok_evac, seen(3 * G + 1))
                for c in range(CH):
                    q = pe.transpose(bank[6][:, c * P:(c + 1) * P], feat[:, 2, c * P:(c + 1) * P], ident[:, :])
                q.then_inc(tr_done, 1)
                pe.wait_ge(silu_done, seen(4 * G + 4))
                pe.wait_ge(tok_evac, seen(3 * G + 2))
                for c in range(CH):
                    t = slice(c * P, (c + 1) * P)
                    q = pe.matmul(bank[7][:, t], feat[:, 2, t], feat[:, 3, t], start=True, stop=True)
                q.then_inc(tr_done, 1)

                def exponent(c):
                    pe.wait_ge(rhs_ready, seen(CH * G + c + 1))
                    if c < 2:
                        pe.wait_ge(yl_done, seen(2 * G))
                    else:
                        pe.wait_ge(exp_done, seen(CH * G + c - 1))
                    b = quarters(bank[4 + c % 2])
                    pe.matmul(b, SL[:, :], rhs[:, FWD], start=True, stop=False)
                    pe.matmul(b, SU[:, :], rhs[:, BWD], start=False, stop=True).then_inc(seg_done, 1)

                def state(n):
                    pe.wait_ge(xw_ready, seen(3 * G + n + 1))
                    pe.wait_ge(tok_evac, seen(3 * G + 3))
                    pe.wait_ge(st_evac, seen(3 * G + n))
                    if n == 0:
                        pe.matmul(bank[6][:, 0:GW], btok[:, 0, :], xw[:, 0, 0, :], start=True, stop=True)
                        q = pe.matmul(bank[6][:, GW:], btok[:, CH - 1, :], xw[:, 0, 1, :], start=True, stop=True)
                    else:
                        q = pe.matmul(halves(bank[6]), btok[:, n, :], xw[:, n % 2], start=True, stop=True)
                    q.then_inc(st_done, 1)

                exponent(0)
                exponent(1)
                state(0)
                exponent(2)
                state(1)
                exponent(3)
                state(2)

            def scan_b(G):
                for c in range(CH):
                    pe.wait_ge(m_ready, seen(CH * G + c + 1))
                    if c == 0:
                        pe.wait_ge(st_evac, seen(3 * G + 3))
                    elif c == 1:
                        pe.wait_ge(cb_done, seen(G + 1))
                    else:
                        pe.wait_ge(yp_read, seen(CH * G + c - 1))
                    for h in range(HG):
                        e = slice(h * HEAD, (h + 1) * HEAD)
                        pe.matmul(bank[6 + c % 2][:, e], E[:, c, h, :], xtok[:, c, e], start=True, stop=True)
                    pe.wait_ge(h_ready, seen(G + 1))
                    if c < 2:
                        pe.wait_ge(exp_done, seen(CH * G + c + 3))
                    a, b = {0: (BWD, BWD + 1), CH - 1: (FWD, FWD + 1)}.get(c, (BWD, FWD + 1))
                    pe.matmul(halves(bank[4 + c % 2])[:, a:b, :], feat[:, 3, c * P:(c + 1) * P],
                              H[:, 2 * c + a:2 * c + b, :], start=True, stop=True).then_inc(yo_done, 1)
                pe.wait_ge(yn_ready, seen(G + 1))
                pe.wait_ge(yp_read, seen(CH * (G + 1)))
                for i in range(2):
                    for c in range(CH):
                        q = pe.transpose(bank[4 + i][:, c * P:(c + 1) * P], y[:, c, i * P:(i + 1) * P], ident[:, :])
                    q.then_inc(yt_done, 1)

            def mean(wait, z):
                for m in range(KT):
                    wait(m)
                    q = pe.matmul(bank[4][:, :], mean1[:, :], z[:, m, :], start=m == 0, stop=m == KT - 1)
                q.then_inc(mean_done, 1)

            def var(n, ready=sq_ready, done=sq_used, b=5):
                for m in range(KT):
                    pe.wait_ge(ready, seen(n + m + 1))
                    pe.matmul(bank[b][:, :], mean1[:, :], u[:, m % 2, :], start=m == 0,
                              stop=m == KT - 1).then_inc(done, 1)

            def phase(base, first, end, mh, ml, nk=KT):
                settle(pe)
                with pe.Fori(first, end) as c:
                    for s in range(SLOTS):
                        dense(base + c, s, mh, ml, nk)

            pe.wait_ge(consts, CONSTS)
            settle(pe)
            with pe.Fori(0, LAYERS) as L:
                base = L * CYCLES
                pe.wait_ge(xl_done, seen(NORMS * KT * L + KT))
                pe.wait_ge(dtw_lo, seen(L + 1))
                for c in range(CH):
                    for k in range(KT):
                        t, w = slice(c * P, (c + 1) * P), slice(k * 2 * HEADS, (k + 1) * 2 * HEADS)
                        q = three(bank[4][:, c * 2 * HEADS:(c + 1) * 2 * HEADS], xh[:, k, t], xl[:, k, t],
                                  yh[:, 0, w], yl[:, 0, w], k == 0, k == KT - 1)
                q.then_inc(dt_done, 1)
                pe.wait_ge(ad_ready, seen(L + 1))
                a = stepf[:, ADT, :].rearrange("p (d e) -> p d e", d=2)
                for o, d, m in ((0, BWD, SU), (1, FWD, SL), (2, BWD, LW), (3, FWD, U)):
                    pe.matmul(quarters(bank[5])[:, o, :], m[:, :], a[:, d, :], start=True, stop=True)
                pe.matmul(bank[6][:, 0:GW], ones[:, :], stepf[:, ADT, :], start=True, stop=True).then_inc(cum_done, 1)
                with pe.Fori(0, PAIRS) as j:
                    c0 = base + j * PAIR_CYCLES
                    G0 = L * GROUPS + j * 2
                    for s in range(SLOTS):
                        dense(c0, s, xh, xl)
                    z_tiles(c0 + 1, 0)
                    scan_a(G0)
                    for c, s in ((1, 2), (1, 3), (2, 0), (2, 1)):
                        dense(c0 + c, s, xh, xl)
                    scan_b(G0)
                    z_tiles(c0 + 2, 2)
                    scan_a(G0 + 1)
                    dense(c0 + 3, 0, xh, xl)
                    dense(c0 + 3, 1, xh, xl)
                    scan_b(G0 + 1)
                    dense(c0 + 3, 2, xh, xl)
                    dense(c0 + 3, 3, xh, xl)
                    pe.wait_ge(yl_done, seen(2 * (G0 + 2)))
                    for c in (4, 5):
                        for s in range(SLOTS):
                            dense(c0 + c, s, yh, yl, 4)
                phase(base, C_GATE_A, C_GATE_B, xh, xl)
                k = NORMS * L
                mean(lambda m: pe.wait_ge(ua_ready, seen(KT * L + m + 1)), za)
                phase(base, C_GATE_B, C_GATE_B + 1, xh, xl)
                var(KT * k)
                phase(base, C_GATE_B + 1, C_A_OUT, xh, xl)
                pe.wait_ge(al_done, seen(KT * (L + 1)))
                phase(base, C_A_OUT, C_O, aah, aal)
                pe.wait_ge(bl_done, seen(KT * (L + 1)))
                phase(base, C_O, C_UP0, abh, abl)
                mean(lambda m: pe.wait_ge(z1_ready, seen(KT * L + m + 1)), za)
                var(KT * (k + 1))
                pe.wait_ge(xl_done, seen(KT * (k + 2)))
                phase(base, C_UP0, C_DOWN0, xh, xl)
                pe.wait_ge(fl_done, seen(FT * L + KT))
                phase(base, C_DOWN0, C_UP2, aah, aal)
                phase(base, C_UP2, C_DOWN1, xh, xl)
                phase(base, C_DOWN1, C_DOWN2, abh, abl)
                pe.wait_ge(fl_done, seen(FT * (L + 1)))
                phase(base, C_DOWN2, C_PLE, aah, aal, LAST)
                pe.wait_ge(p_loaded, 16 * (L + 1))
                pe.wait_ge(ple_loaded, 16 * (L + 1))
                for m in range(KT):
                    if m >= 4:
                        pe.wait_ge(e_evac, seen(KT * L + m - 3))
                    for h in range(2):
                        q = pe.matmul(bank[4 + m % 4][:, :], wpl[:, h, m * P:(m + 1) * P], pin[:, h, :],
                                      start=h == 0, stop=h == 1)
                    q.then_inc(e_done, 1)
                pe.wait_ge(e_evac, seen(KT * (L + 1)))
                mean(lambda m: pe.wait_ge(evac[m % SLOTS], seen(base + C_DOWN2 + m // SLOTS + 1)), zb)
                var(KT * (k + 2))
                var(KT * L, esq_ready, esq_used, 6)
                pe.wait_ge(xl_done, seen(KT * (k + 3)))
                phase(base, C_PLE, CYCLES, xh, xl)

        @block.vector
        def _(dve):
            open_(dve, xl_done, dtw_lo, dt_v, ad_ready, grp_ready, conv_done, cb_done,
                  xw_ready, h_ready, m_ready, yp_read, yg_ready, yn_ready, yl_done,
                  ua_ready, xc_ready, zn_ready, al_done, bl_done, gb_ready, mg_ready,
                  z1_ready, fl_done, en_ready, pg_used, xn_ready, *evac)
            order = [0]

            def step(ins):
                ins.then_inc(dve_order, 1)
                order[0] += 1

            def issued(but=0):
                return order[0] - but

            def restart():
                if order[0]:
                    settle(dve)
                    dve.wait_ge(dve_order, issued())
                    dve.sem_clear(dve_order)
                    order[0] = 0

            def spread(t, shape):
                return t.unsqueeze(len(t.shape)).broadcast_to([P, *shape, HEAD])

            def heads(t):
                return t.rearrange("p (h e) -> p h e", h=HG)

            def group_params(q, G, j2):
                dve.wait_ge(xd_ready, seen(G - 1))
                dve.wait_ge(yl_done, seen(2 * G))
                g = j2
                src = stepf[:, :, :].rearrange("p k (a h) -> p (k a) h", h=HEADS)
                step(dve.tensor_copy(gpar[:, q, :], par[:, bass.ds(O_GRP + g * GP, GP)]))
                step(dve.tensor_copy(gdsk[:, q, :], par[:, bass.ds(O_DSK + g * HG, HG)]))
                dve.tensor_copy(gtab[:, q], src[:, :, bass.ds(g * HG, HG)]).then_inc(grp_ready, 1)
                dve.wait_ge(grp_ready, seen(G + 1))
                dve.wait_ge(dve_order, issued())

            def taps(outs, ins, ws, count, finish):
                mid = count // 2
                for n, k in enumerate([mid] + [k for k in range(count) if k != mid]):
                    for i in range(2):
                        w, o = ws[i], k - mid
                        a, b = max(0, -o), T - max(0, o)
                        if n == 0:
                            step(dve.tensor_scalar(outs[i], ins[i], w[:, k:k + 1], ws[2 + i], ALU.mult, ALU.add))
                            continue
                        dve.wait_ge(dve_order, issued(0 if n == count - 1 and i else 1))
                        q = dve.scalar_tensor_tensor(out=outs[i][:, a:b], in0=ins[i][:, a + o:b + o], scalar=w[:, k:k + 1],
                                                     in1=outs[i][:, a:b], op0=ALU.mult, op1=ALU.add)
                        if n == count - 1:
                            q.then_inc(finish, 1)
                        else:
                            step(q)

            def conv(q, G, tiles):
                for i in (0, 2):
                    for c in (i, i + 1):
                        dve.wait_ge(evac[tiles[c][1]], seen(tiles[c][0] + 1))
                    dve.wait_ge(silu_done, seen(4 * G + i))
                    taps([acc[:, 0, :], acc[:, 1, :]], [cin[:, i, :], cin[:, i + 1, :]],
                         [gpar[:, q, (i + c) * TAPS:(i + c + 1) * TAPS] for c in range(2)]
                         + [gpar[:, q, 4 * TAPS + i + c:4 * TAPS + i + c + 1] for c in range(2)],
                         TAPS, conv_done)

            def scan_a(q, G):
                g = gtab[:, q, :, :].rearrange("p (k d c) h -> p k d c h", k=5, d=2)

                def weighted(slot, part, c, d):
                    return dve.tensor_tensor(heads(xw[:, slot, part, :]), heads(xtok[:, c, :]),
                                             spread(g[:, WDEC, d, c, :], [HG]), ALU.mult)

                dve.wait_ge(st_done, seen(3 * G))
                dve.wait_ge(tok_evac, seen(3 * G + 2))
                step(weighted(0, 0, 0, FWD))
                weighted(0, 1, CH - 1, BWD).then_inc(xw_ready, 1)
                step(weighted(1, BWD, 1, BWD))
                weighted(1, FWD, 1, FWD).then_inc(xw_ready, 1)
                dve.wait_ge(tr_done, seen(4 * G + 4))
                for d, m in ((FWD, U), (BWD, LW)):
                    r = dve.tensor_tensor(cb[:, d], quarters(bank[7]), m[:, :].unsqueeze(1).broadcast_to([P, CH, P]), ALU.mult)
                    if d == FWD:
                        step(r)
                    else:
                        r.then_inc(cb_done, 1)
                dve.wait_ge(st_done, seen(3 * G + 1))
                step(weighted(0, BWD, 2, BWD))
                weighted(0, FWD, 2, FWD).then_inc(xw_ready, 1)
                dve.wait_ge(st_evac, seen(3 * G + 2))

                def carry(n, src, d, c):
                    return dve.tensor_tensor(heads(ty[:, n, :]), heads(H[:, src, :]), spread(g[:, TOT, d, c, :], [HG]), ALU.mult)

                def gain(n, dst):
                    return dve.tensor_tensor(H[:, dst, :], H[:, dst, :], ty[:, n, :], ALU.add)

                dve.wait_ge(yp_read, seen(CH * G))
                dve.wait_ge(dve_order, issued())
                step(carry(0, 3, FWD, 1))
                step(carry(1, 4, BWD, 2))
                dve.wait_ge(dve_order, issued(1))
                step(gain(0, 5))
                dve.wait_ge(st_evac, seen(3 * G + 3))
                dve.wait_ge(dve_order, issued(1))
                step(gain(1, 2))
                dve.wait_ge(dve_order, issued(1))
                step(carry(0, 5, FWD, 2))
                dve.wait_ge(dve_order, issued(1))
                step(carry(1, 2, BWD, 1))
                dve.wait_ge(dve_order, issued(1))
                step(gain(0, 7))
                dve.wait_ge(dve_order, issued(1))
                gain(1, 0).then_inc(h_ready, 1)

            def mix(q, G, c):
                g = gtab[:, q, :, :].rearrange("p (k d c) h -> p k d c h", k=5, d=2)
                dve.wait_ge(cb_done, seen(G + 1))
                dve.wait_ge(m_ready, seen(CH * G + c))
                for h in range(HG):
                    step(dve.tensor_scalar(tm[:, h, :], cb[:, BWD, c, :], g[:, DTK, BWD, c, h:h + 1], None, ALU.mult))
                for h in range(HG):
                    dve.wait_ge(dve_order, issued(HG - 1))
                    step(dve.scalar_tensor_tensor(out=tm[:, h, :], in0=cb[:, FWD, c, :], scalar=g[:, DTK, FWD, c, h:h + 1],
                                                  in1=tm[:, h, :], op0=ALU.mult, op1=ALU.add))
                dve.wait_ge(dve_order, issued())
                dve.wait_ge(exp_done, seen(CH * G + c + 1))
                dve.tensor_tensor(E[:, c], E[:, c], tm[:, :, :], ALU.mult).then_inc(m_ready, 1)

            def outputs(q, G, c):
                g = gtab[:, q, :, :].rearrange("p (k d c) h -> p k d c h", k=5, d=2)
                dve.wait_ge(yo_done, seen(CH * G + c + 1))
                if c == 0:
                    dve.wait_ge(xd_ready, seen(G + 1))
                    dve.wait_ge(h_ready, seen(G + 1))
                off, yd = bank[4 + c % 2], bank[6 + c % 2][:, 0:GW]
                if 0 < c < CH - 1:
                    step(dve.tensor_tensor(ty[:, :, :].rearrange("p d (h e) -> p d h e", h=HG),
                                           off[:, :].rearrange("p (d h e) -> p d h e", d=2, h=HG),
                                           spread(g[:, DOUT, :, c, :], [2, HG]), ALU.mult))
                    dve.wait_ge(dve_order, issued())
                    step(dve.tensor_tensor(ty[:, 0, :], ty[:, 0, :], ty[:, 1, :], ALU.add))
                else:
                    d = BWD if c == 0 else FWD
                    step(dve.tensor_tensor(heads(ty[:, 0, :]), heads(halves(off)[:, d, :]),
                                           spread(g[:, DOUT, d, c, :], [HG]), ALU.mult))
                dve.wait_ge(dve_order, issued())
                dve.tensor_tensor(ty[:, 0, :], ty[:, 0, :], yd, ALU.add).then_inc(yp_read, 1)
                dve.wait_ge(yp_read, seen(CH * G + c + 1))
                step(dve.tensor_tensor(y[:, c, :], y[:, c, :], ty[:, 0, :], ALU.add))
                dve.wait_ge(dve_order, issued())
                dve.tensor_tensor(y[:, c, :], y[:, c, :], ztok[:, c // 2, (c % 2) * GW:(c % 2 + 1) * GW],
                                  ALU.mult).then_inc(yg_ready, 1)

            def scan_b(q, G):
                mix(q, G, 0)
                mix(q, G, 1)
                outputs(q, G, 0)
                mix(q, G, 2)
                outputs(q, G, 1)
                mix(q, G, 3)
                outputs(q, G, 2)
                outputs(q, G, 3)
                dve.wait_ge(rms_done, seen(2 * (G + 1)))
                for c in range(CH):
                    r = dve.tensor_scalar(y[:, c, :], y[:, c, :], rst[:, c:c + 1], None, ALU.mult)
                    if c < CH - 1:
                        step(r)
                    else:
                        r.then_inc(yn_ready, 1)
                for i in range(2):
                    dve.wait_ge(yh_done, seen(2 * G + i + 1))
                    dve.scalar_tensor_tensor(out=yl[:, 2 * q + i, :], in0=bank[4 + i][:, :], scalar=gpar[:, q, 24 + i:25 + i],
                                             in1=yh[:, 2 * q + i, :].bitcast(F32), op0=ALU.mult,
                                             op1=ALU.subtract).then_inc(yl_done, 1)

            def rest(dst, z, h, split):
                dve.tensor_tensor(dst, z, h.bitcast(F32), ALU.subtract).then_inc(split, 1)

            def glu(cyc, s, r):
                dve.wait_ge(evac[s + 1], seen(cyc + 1))
                dve.wait_ge(used[s], seen(cyc + 1))
                dve.tensor_tensor(u[:, r, :], bank[s][:, :], sg[:, :], ALU.mult).then_inc(evac[s], 1)

            def norm(L, kind, z, hi, lo, lo_sem):
                k = NORMS * L + kind
                dve.wait_ge(mean_done, seen(k + 1))
                for m in range(KT):
                    dve.tensor_tensor(z[:, m, :], z[:, m, :], bank[4][:, :], ALU.subtract).then_inc(xc_ready, 1)
                dve.wait_ge(std_ready, seen(k + 1))
                step(dve.reciprocal(rstd[:, :], rstd[:, :]))
                dve.wait_ge(dve_order, issued())
                for m in range(KT):
                    dve.tensor_tensor(z[:, m, :], z[:, m, :], rstd[:, :], ALU.mult).then_inc(zn_ready, 1)
                for m in range(KT):
                    dve.wait_ge(zh_ready, seen(KT * k + m + 1))
                    rest(lo[:, m, :], z[:, m, :], hi[:, m, :], lo_sem)

            dve.wait_ge(consts, CONSTS)
            dve.wait_ge(x_loaded, 16)
            settle(dve)
            with dve.Fori(0, LAYERS) as L:
                base = L * CYCLES
                for m in range(KT):
                    dve.wait_ge(xh_done, seen(KT * L + m + 1))
                    rest(xl[:, m, :], zb[:, m, :], xh[:, m, :], xl_done)
                dve.wait_ge(dtw_hi, seen(L + 1))
                rest(yl[:, 0, :], tmf, yh[:, 0, :], dtw_lo)
                dve.wait_ge(par_loaded, 16 * (L + 1))
                dve.wait_ge(dt_done, seen(L + 1))
                bias = par[:, O_DTB:O_DTB + 2 * HEADS].rearrange("p (d h) -> p d h", d=2)
                dch = "p (d c h) -> p d c h"
                dve.tensor_tensor(ty[:, 0, :].rearrange(dch, d=2, c=CH),
                                  bank[4][:, 0:GW].rearrange("p (c d h) -> p d c h", c=CH, d=2),
                                  bias.unsqueeze(2).broadcast_to([P, 2, CH, HEADS]), ALU.add).then_inc(dt_v, 1)
                dve.wait_ge(nega_e, seen(L + 1))
                step(dve.tensor_scalar(nega[:, :], nega[:, :], -1.0, None, ALU.mult))
                dve.wait_ge(dt_e, seen(2 * L + 2))
                e = ty[:, 1, :]
                r_, s_, s2, q_ = (tmf[:, 0:GW], tmf[:, GW:2 * GW], E[:, 0, 0:2, :].rearrange("p a b -> p (a b)"),
                                  E[:, 0, 2:4, :].rearrange("p a b -> p (a b)"))
                step(dve.tensor_scalar(r_, e, 2.0, None, ALU.add))
                dve.wait_ge(dve_order, issued())
                step(dve.reciprocal(r_, r_))
                dve.wait_ge(dve_order, issued())
                step(dve.tensor_tensor(s_, e, r_, ALU.mult))
                dve.wait_ge(dve_order, issued())
                step(dve.tensor_tensor(s2, s_, s_, ALU.mult))
                dve.wait_ge(dve_order, issued())
                step(dve.tensor_scalar(q_, s2, 1.0 / (2 * LOG_TERMS + 1), None, ALU.mult))
                for n in range(LOG_TERMS - 1, 0, -1):
                    dve.wait_ge(dve_order, issued())
                    step(dve.scalar_tensor_tensor(out=q_, in0=q_, scalar=1.0 / (2 * n + 1), in1=s2, op0=ALU.add, op1=ALU.mult))
                dve.wait_ge(dve_order, issued())
                step(dve.scalar_tensor_tensor(out=q_, in0=q_, scalar=1.0, in1=s_, op0=ALU.add, op1=ALU.mult))
                step(dve.tensor_scalar(r_, ty[:, 0, :], 0.0, None, ALU.max))
                dve.wait_ge(dve_order, issued())
                step(dve.scalar_tensor_tensor(out=stepf[:, DTK, :], in0=q_, scalar=2.0, in1=r_, op0=ALU.mult, op1=ALU.add))
                dve.wait_ge(dve_order, issued())
                dve.tensor_tensor(steps[:, ADT], steps[:, DTK],
                                  nega[:, :].rearrange("p (d h) -> p d h", d=2).unsqueeze(2).broadcast_to([P, 2, CH, HEADS]),
                                  ALU.mult).then_inc(ad_ready, 1)
                dve.wait_ge(cum_exp, seen(2 * L + 2))
                step(dve.tensor_tensor(stepf[:, WDEC, :], stepf[:, WDEC, :], stepf[:, DTK, :], ALU.mult))
                restart()
                with dve.Fori(0, PAIRS) as j:
                    c0 = base + j * PAIR_CYCLES
                    G0 = L * GROUPS + j * 2
                    group_params(0, G0, j * 2)
                    conv(0, G0, [(c0, 0), (c0, 1), (c0, 2), (c0, 3)])
                    scan_a(0, G0)
                    scan_b(0, G0)
                    group_params(1, G0 + 1, j * 2 + 1)
                    conv(1, G0 + 1, [(c0 + 1, 2), (c0 + 1, 3), (c0 + 2, 0), (c0 + 2, 1)])
                    scan_a(1, G0 + 1)
                    dve.wait_ge(ua_ready, seen(KT * L + 2 * j))
                    glu(c0 + 3, 0, 0)
                    scan_b(1, G0 + 1)
                    glu(c0 + 3, 2, 1)
                    dve.wait_ge(zb_zero, seen(L + 1))
                    for c in (4, 5):
                        for s in range(SLOTS):
                            m = (c - 4) * SLOTS + s
                            dve.wait_ge(used[s], seen(c0 + c + 1))
                            if c == 4 and s == 0:
                                dve.wait_ge(evac[2], seen(c0 + 4))
                            dve.tensor_tensor(zb[:, m, :], zb[:, m, :], bank[s][:, :], ALU.add).then_inc(evac[s], 1)
                    step(dve.tensor_copy(caw[:, :, :], par[:, bass.ds(O_CAW + j * (2 * CP), 2 * CP)]
                                         .rearrange("p (a b) -> p a b", a=2)))
                    dve.wait_ge(dve_order, issued())
                    outs = [za[:, bass.ds(2 * j + r, 1), :].rearrange("p a t -> p (a t)") for r in range(2)]
                    taps(outs, [u[:, 0, :], u[:, 1, :]],
                         [caw[:, 0, :], caw[:, 1, :], caw[:, 0, CONV_A:CP], caw[:, 1, CONV_A:CP]], CONV_A, ua_ready)
                    dve.wait_ge(ua_ready, seen(KT * L + 2 * j + 2))
                    restart()
                dve.wait_ge(evac[3], seen(base + C_GATE_A))
                norm(L, LN_A, za, aah, aal, al_done)
                restart()
                with dve.Fori(0, KT // SLOTS) as i:
                    for s in range(SLOTS):
                        m = bass.ds(SLOTS * i + s, 1)
                        dve.wait_ge(evac[s], seen(base + C_GATE_B + i + 1))
                        dve.tensor_tensor(zb[:, m, :], zb[:, m, :], sg[:, :].unsqueeze(1), ALU.mult).then_inc(gb_ready, 1)
                dve.wait_ge(gb_ready, seen(KT * (L + 1)))
                settle(dve)
                with dve.Fori(0, KT // SLOTS) as i:
                    for s in range(SLOTS):
                        n = KT * L + SLOTS * i + s
                        m = bass.ds(SLOTS * i + s, 1)
                        dve.wait_ge(used[s], seen(base + C_A_OUT + i + 1))
                        dve.tensor_tensor(ge[:, m, :], bank[s][:, :].unsqueeze(1), ge[:, m, :], ALU.mult).then_inc(evac[s], 1)
                        dve.wait_ge(evac[s], seen(base + C_A_OUT + i + 1))
                        dve.tensor_tensor(zb[:, m, :], zb[:, m, :], ge[:, m, :], ALU.add).then_inc(mg_ready, 1)
                        dve.wait_ge(bh_done, seen(n + 1))
                        rest(abl[:, m, :], zb[:, m, :], abh[:, m, :], bl_done)
                dve.wait_ge(al_done, seen(KT * (L + 1)))
                settle(dve)
                with dve.Fori(0, KT // SLOTS) as i:
                    for s in range(SLOTS):
                        m = bass.ds(SLOTS * i + s, 1)
                        dve.wait_ge(used[s], seen(base + C_O + i + 1))
                        dve.scalar_tensor_tensor(out=za[:, m, :], in0=xh[:, m, :].bitcast(F32), scalar=ALPHA,
                                                 in1=bank[s][:, :].unsqueeze(1), op0=ALU.mult, op1=ALU.add).then_inc(evac[s], 1)
                        dve.wait_ge(evac[s], seen(base + C_O + i + 1))
                        dve.scalar_tensor_tensor(out=za[:, m, :], in0=xl[:, m, :].bitcast(F32), scalar=ALPHA,
                                                 in1=za[:, m, :], op0=ALU.mult, op1=ALU.add).then_inc(z1_ready, 1)
                dve.wait_ge(z1_ready, seen(KT * (L + 1)))
                norm(L, LN_1, za, xh, xl, xl_done)

                def swiglu(c0, count, hi, lo, n0):
                    restart()
                    with dve.Fori(0, count // 2) as i:
                        for r in range(2):
                            dve.wait_ge(fl_done, seen(n0 + 2 * i))
                            dve.wait_ge(evac[2 * r], seen(c0 + i + 1))
                            dve.wait_ge(used[2 * r + 1], seen(c0 + i + 1))
                            dve.tensor_tensor(u[:, r, :], bank[2 * r + 1][:, :], sg[:, :], ALU.mult).then_inc(evac[2 * r + 1], 1)
                        for r in range(2):
                            dve.wait_ge(fh_done, seen(n0 + 2 * i + r + 1))
                            m = bass.ds(2 * i + r, 1)
                            rest(lo[:, m, :], u[:, r, :].unsqueeze(1), hi[:, m, :], fl_done)

                def down(c0, first):
                    with dve.Fori(0, KT // SLOTS) as i:
                        for s in range(SLOTS):
                            m = bass.ds(SLOTS * i + s, 1)
                            b = bank[s][:, :].unsqueeze(1)
                            dve.wait_ge(used[s], seen(c0 + i + 1))
                            dve.wait_ge(evac[s], seen(c0 + i))
                            if first:
                                r = dve.scalar_tensor_tensor(out=zb[:, m, :], in0=za[:, m, :], scalar=ALPHA, in1=b,
                                                             op0=ALU.mult, op1=ALU.add)
                            else:
                                r = dve.tensor_tensor(zb[:, m, :], zb[:, m, :], b, ALU.add)
                            r.then_inc(evac[s], 1)

                f = FT * L
                swiglu(base + C_UP0, KT, aah, aal, f)
                swiglu(base + C_UP1, KT, abh, abl, f + KT)
                down(base + C_DOWN0, True)
                swiglu(base + C_UP2, LAST, aah, aal, f + 2 * KT)
                down(base + C_DOWN1, False)
                down(base + C_DOWN2, False)
                for s in range(SLOTS):
                    dve.wait_ge(evac[s], seen(base + C_PLE))
                norm(L, LN_2, zb, xh, xl, xl_done)
                dve.wait_ge(estd_ready, seen(L + 1))
                step(dve.reciprocal(rstd[:, :], rstd[:, :]))
                dve.wait_ge(dve_order, issued())
                for m in range(KT):
                    dve.tensor_tensor(ge[:, m, :], ge[:, m, :], rstd[:, :], ALU.mult).then_inc(en_ready, 1)
                restart()
                with dve.Fori(0, KT // SLOTS) as i:
                    for s in range(SLOTS):
                        n = KT * L + SLOTS * i + s
                        m = bass.ds(SLOTS * i + s, 1)
                        dve.wait_ge(ef_ready, seen(n + 1))
                        dve.wait_ge(evac[s], seen(base + C_PLE + i + 1))
                        dve.tensor_tensor(ge[:, m, :], ge[:, m, :], sg[:, :].unsqueeze(1), ALU.mult).then_inc(pg_used, 1)
                        dve.wait_ge(pg_used, seen(n + 1))
                        dve.tensor_tensor(zb[:, m, :], zb[:, m, :], ge[:, m, :], ALU.add).then_inc(xn_ready, 1)
                dve.wait_ge(xn_ready, seen(KT * (L + 1)))


def layout(x, p, w_in, conv_a_w, conv_a_b, ln_a_g, ln_a_b, w_a_out, ssm_conv_w, ssm_conv_b, a_log, dt_bias,
           d_skip, ssm_norm_g, w_b_out, w_o, ln1_g, ln1_b, w_gate_up, w_down, ln2_g, ln2_b, w_ple, ple_norm_g,
           w_ple_gate):
    import numpy as np

    def cols(w, c, rows=slice(None)):
        t = w[rows, c:c + P].reshape(-1, P, P).transpose(1, 0, 2).reshape(P, -1)
        return np.concatenate([t, np.zeros((P, WT - t.shape[1]), t.dtype)], 1)

    Z0 = 2 * D + 2 * D
    XS0 = Z0 + INNER
    B0 = XS0 + INNER
    C0 = B0 + GROUPS * STATE
    DT0 = C0 + GROUPS * STATE
    stream, w_dt, par = [], [], []
    for i in range(LAYERS):
        wi = w_in[i]
        for j in range(PAIRS):
            for g in (2 * j, 2 * j + 1):
                stream += [cols(wi, XS0 + g * GW), cols(wi, XS0 + g * GW + P), cols(wi, B0 + g * STATE), cols(wi, C0 + g * STATE)]
                stream += [cols(wi, Z0 + g * GW), cols(wi, Z0 + g * GW + P)]
            for t in (2 * j, 2 * j + 1):
                stream += [cols(wi, t * P), cols(wi, D + t * P)]
            stream += [cols(w_b_out[i], m * P, slice(j * 2 * GW, (j + 1) * 2 * GW)) for m in range(KT)]
        stream += [cols(wi, 2 * D + m * P) for m in range(KT)]
        stream += [cols(wi, 3 * D + m * P) for m in range(KT)]
        stream += [cols(w_a_out[i], m * P) for m in range(KT)]
        stream += [cols(w_o[i], m * P) for m in range(KT)]

        def up(f):
            return [cols(w_gate_up[i], f * P), cols(w_gate_up[i], FFN + f * P)]

        def down(f, n):
            return [cols(w_down[i], m * P, slice(f * P, (f + n) * P)) for m in range(KT)]

        for f in range(2 * KT):
            stream += up(f)
        stream += down(0, KT)
        for f in range(2 * KT, FT):
            stream += up(f)
        stream += down(KT, KT) + down(2 * KT, LAST)
        stream += [cols(w_ple_gate[i], m * P) for m in range(KT)]
        back = lambda v: np.concatenate([v[HEADS:], v[:HEADS]])
        wd = np.concatenate([wi[:, DT0 + HEADS:DT0 + 2 * HEADS], wi[:, DT0:DT0 + HEADS]], 1)
        w_dt.append(wd.reshape(KT, P, 2 * HEADS).transpose(1, 0, 2).reshape(P, -1))
        tiled = lambda v: v.reshape(-1, P).T
        every = lambda v: np.broadcast_to(v[None, :], (P, v.shape[0]))
        cols_ = []
        for t in range(KT):
            cols_ += [conv_a_w[i][:, t * P:(t + 1) * P].T, tiled(conv_a_b[i])[:, t:t + 1]]
        for g in range(GROUPS):
            at = [g * GW, g * GW + P, INNER + g * STATE, INNER + GROUPS * STATE + g * STATE]
            cols_ += [ssm_conv_w[i][:, a:a + P].T for a in at] + [ssm_conv_b[i][a:a + P, None] for a in at]
            cols_ += [tiled(ssm_norm_g[i])[:, 2 * g:2 * g + 2]]
        for v in (ln_a_g, ln_a_b, ln1_g, ln1_b, ln2_g, ln2_b, ple_norm_g):
            cols_.append(tiled(v[i]))
        cols_ += [every(back(dt_bias[i].reshape(-1))), every(back(a_log[i].reshape(-1))), every(d_skip[i])]
        par.append(np.concatenate(cols_, 1))
    stream += [stream[0]] * SLOTS
    return {
        "x_in": x[0].T.reshape(KT, P, T).transpose(1, 0, 2),
        "p_in": p[:, 0].transpose(0, 2, 1).reshape(LAYERS, 2, P, T).transpose(0, 2, 1, 3),
        "w_stream": np.stack(stream).reshape(ALL_CYCLES, SLOTS, P, WT),
        "w_dt": np.stack(w_dt),
        "w_ple": w_ple.reshape(LAYERS, 2, P, D).transpose(0, 2, 1, 3),
        "par_in": np.stack(par),
    }


def kernel(**inputs):
    import numpy as np
    import concourse.bacc as bacc
    from concourse.bass_utils import run_bass_kernel_spmd

    nc = bacc.Bacc("TRN2", target_bir_lowering=False, num_devices=1)
    arrays = {k: np.ascontiguousarray(v) for k, v in layout(**{k: np.asarray(v) for k, v in inputs.items()}).items()}
    args = [nc.dram_tensor(k, v.shape, mybir.dt.from_np(v.dtype), kind="ExternalInput").ap() for k, v in arrays.items()]
    out = nc.dram_tensor("out", (P, KT, T), F32, kind="ExternalOutput").ap()
    build(nc, *args, out)
    r = run_bass_kernel_spmd(nc, [arrays], core_ids=[0])
    got = r.results[0]["out"]
    return np.ascontiguousarray(got.transpose(2, 1, 0).reshape(1, T, D))
```

```python
import concourse.bass as bass
from concourse import mybir
from contextlib import ExitStack
import math

F32 = mybir.dt.float32
F32R = mybir.dt.float32r
ALU = mybir.AluOpType
ACT = mybir.ActivationFunctionType

D, T, LAYERS, CONV_A, HEADS, GROUPS, STATE, HEAD = 1024, 512, 2, 31, 32, 8, 128, 64
INNER, FFN, PLE, TAPS = 2048, 2816, 256, 5
P = 128
KT = D // P
CH = T // P
HG = HEADS // GROUPS
GW = INNER // GROUPS
ALPHA = (2 * LAYERS) ** 0.25
LN_EPS, RMS_EPS = 1e-5, 1e-6
SLOTS = 4
WT = KT * P
HALF = WT // 2

PAIRS = GROUPS // 2
PAIR_CYCLES = 6
C_GATE_A = PAIRS * PAIR_CYCLES
C_GATE_B = C_GATE_A + KT // SLOTS
C_A_OUT = C_GATE_B + KT // SLOTS
C_O = C_A_OUT + KT // SLOTS
C_UP0 = C_O + KT // SLOTS
C_UP1 = C_UP0 + 2 * KT // SLOTS
C_DOWN0 = C_UP1 + 2 * KT // SLOTS
FT = FFN // P
LAST = FT - 2 * KT
C_UP2 = C_DOWN0 + KT // SLOTS
C_DOWN1 = C_UP2 + 2 * LAST // SLOTS
C_DOWN2 = C_DOWN1 + KT // SLOTS
C_PLE = C_DOWN2 + KT // SLOTS
CYCLES = C_PLE + KT // SLOTS
ALL_CYCLES = LAYERS * CYCLES + 1

O_CAW = 0
CP = CONV_A + 1
GP = 4 * TAPS + 4 + 2
O_GRP = O_CAW + KT * CP
O_LNA = O_GRP + GROUPS * GP
O_LN1 = O_LNA + 2 * KT
O_LN2 = O_LN1 + 2 * KT
O_PLE = O_LN2 + 2 * KT
O_DTB = O_PLE + KT
O_ALOG = O_DTB + 2 * HEADS
O_DSK = O_ALOG + 2 * HEADS
NPAR = O_DSK + HEADS
DTK, ADT, WDEC, DOUT, TOT = range(5)
BWD, FWD = 0, 1
LN_A, LN_1, LN_2 = range(3)
NORMS = 3
CONSTS = 15
LOG_TERMS = 8


def build(nc, x_in, p_in, w_stream, w_dt, w_ple, par_in, out):
    ctx = ExitStack()
    with ctx:
        def sb(name, shape, dtype=F32, where=None):
            return (where or ctx).enter_context(nc.sbuf_tensor(name, shape, dtype))

        def sem(name):
            return ctx.enter_context(nc.semaphore(name))

        xh = sb("x_hi", [P, KT, T], F32R)
        xl = sb("x_lo", [P, KT, T], F32R)
        raw = sb("w_raw", [P, 2, WT])
        whi = sb("w_hi", [P, SLOTS, WT], F32R)
        wlo = sb("w_lo", [P, SLOTS, WT], F32R)
        u = sb("glu_out", [P, 2, T])
        za = sb("z_a", [P, KT, T])
        zb = sb("z_b", [P, KT, T])
        sg = sb("sigmoids", [P, T])
        par = sb("params", [P, NPAR])
        steps = sb("steps", [P, 5, 2, CH, HEADS])
        gtab = sb("group_steps", [P, 2, 5 * 2 * CH, HG])
        gpar = sb("group_params", [P, 2, GP])
        gdsk = sb("group_skip", [P, 2, HG])
        nega = sb("neg_a", [P, 2 * HEADS])
        U = sb("tri_le", [P, P])
        LW = sb("tri_ge", [P, P])
        SL = sb("tri_gt", [P, P])
        SU = sb("tri_lt", [P, P])
        ones = sb("ones", [P, P])
        mean1 = sb("ones_over_d", [P, P])
        ident = sb("ident", [P, P])
        neghalf = sb("neg_half", [P, CH])
        ms = sb("mean_squares", [P, CH])
        mse = sb("mean_squares_eps", [P, CH])
        rst = sb("group_rstd", [P, CH])

        caw = sb("conv_a_params", [P, 2, CP])
        eps = sb("eps", [P, 2])

        with ExitStack() as r:
            cin = sb("conv_in", [P, 4, T], F32, r)
            acc = sb("conv_acc", [P, 2, T], F32, r)
            feat = sb("xs_b_c", [P, 4, T], F32, r)
            xtok = sb("x_tok", [P, CH, GW], F32, r)
            btok = sb("b_tok", [P, CH, STATE], F32, r)
            ztok = sb("z_tok", [P, 2, T], F32, r)
            E = sb("decay", [P, CH, HG, P], F32, r)
            rhs = sb("seg_rhs", [P, 2, HG, P], F32, r)
            cb = sb("cb_masked", [P, 2, CH, P], F32, r)
            xw = sb("x_weighted", [P, 2, 2, GW], F32, r)
            H = sb("states", [P, CH * 2, GW], F32, r)
            y = sb("y_tok", [P, CH, GW], F32, r)
            tm = sb("tmp_m", [P, HG, P], F32, r)
            ty = sb("tmp_y", [P, 2, GW], F32, r)
            junk = sb("squares", [P, GW], F32, r)
        with ExitStack() as r:
            aah = sb("act_a_hi", [P, KT, T], F32R, r)
            aal = sb("act_a_lo", [P, KT, T], F32R, r)
            with ExitStack() as r_b:
                abh = sb("act_b_hi", [P, KT, T], F32R, r_b)
                abl = sb("act_b_lo", [P, KT, T], F32R, r_b)
            with ExitStack() as r_b:
                pin = sb("ple_p", [P, 2, T], F32, r_b)
                wpl = sb("w_ple_in", [P, 2, D], F32, r_b)
            sb("act_b_place", [P, 2 * KT, T], F32, r)
            rstd = sb("rstd", [P, T], F32, r)
        sb("region_1", [P, 33 * T + GW])
        with ExitStack() as r:
            yh = sb("y_hi", [P, 4, T], F32R, r)
            yl = sb("y_lo", [P, 4, T], F32R, r)
        ge = sb("gate_or_e", [P, KT, T])
        stepf = steps[:, :, :, :, :].rearrange("p k d c h -> p k (d c h)")
        tmf = tm[:, :, :].rearrange("p a b -> p (a b)")
        tyf = ty[:, :, :].rearrange("p a b -> p (a b)")

        bank = [ctx.enter_context(nc.psum_tensor(f"bank{b}", [P, T], F32)) for b in range(8)]

        def halves(b):
            return b[:, :].rearrange("p (c e) -> p c e", c=2)

        def quarters(b):
            return b[:, :].rearrange("p (c e) -> p c e", c=4)

        raw_ready = [sem(f"raw_ready{s}") for s in range(SLOTS)]
        hi_done = [sem(f"hi_done{s}") for s in range(SLOTS)]
        lo_done = [sem(f"lo_done{s}") for s in range(SLOTS)]
        used = [sem(f"used{s}") for s in range(SLOTS)]
        evac = [sem(f"evac{s}") for s in range(SLOTS)]
        consts = sem("consts")
        x_loaded = sem("x_loaded")
        par_loaded = sem("par_loaded")
        p_loaded = sem("p_loaded")
        ple_loaded = sem("ple_loaded")
        dtw_loaded = sem("dtw_loaded")
        out_stored = sem("out_stored")
        xh_done = sem("xh_done")
        xl_done = sem("xl_done")
        zb_zero = sem("zb_zero")
        dtw_hi = sem("dtw_hi")
        dtw_lo = sem("dtw_lo")
        dt_done = sem("dt_done")
        dt_v = sem("dt_v")
        dt_e = sem("dt_e")
        ad_ready = sem("ad_ready")
        cum_done = sem("cum_done")
        cum_exp = sem("cum_exp")
        nega_e = sem("nega_e")
        grp_ready = sem("grp_ready")
        conv_done = sem("conv_done")
        silu_done = sem("silu_done")
        tr_done = sem("tr_done")
        tok_evac = sem("tok_evac")
        cb_done = sem("cb_done")
        xw_ready = sem("xw_ready")
        seg_done = sem("seg_done")
        rhs_ready = sem("rhs_ready")
        exp_done = sem("exp_done")
        st_done = sem("st_done")
        st_evac = sem("st_evac")
        h_ready = sem("h_ready")
        m_ready = sem("m_ready")
        yo_done = sem("yo_done")
        xd_ready = sem("xd_ready")
        yp_read = sem("yp_read")
        yg_ready = sem("yg_ready")
        ss_done = sem("ss_done")
        rms_done = sem("rms_done")
        yn_ready = sem("yn_ready")
        yt_done = sem("yt_done")
        yh_done = sem("yh_done")
        yl_done = sem("yl_done")
        ua_ready = sem("ua_ready")
        mean_done = sem("mean_done")
        xc_ready = sem("xc_ready")
        sq_ready = sem("sq_ready")
        sq_used = sem("sq_used")
        std_ready = sem("std_ready")
        zn_ready = sem("zn_ready")
        zf_ready = sem("zf_ready")
        zh_ready = sem("zh_ready")
        al_done = sem("al_done")
        bh_done = sem("bh_done")
        bl_done = sem("bl_done")
        gb_ready = sem("gb_ready")
        mg_ready = sem("mg_ready")
        z1_ready = sem("z1_ready")
        fh_done = sem("fh_done")
        fl_done = sem("fl_done")
        e_done = sem("e_done")
        e_evac = sem("e_evac")
        esq_ready = sem("esq_ready")
        esq_used = sem("esq_used")
        estd_ready = sem("estd_ready")
        en_ready = sem("en_ready")
        ef_ready = sem("ef_ready")
        pg_used = sem("pg_used")
        xn_ready = sem("xn_ready")
        dve_order = sem("dve_order")
        settled = sem("settled")
        EARLY = 2

        def seen(n):
            return n + EARLY

        def settle(e):
            e.sem_inc(settled, 1)

        def open_(e, *ss):
            for s in ss:
                e.sem_inc(s, EARLY)

        block = ctx.enter_context(nc.Block())

        @block.sync
        def _(sp):
            def tile(cyc, s):
                sp.wait_ge(lo_done[(s + 2) % SLOTS], seen(cyc + (1 if s >= 2 else 0)))
                sp.dma_start(raw[:, s % 2, :], w_stream[cyc, s]).then_inc(raw_ready[s], 16)

            sp.dma_start(zb[:, :, :], x_in).then_inc(x_loaded, 16)
            sp.dma_start(raw[:, 0, :], w_stream[0, 0]).then_inc(raw_ready[0], 16)
            sp.dma_start(raw[:, 1, :], w_stream[0, 1]).then_inc(raw_ready[1], 16)
            tile(0, 2)
            tile(0, 3)
            with sp.Fori(1, ALL_CYCLES) as cyc:
                for s in range(SLOTS):
                    tile(cyc, s)
            sp.wait_ge(xn_ready, seen(LAYERS * KT))
            sp.dma_start(out, zb[:, :, :]).then_inc(out_stored, 16)
            sp.wait_ge(out_stored, 16)

        @block.gpsimd
        def _(gp):
            open_(gp, rhs_ready, xd_ready, rms_done, zb_zero, *lo_done)

            def lo(cyc, *slots, n=WT):
                for s in slots:
                    gp.wait_ge(hi_done[s], seen(cyc + 1))
                    gp.tensor_tensor(wlo[:, s, 0:n], raw[:, s % 2, 0:n], whi[:, s, 0:n].bitcast(F32),
                                     ALU.subtract).then_inc(lo_done[s], 1)

            def masked_steps(q, G, c):
                gp.wait_ge(seg_done, seen(CH * G + c))
                g = gtab[:, q, :, :].rearrange("p (k d c) h -> p k d c h", k=5, d=2)
                for d, m in ((FWD, U), (BWD, LW)):
                    ad = g[:, ADT, d, c, :].unsqueeze(2).broadcast_to([P, HG, P])
                    i = gp.tensor_tensor(rhs[:, d], ad, m[:, :].unsqueeze(1).broadcast_to([P, HG, P]), ALU.mult)
                i.then_inc(rhs_ready, 1)

            def skip(q, G):
                gp.wait_ge(tok_evac, seen(3 * G + 2))
                gp.wait_ge(yt_done, seen(2 * G))
                d = gdsk[:, q, :].unsqueeze(1).unsqueeze(3).broadcast_to([P, CH, HG, HEAD])
                v = "p c (h e) -> p c h e"
                gp.tensor_tensor(y[:, :, :].rearrange(v, h=HG), xtok[:, :, :].rearrange(v, h=HG), d,
                                 ALU.mult).then_inc(xd_ready, 1)

            def group_rms(G):
                gp.wait_ge(ss_done, seen(CH * (G + 1)))
                gp.wait_ge(yn_ready, seen(G))
                settle(gp)
                gp.tensor_scalar(mse[:, :], ms[:, :], RMS_EPS, None, ALU.add).then_inc(rms_done, 1)
                gp.wait_ge(rms_done, seen(2 * G + 1))
                gp.tensor_tensor(rst[:, :], mse[:, :], neghalf[:, :], ALU.pow).then_inc(rms_done, 1)

            n = [0]

            def fill(dst, pattern=None, value=1.0):
                gp.memset(dst, value).then_inc(consts, 1)
                n[0] += 1
                if pattern:
                    gp.wait_ge(consts, n[0])
                    base, mult, step, op = pattern
                    gp.affine_select(out=dst, in_=dst, compare_op=op, fill=0.0, base=base,
                                     pattern=[[step, P]], channel_multiplier=mult).then_inc(consts, 1)
                    n[0] += 1

            fill(ones[:, :])
            fill(eps[:, 0:1], value=LN_EPS)
            fill(eps[:, 1:2], value=RMS_EPS)
            fill(mean1[:, :], value=1.0 / D)
            fill(neghalf[:, :], value=-0.5)
            fill(U[:, :], (0, -1, 1, ALU.is_ge))
            fill(LW[:, :], (0, 1, -1, ALU.is_ge))
            fill(SL[:, :], (0, 1, -1, ALU.is_gt))
            fill(SU[:, :], (0, -1, 1, ALU.is_gt))
            fill(ident[:, :], (0, 1, -1, ALU.is_equal))
            assert n[0] == CONSTS
            lo(0, 0, 1, 2, 3)
            with gp.Fori(0, LAYERS) as L:
                base = L * CYCLES
                gp.wait_ge(xl_done, seen(NORMS * KT * L + KT))
                settle(gp)
                gp.memset(zb[:, :, :], 0.0).then_inc(zb_zero, 1)
                with gp.Fori(0, PAIRS) as j:
                    c0 = base + j * PAIR_CYCLES
                    G0 = L * GROUPS + j * 2
                    lo(c0 + 1, 0, 1, 2, 3)
                    gp.wait_ge(grp_ready, seen(G0 + 1))
                    masked_steps(0, G0, 0)
                    lo(c0 + 2, 0, 1, 2)
                    masked_steps(0, G0, 1)
                    lo(c0 + 2, 3)
                    masked_steps(0, G0, 2)
                    skip(0, G0)
                    lo(c0 + 3, 0)
                    masked_steps(0, G0, 3)
                    lo(c0 + 3, 1)
                    gp.wait_ge(grp_ready, seen(G0 + 2))
                    masked_steps(1, G0 + 1, 0)
                    group_rms(G0)
                    lo(c0 + 3, 2, 3)
                    lo(c0 + 4, 0, n=HALF)
                    skip(1, G0 + 1)
                    masked_steps(1, G0 + 1, 1)
                    lo(c0 + 4, 1, n=HALF)
                    masked_steps(1, G0 + 1, 2)
                    lo(c0 + 4, 2, n=HALF)
                    masked_steps(1, G0 + 1, 3)
                    lo(c0 + 4, 3, n=HALF)
                    group_rms(G0 + 1)
                    lo(c0 + 5, 0, 1, 2, 3, n=HALF)
                    lo(c0 + 6, 0, 1, 2, 3)
                with gp.Fori(C_GATE_A, CYCLES) as c:
                    lo(base + c + 1, 0, 1, 2, 3)

        @block.scalar
        def _(act):
            open_(act, xh_done, silu_done, tok_evac, exp_done, st_evac, ss_done, yh_done,
                  sq_ready, std_ready, zf_ready, zh_ready, bh_done, fh_done,
                  e_evac, esq_ready, estd_ready, ef_ready, dt_e, cum_exp, nega_e,
                  dtw_hi, *hi_done)

            def hi(cyc, *slots, n=WT):
                for s in slots:
                    act.wait_ge(raw_ready[s], (cyc + 1) * 16)
                    act.wait_ge(used[s], seen(cyc))
                    act.activation(whi[:, s, 0:n], raw[:, s % 2, 0:n], ACT.Copy).then_inc(hi_done[s], 1)

            def take(cyc, s, dst, func=ACT.Copy):
                act.wait_ge(used[s], seen(cyc + 1))
                act.activation(dst, bank[s][:, :], func).then_inc(evac[s], 1)

            def conv_input(G, c, cyc, s):
                take(cyc, s, cin[:, c, :])
                hi(cyc + 1, s)

            def z_gates(G, cyc, slots):
                act.wait_ge(yg_ready, seen(CH * G))
                for i, s in enumerate(slots):
                    take(cyc, s, ztok[:, i, :], ACT.Silu)
                    hi(cyc + 1, s)

            def silu(G, c):
                if c == 0:
                    act.wait_ge(tr_done, seen(4 * G))
                if c == 3:
                    act.wait_ge(yo_done, seen(CH * G))
                act.wait_ge(conv_done, seen(4 * G + c + 1))
                act.activation(feat[:, c, :], acc[:, c % 2, :], ACT.Silu).then_inc(silu_done, 1)

            def xs_tokens(G, i):
                act.wait_ge(xd_ready, seen(G))
                act.wait_ge(yo_done, seen(CH * G))
                act.wait_ge(tr_done, seen(4 * G + i + 1))
                act.activation(xtok[:, 2 * i:2 * i + 2, :], halves(bank[6 + i]), ACT.Copy).then_inc(tok_evac, 1)

            def b_tokens(G):
                act.wait_ge(tr_done, seen(4 * G + 3))
                act.activation(btok[:, :, :], quarters(bank[6]), ACT.Copy).then_inc(tok_evac, 1)

            def decay(G, c):
                act.wait_ge(seg_done, seen(CH * G + c + 1))
                act.activation(E[:, c], quarters(bank[4 + c % 2]), ACT.Exp).then_inc(exp_done, 1)

            def state(G, n):
                act.wait_ge(st_done, seen(3 * G + n + 1))
                dst = (H[:, 3:5, :], H[:, 0:6:5, :], H[:, 2:8:5, :])[n]
                act.activation(dst, halves(bank[6 + n % 2]), ACT.Copy).then_inc(st_evac, 1)

            def square(G, c):
                act.wait_ge(ss_done, seen(CH * G + c))
                act.wait_ge(yg_ready, seen(CH * G + c + 1))
                act.activation(junk[:, :], y[:, c, :], ACT.Square, scale=GW ** -0.5,
                               accum_out=ms[:, c:c + 1]).then_inc(ss_done, 1)

            def round_y(q, G, i):
                act.wait_ge(yt_done, seen(2 * G + i + 1))
                act.activation(yh[:, 2 * q + i, :], bank[4 + i][:, :], ACT.Copy,
                               scale=gpar[:, q, 24 + i:25 + i]).then_inc(yh_done, 1)

            def norm(L, kind, z, hi_dst, off, func):
                k = NORMS * L + kind
                for m in range(KT):
                    act.wait_ge(xc_ready, seen(k * KT + m + 1))
                    if m >= 2:
                        act.wait_ge(sq_used, seen(k * KT + m - 1))
                    act.activation(u[:, m % 2, :], z[:, m, :], ACT.Square).then_inc(sq_ready, 1)
                act.wait_ge(sq_used, seen(KT * (k + 1)))
                act.activation(rstd[:, :], bank[5][:, :], ACT.Sqrt, bias=eps[:, 0:1]).then_inc(std_ready, 1)
                for m in range(KT + 1):
                    if m < KT:
                        act.wait_ge(zn_ready, seen(k * KT + m + 1))
                        act.activation(z[:, m, :], z[:, m, :], func, scale=par[:, off + m:off + m + 1],
                                       bias=par[:, off + KT + m:off + KT + m + 1]).then_inc(zf_ready, 1)
                    if m >= 1:
                        act.wait_ge(zf_ready, seen(k * KT + m))
                        act.activation(hi_dst[:, m - 1, :], z[:, m - 1, :], ACT.Copy).then_inc(zh_ready, 1)

            act.wait_ge(consts, CONSTS)
            hi(0, 0, 1, 2, 3)
            with act.Fori(0, LAYERS) as L:
                base = L * CYCLES
                act.wait_ge(xn_ready, seen(KT * L))
                act.dma_start(par[:, :], par_in[L]).then_inc(par_loaded, 16)
                act.dma_start(tmf, w_dt[L]).then_inc(dtw_loaded, 16)
                act.wait_ge(x_loaded, 16)
                for m in range(KT):
                    act.activation(xh[:, m, :], zb[:, m, :], ACT.Copy).then_inc(xh_done, 1)
                act.wait_ge(dtw_loaded, 16 * (L + 1))
                act.activation(yh[:, 0, :], tmf, ACT.Copy).then_inc(dtw_hi, 1)
                act.wait_ge(par_loaded, 16 * (L + 1))
                act.activation(nega[:, :], par[:, O_ALOG:O_ALOG + 2 * HEADS], ACT.Exp).then_inc(nega_e, 1)
                act.wait_ge(dt_v, seen(L + 1))
                act.activation(ty[:, 1, :], ty[:, 0, :], ACT.Abs).then_inc(dt_e, 1)
                act.wait_ge(dt_e, seen(2 * L + 1))
                act.activation(ty[:, 1, :], ty[:, 1, :], ACT.Exp, scale=-1.0).then_inc(dt_e, 1)
                act.wait_ge(cum_done, seen(L + 1))
                act.activation(stepf[:, WDEC:DOUT + 1, :], halves(bank[5]), ACT.Exp).then_inc(cum_exp, 1)
                act.activation(stepf[:, TOT, :], bank[6][:, 0:GW], ACT.Exp).then_inc(cum_exp, 1)
                with act.Fori(0, PAIRS) as j:
                    c0 = base + j * PAIR_CYCLES
                    G0 = L * GROUPS + j * 2
                    G1 = G0 + 1
                    act.wait_ge(conv_done, seen(4 * G0))
                    for c in range(4):
                        conv_input(G0, c, c0, c)
                    z_gates(G0, c0 + 1, (0, 1))
                    for c in range(4):
                        silu(G0, c)
                    act.wait_ge(conv_done, seen(4 * G0 + 2))
                    conv_input(G1, 0, c0 + 1, 2)
                    xs_tokens(G0, 0)
                    xs_tokens(G0, 1)
                    decay(G0, 0)
                    conv_input(G1, 1, c0 + 1, 3)
                    decay(G0, 1)
                    b_tokens(G0)
                    act.wait_ge(conv_done, seen(4 * G0 + 4))
                    conv_input(G1, 2, c0 + 2, 0)
                    decay(G0, 2)
                    state(G0, 0)
                    silu(G1, 0)
                    silu(G1, 1)
                    conv_input(G1, 3, c0 + 2, 1)
                    decay(G0, 3)
                    state(G0, 1)
                    state(G0, 2)
                    for c in range(CH):
                        square(G0, c)
                    z_gates(G1, c0 + 2, (2, 3))
                    hi(c0 + 4, 0, n=HALF)
                    silu(G1, 2)
                    silu(G1, 3)
                    xs_tokens(G1, 0)
                    xs_tokens(G1, 1)
                    round_y(0, G0, 0)
                    round_y(0, G0, 1)
                    take(c0 + 3, 1, sg[:, :], ACT.Sigmoid)
                    hi(c0 + 4, 1, n=HALF)
                    b_tokens(G1)
                    decay(G1, 0)
                    decay(G1, 1)
                    state(G1, 0)
                    state(G1, 1)
                    hi(c0 + 4, 2, n=HALF)
                    decay(G1, 2)
                    state(G1, 2)
                    decay(G1, 3)
                    act.wait_ge(evac[0], seen(c0 + 4))
                    take(c0 + 3, 3, sg[:, :], ACT.Sigmoid)
                    hi(c0 + 4, 3, n=HALF)
                    for c in range(CH):
                        square(G1, c)
                    round_y(1, G1, 0)
                    round_y(1, G1, 1)
                    hi(c0 + 5, 0, 1, 2, 3, n=HALF)
                    hi(c0 + 6, 0, 1, 2, 3)
                act.wait_ge(yl_done, seen(2 * GROUPS * (L + 1)))
                settle(act)
                with act.Fori(0, KT // SLOTS) as i:
                    for s in range(SLOTS):
                        take(base + C_GATE_A + i, s, ge[:, SLOTS * i + s, :], ACT.Sigmoid)
                        hi(base + C_GATE_A + i + 1, s)
                norm(L, LN_A, za, aah, O_LNA, ACT.Silu)
                with act.Fori(0, KT // SLOTS) as i:
                    for s in range(SLOTS):
                        act.wait_ge(gb_ready, seen(KT * L + SLOTS * i + s))
                        take(base + C_GATE_B + i, s, sg[:, :], ACT.Sigmoid)
                        hi(base + C_GATE_B + i + 1, s)
                with act.Fori(0, KT // SLOTS) as i:
                    for s in range(SLOTS):
                        act.wait_ge(mg_ready, seen(KT * L + SLOTS * i + s + 1))
                        act.activation(abh[:, SLOTS * i + s, :], zb[:, SLOTS * i + s, :], ACT.Copy).then_inc(bh_done, 1)
                        hi(base + C_A_OUT + i + 1, s)
                with act.Fori(C_O, C_UP0) as c:
                    hi(base + c + 1, 0, 1, 2, 3)
                norm(L, LN_1, za, xh, O_LN1, ACT.Identity)

                def swiglu(c0, count, dst):
                    with act.Fori(0, count // 2) as i:
                        for r in range(2):
                            take(c0 + i, 2 * r, sg[:, :], ACT.Silu)
                            hi(c0 + i + 1, 2 * r)
                            act.wait_ge(evac[2 * r + 1], seen(c0 + i + 1))
                            act.activation(dst[:, 2 * i + r, :], u[:, r, :], ACT.Copy).then_inc(fh_done, 1)
                            hi(c0 + i + 1, 2 * r + 1)

                swiglu(base + C_UP0, KT, aah)
                swiglu(base + C_UP1, KT, abh)
                with act.Fori(C_DOWN0, C_UP2) as c:
                    hi(base + c + 1, 0, 1, 2, 3)
                swiglu(base + C_UP2, LAST, aah)
                with act.Fori(C_DOWN1, C_DOWN2) as c:
                    hi(base + c + 1, 0, 1, 2, 3)
                act.wait_ge(used[3], seen(base + C_DOWN2))
                act.dma_start(pin[:, :, :], p_in[L]).then_inc(p_loaded, 16)
                act.dma_start(wpl[:, :, :], w_ple[L]).then_inc(ple_loaded, 16)
                with act.Fori(C_DOWN2, C_PLE) as c:
                    hi(base + c + 1, 0, 1, 2, 3)
                for m in range(KT):
                    act.wait_ge(e_done, seen(KT * L + m + 1))
                    act.activation(ge[:, m, :], bank[4 + m % 4][:, :], ACT.Copy).then_inc(e_evac, 1)
                norm(L, LN_2, zb, xh, O_LN2, ACT.Identity)
                for m in range(KT):
                    act.wait_ge(e_evac, seen(KT * L + m + 1))
                    if m >= 2:
                        act.wait_ge(esq_used, seen(KT * L + m - 1))
                    act.activation(u[:, m % 2, :], ge[:, m, :], ACT.Square).then_inc(esq_ready, 1)
                act.wait_ge(esq_used, seen(KT * (L + 1)))
                act.activation(rstd[:, :], bank[6][:, :], ACT.Sqrt, bias=eps[:, 1:2]).then_inc(estd_ready, 1)
                for m in range(KT):
                    act.wait_ge(en_ready, seen(KT * L + m + 1))
                    act.activation(ge[:, m, :], ge[:, m, :], ACT.Copy,
                                   scale=par[:, O_PLE + m:O_PLE + m + 1]).then_inc(ef_ready, 1)
                with act.Fori(0, KT // SLOTS) as i:
                    for s in range(SLOTS):
                        act.wait_ge(pg_used, seen(KT * L + SLOTS * i + s))
                        take(base + C_PLE + i, s, sg[:, :], ACT.Sigmoid)
                        hi(base + C_PLE + i + 1, s)

        @block.tensor
        def _(pe):
            open_(pe, dt_done, cum_done, tr_done, seg_done, st_done, yo_done, yt_done,
                  mean_done, sq_used, e_done, esq_used, *used)

            def three(dst, wh, wl, mh, ml, first, last):
                pe.matmul(dst, wh, mh, start=first, stop=False)
                pe.matmul(dst, wh, ml, start=False, stop=False)
                return pe.matmul(dst, wl, mh, start=False, stop=last)

            def slot_ready(cyc, s):
                pe.wait_ge(lo_done[s], seen(cyc + 1))
                pe.wait_ge(evac[s], seen(cyc))

            def dense(cyc, s, mh, ml, nk=KT, ks=None):
                ks = ks or range(nk)
                if ks[0] == 0:
                    slot_ready(cyc, s)
                for k in ks:
                    w = slice(k * P, (k + 1) * P)
                    i = three(bank[s][:, :], whi[:, s, w], wlo[:, s, w], mh[:, k, :], ml[:, k, :],
                              k == 0, k == nk - 1)
                if ks[-1] == nk - 1:
                    i.then_inc(used[s], 1)

            def z_tiles(cyc, s, chunks=range(CH)):
                if chunks[0] == 0:
                    slot_ready(cyc, s)
                    slot_ready(cyc, s + 1)
                for c in chunks:
                    dst = halves(bank[s + c // 2])[:, c % 2, :].rearrange("p (b e) -> p b e", b=2)
                    for k in range(KT):
                        t, w = slice(c * P, (c + 1) * P), slice(k * P, (k + 1) * P)
                        h, l, end = whi[:, s:s + 2, w], wlo[:, s:s + 2, w], k == KT - 1
                        pe.matmul(dst, xh[:, k, t], h, start=k == 0, stop=False)
                        pe.matmul(dst, xh[:, k, t], l, start=False, stop=False)
                        if c < CH - 1 or not end:
                            pe.matmul(dst, xl[:, k, t], h, start=False, stop=end)
                        else:
                            pe.matmul(dst[:, 0], xl[:, k, t], h[:, 0], start=False, stop=False).then_inc(used[s], 1)
                            pe.matmul(dst[:, 1], xl[:, k, t], h[:, 1], start=False, stop=end).then_inc(used[s + 1], 1)

            def xs_transpose(G):
                for i in range(2):
                    pe.wait_ge(silu_done, seen(4 * G + 2))
                    pe.wait_ge(yp_read, seen(CH * G))
                    for n in range(4):
                        c, t = 2 * i + n // 2, n % 2
                        q = pe.transpose(bank[6 + i][:, n * P:(n + 1) * P], feat[:, t, c * P:(c + 1) * P], ident[:, :])
                    q.then_inc(tr_done, 1)

            def b_transpose(G):
                pe.wait_ge(silu_done, seen(4 * G + 3))
                pe.wait_ge(tok_evac, seen(3 * G + 1))
                for c in range(CH):
                    q = pe.transpose(bank[6][:, c * P:(c + 1) * P], feat[:, 2, c * P:(c + 1) * P], ident[:, :])
                q.then_inc(tr_done, 1)

            def c_dot_b(G):
                pe.wait_ge(silu_done, seen(4 * G + 4))
                pe.wait_ge(tok_evac, seen(3 * G + 2))
                for c in range(CH):
                    t = slice(c * P, (c + 1) * P)
                    q = pe.matmul(bank[7][:, t], feat[:, 2, t], feat[:, 3, t], start=True, stop=True)
                q.then_inc(tr_done, 1)

            def exponent(G, c):
                pe.wait_ge(rhs_ready, seen(CH * G + c + 1))
                if c < 2:
                    pe.wait_ge(yl_done, seen(2 * G))
                else:
                    pe.wait_ge(exp_done, seen(CH * G + c - 1))
                b = quarters(bank[4 + c % 2])
                pe.matmul(b, SL[:, :], rhs[:, FWD], start=True, stop=False)
                pe.matmul(b, SU[:, :], rhs[:, BWD], start=False, stop=True).then_inc(seg_done, 1)

            def state(G, n):
                pe.wait_ge(xw_ready, seen(3 * G + n + 1))
                if n == 0:
                    pe.wait_ge(tok_evac, seen(3 * G + 3))
                elif n == 1:
                    pe.wait_ge(cb_done, seen(G + 1))
                else:
                    pe.wait_ge(st_evac, seen(3 * G + 1))
                if n == 0:
                    pe.matmul(bank[6][:, 0:GW], btok[:, 0, :], xw[:, 0, 0, :], start=True, stop=True)
                    q = pe.matmul(bank[6][:, GW:], btok[:, CH - 1, :], xw[:, 0, 1, :], start=True, stop=True)
                else:
                    q = pe.matmul(halves(bank[6 + n % 2]), btok[:, n, :], xw[:, n % 2], start=True, stop=True)
                q.then_inc(st_done, 1)

            def y_chunk(G, c):
                pe.wait_ge(m_ready, seen(CH * G + c + 1))
                if c < 2:
                    pe.wait_ge(st_evac, seen(3 * G + 3 - c))
                else:
                    pe.wait_ge(yp_read, seen(CH * G + c - 1))
                for h in range(HG):
                    e = slice(h * HEAD, (h + 1) * HEAD)
                    pe.matmul(bank[6 + c % 2][:, e], E[:, c, h, :], xtok[:, c, e], start=True, stop=True)
                pe.wait_ge(h_ready, seen(G + 1))
                if c < 2:
                    pe.wait_ge(exp_done, seen(CH * G + c + 3))
                a, b = {0: (BWD, BWD + 1), CH - 1: (FWD, FWD + 1)}.get(c, (BWD, FWD + 1))
                pe.matmul(halves(bank[4 + c % 2])[:, a:b, :], feat[:, 3, c * P:(c + 1) * P],
                          H[:, 2 * c + a:2 * c + b, :], start=True, stop=True).then_inc(yo_done, 1)

            def y_transpose(G):
                pe.wait_ge(yn_ready, seen(G + 1))
                pe.wait_ge(yp_read, seen(CH * (G + 1)))
                for i in range(2):
                    for c in range(CH):
                        q = pe.transpose(bank[4 + i][:, c * P:(c + 1) * P], y[:, c, i * P:(i + 1) * P], ident[:, :])
                    q.then_inc(yt_done, 1)

            def mean(wait, z):
                for m in range(KT):
                    wait(m)
                    q = pe.matmul(bank[4][:, :], mean1[:, :], z[:, m, :], start=m == 0, stop=m == KT - 1)
                q.then_inc(mean_done, 1)

            def var(n, ready=sq_ready, done=sq_used, b=5):
                for m in range(KT):
                    pe.wait_ge(ready, seen(n + m + 1))
                    pe.matmul(bank[b][:, :], mean1[:, :], u[:, m % 2, :], start=m == 0,
                              stop=m == KT - 1).then_inc(done, 1)

            def phase(base, first, end, mh, ml, nk=KT):
                settle(pe)
                with pe.Fori(first, end) as c:
                    for s in range(SLOTS):
                        dense(base + c, s, mh, ml, nk)

            pe.wait_ge(consts, CONSTS)
            settle(pe)
            with pe.Fori(0, LAYERS) as L:
                base = L * CYCLES
                pe.wait_ge(xl_done, seen(NORMS * KT * L + KT))
                pe.wait_ge(dtw_lo, seen(L + 1))
                for c in range(CH):
                    for k in range(KT):
                        t, w = slice(c * P, (c + 1) * P), slice(k * 2 * HEADS, (k + 1) * 2 * HEADS)
                        q = three(bank[4][:, c * 2 * HEADS:(c + 1) * 2 * HEADS], xh[:, k, t], xl[:, k, t],
                                  yh[:, 0, w], yl[:, 0, w], k == 0, k == KT - 1)
                q.then_inc(dt_done, 1)
                pe.wait_ge(ad_ready, seen(L + 1))
                a = stepf[:, ADT, :].rearrange("p (d e) -> p d e", d=2)
                for o, d, m in ((0, BWD, SU), (1, FWD, SL), (2, BWD, LW), (3, FWD, U)):
                    pe.matmul(quarters(bank[5])[:, o, :], m[:, :], a[:, d, :], start=True, stop=True)
                pe.matmul(bank[6][:, 0:GW], ones[:, :], stepf[:, ADT, :], start=True, stop=True).then_inc(cum_done, 1)
                with pe.Fori(0, PAIRS) as j:
                    c0 = base + j * PAIR_CYCLES
                    G0 = L * GROUPS + j * 2
                    G1 = G0 + 1
                    low, high = range(KT // 2), range(KT // 2, KT)
                    for s in range(SLOTS):
                        dense(c0, s, xh, xl)
                    z_tiles(c0 + 1, 0)
                    dense(c0 + 1, 2, xh, xl)
                    xs_transpose(G0)
                    exponent(G0, 0)
                    dense(c0 + 1, 3, xh, xl)
                    b_transpose(G0)
                    c_dot_b(G0)
                    exponent(G0, 1)
                    dense(c0 + 2, 0, xh, xl)
                    exponent(G0, 2)
                    state(G0, 0)
                    dense(c0 + 2, 1, xh, xl)
                    exponent(G0, 3)
                    state(G0, 1)
                    state(G0, 2)
                    z_tiles(c0 + 2, 2, (0, 1))
                    y_chunk(G0, 0)
                    z_tiles(c0 + 2, 2, (2,))
                    y_chunk(G0, 1)
                    z_tiles(c0 + 2, 2, (3,))
                    y_chunk(G0, 2)
                    y_chunk(G0, 3)
                    dense(c0 + 3, 0, xh, xl)
                    xs_transpose(G1)
                    dense(c0 + 3, 1, xh, xl, ks=low)
                    y_transpose(G0)
                    dense(c0 + 3, 1, xh, xl, ks=high)
                    b_transpose(G1)
                    c_dot_b(G1)
                    exponent(G1, 0)
                    dense(c0 + 3, 2, xh, xl, ks=low)
                    exponent(G1, 1)
                    state(G1, 0)
                    state(G1, 1)
                    dense(c0 + 3, 2, xh, xl, ks=high)
                    exponent(G1, 2)
                    state(G1, 2)
                    dense(c0 + 3, 3, xh, xl, ks=low)
                    exponent(G1, 3)
                    y_chunk(G1, 0)
                    dense(c0 + 3, 3, xh, xl, ks=high)
                    y_chunk(G1, 1)
                    y_chunk(G1, 2)
                    y_chunk(G1, 3)
                    for s in range(SLOTS):
                        dense(c0 + 4, s, yh, yl, 4, ks=(0, 1))
                    y_transpose(G1)
                    pe.wait_ge(yl_done, seen(2 * (G0 + 2)))
                    for s in range(SLOTS):
                        dense(c0 + 4, s, yh, yl, 4, ks=(2, 3))
                    for s in range(SLOTS):
                        dense(c0 + 5, s, yh, yl, 4)
                phase(base, C_GATE_A, C_GATE_B, xh, xl)
                k = NORMS * L
                mean(lambda m: pe.wait_ge(ua_ready, seen(KT * L + m + 1)), za)
                phase(base, C_GATE_B, C_GATE_B + 1, xh, xl)
                var(KT * k)
                phase(base, C_GATE_B + 1, C_A_OUT, xh, xl)
                pe.wait_ge(al_done, seen(KT * (L + 1)))
                phase(base, C_A_OUT, C_O, aah, aal)
                pe.wait_ge(bl_done, seen(KT * (L + 1)))
                phase(base, C_O, C_UP0, abh, abl)
                mean(lambda m: pe.wait_ge(z1_ready, seen(KT * L + m + 1)), za)
                var(KT * (k + 1))
                pe.wait_ge(xl_done, seen(KT * (k + 2)))
                phase(base, C_UP0, C_DOWN0, xh, xl)
                pe.wait_ge(fl_done, seen(FT * L + KT))
                phase(base, C_DOWN0, C_UP2, aah, aal)
                phase(base, C_UP2, C_DOWN1, xh, xl)
                phase(base, C_DOWN1, C_DOWN2, abh, abl)
                pe.wait_ge(fl_done, seen(FT * (L + 1)))
                phase(base, C_DOWN2, C_PLE, aah, aal, LAST)
                pe.wait_ge(p_loaded, 16 * (L + 1))
                pe.wait_ge(ple_loaded, 16 * (L + 1))
                for m in range(KT):
                    if m >= 4:
                        pe.wait_ge(e_evac, seen(KT * L + m - 3))
                    for h in range(2):
                        q = pe.matmul(bank[4 + m % 4][:, :], wpl[:, h, m * P:(m + 1) * P], pin[:, h, :],
                                      start=h == 0, stop=h == 1)
                    q.then_inc(e_done, 1)
                pe.wait_ge(e_evac, seen(KT * (L + 1)))
                mean(lambda m: pe.wait_ge(evac[m % SLOTS], seen(base + C_DOWN2 + m // SLOTS + 1)), zb)
                var(KT * (k + 2))
                var(KT * L, esq_ready, esq_used, 6)
                pe.wait_ge(xl_done, seen(KT * (k + 3)))
                phase(base, C_PLE, CYCLES, xh, xl)

        @block.vector
        def _(dve):
            open_(dve, xl_done, dtw_lo, dt_v, ad_ready, grp_ready, conv_done, cb_done,
                  xw_ready, h_ready, m_ready, yp_read, yg_ready, yn_ready, yl_done,
                  ua_ready, xc_ready, zn_ready, al_done, bl_done, gb_ready, mg_ready,
                  z1_ready, fl_done, en_ready, pg_used, xn_ready, *evac)
            order = [0]

            def step(ins):
                ins.then_inc(dve_order, 1)
                order[0] += 1

            def issued(but=0):
                return order[0] - but

            def restart():
                if order[0]:
                    settle(dve)
                    dve.wait_ge(dve_order, issued())
                    dve.sem_clear(dve_order)
                    order[0] = 0

            def spread(t, shape):
                return t.unsqueeze(len(t.shape)).broadcast_to([P, *shape, HEAD])

            def heads(t):
                return t.rearrange("p (h e) -> p h e", h=HG)

            def group_params(q, G, j2):
                dve.wait_ge(xd_ready, seen(G - 1))
                dve.wait_ge(yl_done, seen(2 * (G - q)))
                g = j2
                src = stepf[:, :, :].rearrange("p k (a h) -> p (k a) h", h=HEADS)
                step(dve.tensor_copy(gpar[:, q, :], par[:, bass.ds(O_GRP + g * GP, GP)]))
                step(dve.tensor_copy(gdsk[:, q, :], par[:, bass.ds(O_DSK + g * HG, HG)]))
                dve.tensor_copy(gtab[:, q], src[:, :, bass.ds(g * HG, HG)]).then_inc(grp_ready, 1)
                dve.wait_ge(grp_ready, seen(G + 1))
                dve.wait_ge(dve_order, issued())

            def taps(outs, ins, ws, count, finish, between=lambda n: None):
                mid = count // 2
                for n, k in enumerate([mid] + [k for k in range(count) if k != mid]):
                    for i in range(2):
                        w, o = ws[i], k - mid
                        a, b = max(0, -o), T - max(0, o)
                        if n == 0:
                            step(dve.tensor_scalar(outs[i], ins[i], w[:, k:k + 1], ws[2 + i], ALU.mult, ALU.add))
                            continue
                        dve.wait_ge(dve_order, issued(0 if n == count - 1 and i else 1))
                        q = dve.scalar_tensor_tensor(out=outs[i][:, a:b], in0=ins[i][:, a + o:b + o], scalar=w[:, k:k + 1],
                                                     in1=outs[i][:, a:b], op0=ALU.mult, op1=ALU.add)
                        if n == count - 1:
                            q.then_inc(finish, 1)
                        else:
                            step(q)
                    between(n)

            def conv(q, G, i, tiles):
                for cyc, s in tiles:
                    dve.wait_ge(evac[s], seen(cyc + 1))
                dve.wait_ge(silu_done, seen(4 * G + i))
                taps([acc[:, 0, :], acc[:, 1, :]], [cin[:, i, :], cin[:, i + 1, :]],
                     [gpar[:, q, (i + c) * TAPS:(i + c + 1) * TAPS] for c in range(2)]
                     + [gpar[:, q, 4 * TAPS + i + c:4 * TAPS + i + c + 1] for c in range(2)],
                     TAPS, conv_done)

            def weighted_xs(q, G, n):
                dve.wait_ge(st_done, seen(3 * G + n // 2))
                dve.wait_ge(tok_evac, seen(3 * G + 2))
                for part, c, d in (((0, 0, FWD), (1, CH - 1, BWD)), ((BWD, 1, BWD), (FWD, 1, FWD)),
                                   ((BWD, 2, BWD), (FWD, 2, FWD)))[n]:
                    w = gtab[:, q, :, :].rearrange("p (k d c) h -> p k d c h", k=5, d=2)[:, WDEC, d, c, :]
                    r = dve.tensor_tensor(heads(xw[:, n % 2, part, :]), heads(xtok[:, c, :]), spread(w, [HG]), ALU.mult)
                    if part == (0, BWD, BWD)[n]:
                        step(r)
                    else:
                        r.then_inc(xw_ready, 1)

            def mask_cb(G):
                dve.wait_ge(tr_done, seen(4 * G + 4))
                for d, m in ((FWD, U), (BWD, LW)):
                    r = dve.tensor_tensor(cb[:, d], quarters(bank[7]), m[:, :].unsqueeze(1).broadcast_to([P, CH, P]), ALU.mult)
                    if d == FWD:
                        step(r)
                    else:
                        r.then_inc(cb_done, 1)

            def entering(q, G):
                g = gtab[:, q, :, :].rearrange("p (k d c) h -> p k d c h", k=5, d=2)
                dve.wait_ge(st_evac, seen(3 * G + 2))

                def carry(n, src, d, c):
                    return dve.tensor_tensor(heads(ty[:, n, :]), heads(H[:, src, :]), spread(g[:, TOT, d, c, :], [HG]), ALU.mult)

                def gain(n, dst):
                    return dve.tensor_tensor(H[:, dst, :], H[:, dst, :], ty[:, n, :], ALU.add)

                dve.wait_ge(yp_read, seen(CH * G))
                dve.wait_ge(dve_order, issued())
                step(carry(0, 3, FWD, 1))
                step(carry(1, 4, BWD, 2))
                dve.wait_ge(dve_order, issued(1))
                step(gain(0, 5))
                dve.wait_ge(st_evac, seen(3 * G + 3))
                dve.wait_ge(dve_order, issued(1))
                step(gain(1, 2))
                dve.wait_ge(dve_order, issued(1))
                step(carry(0, 5, FWD, 2))
                dve.wait_ge(dve_order, issued(1))
                step(carry(1, 2, BWD, 1))
                dve.wait_ge(dve_order, issued(1))
                step(gain(0, 7))
                dve.wait_ge(dve_order, issued(1))
                gain(1, 0).then_inc(h_ready, 1)

            def mix(q, G, c):
                g = gtab[:, q, :, :].rearrange("p (k d c) h -> p k d c h", k=5, d=2)
                dve.wait_ge(cb_done, seen(G + 1))
                dve.wait_ge(m_ready, seen(CH * G + c))
                for h in range(HG):
                    step(dve.tensor_scalar(tm[:, h, :], cb[:, BWD, c, :], g[:, DTK, BWD, c, h:h + 1], None, ALU.mult))
                for h in range(HG):
                    dve.wait_ge(dve_order, issued(HG - 1))
                    step(dve.scalar_tensor_tensor(out=tm[:, h, :], in0=cb[:, FWD, c, :], scalar=g[:, DTK, FWD, c, h:h + 1],
                                                  in1=tm[:, h, :], op0=ALU.mult, op1=ALU.add))
                dve.wait_ge(dve_order, issued())
                dve.wait_ge(exp_done, seen(CH * G + c + 1))
                dve.tensor_tensor(E[:, c], E[:, c], tm[:, :, :], ALU.mult).then_inc(m_ready, 1)

            def outputs(q, G, c):
                g = gtab[:, q, :, :].rearrange("p (k d c) h -> p k d c h", k=5, d=2)
                dve.wait_ge(yo_done, seen(CH * G + c + 1))
                if c == 0:
                    dve.wait_ge(xd_ready, seen(G + 1))
                    dve.wait_ge(h_ready, seen(G + 1))
                off, yd = bank[4 + c % 2], bank[6 + c % 2][:, 0:GW]
                if 0 < c < CH - 1:
                    step(dve.tensor_tensor(ty[:, :, :].rearrange("p d (h e) -> p d h e", h=HG),
                                           off[:, :].rearrange("p (d h e) -> p d h e", d=2, h=HG),
                                           spread(g[:, DOUT, :, c, :], [2, HG]), ALU.mult))
                    dve.wait_ge(dve_order, issued())
                    step(dve.tensor_tensor(ty[:, 0, :], ty[:, 0, :], ty[:, 1, :], ALU.add))
                else:
                    d = BWD if c == 0 else FWD
                    step(dve.tensor_tensor(heads(ty[:, 0, :]), heads(halves(off)[:, d, :]),
                                           spread(g[:, DOUT, d, c, :], [HG]), ALU.mult))
                dve.wait_ge(dve_order, issued())
                dve.tensor_tensor(ty[:, 0, :], ty[:, 0, :], yd, ALU.add).then_inc(yp_read, 1)
                dve.wait_ge(yp_read, seen(CH * G + c + 1))
                step(dve.tensor_tensor(y[:, c, :], y[:, c, :], ty[:, 0, :], ALU.add))
                dve.wait_ge(dve_order, issued())
                dve.tensor_tensor(y[:, c, :], y[:, c, :], ztok[:, c // 2, (c % 2) * GW:(c % 2 + 1) * GW],
                                  ALU.mult).then_inc(yg_ready, 1)

            def normalise_y(G):
                dve.wait_ge(rms_done, seen(2 * (G + 1)))
                for c in range(CH):
                    r = dve.tensor_scalar(y[:, c, :], y[:, c, :], rst[:, c:c + 1], None, ALU.mult)
                    if c < CH - 1:
                        step(r)
                    else:
                        r.then_inc(yn_ready, 1)

            def rest_of_y(q, G):
                for i in range(2):
                    dve.wait_ge(yh_done, seen(2 * G + i + 1))
                    dve.scalar_tensor_tensor(out=yl[:, 2 * q + i, :], in0=bank[4 + i][:, :], scalar=gpar[:, q, 24 + i:25 + i],
                                             in1=yh[:, 2 * q + i, :].bitcast(F32), op0=ALU.mult,
                                             op1=ALU.subtract).then_inc(yl_done, 1)

            def rest(dst, z, h, split):
                dve.tensor_tensor(dst, z, h.bitcast(F32), ALU.subtract).then_inc(split, 1)

            def glu(cyc, s, r):
                dve.wait_ge(evac[s + 1], seen(cyc + 1))
                dve.wait_ge(used[s], seen(cyc + 1))
                dve.tensor_tensor(u[:, r, :], bank[s][:, :], sg[:, :], ALU.mult).then_inc(evac[s], 1)

            def norm(L, kind, z, hi, lo, lo_sem):
                k = NORMS * L + kind
                dve.wait_ge(mean_done, seen(k + 1))
                for m in range(KT):
                    dve.tensor_tensor(z[:, m, :], z[:, m, :], bank[4][:, :], ALU.subtract).then_inc(xc_ready, 1)
                dve.wait_ge(std_ready, seen(k + 1))
                step(dve.reciprocal(rstd[:, :], rstd[:, :]))
                dve.wait_ge(dve_order, issued())
                for m in range(KT):
                    dve.tensor_tensor(z[:, m, :], z[:, m, :], rstd[:, :], ALU.mult).then_inc(zn_ready, 1)
                for m in range(KT):
                    dve.wait_ge(zh_ready, seen(KT * k + m + 1))
                    rest(lo[:, m, :], z[:, m, :], hi[:, m, :], lo_sem)

            dve.wait_ge(consts, CONSTS)
            dve.wait_ge(x_loaded, 16)
            settle(dve)
            with dve.Fori(0, LAYERS) as L:
                base = L * CYCLES
                for m in range(KT):
                    dve.wait_ge(xh_done, seen(KT * L + m + 1))
                    rest(xl[:, m, :], zb[:, m, :], xh[:, m, :], xl_done)
                dve.wait_ge(dtw_hi, seen(L + 1))
                rest(yl[:, 0, :], tmf, yh[:, 0, :], dtw_lo)
                dve.wait_ge(par_loaded, 16 * (L + 1))
                dve.wait_ge(dt_done, seen(L + 1))
                bias = par[:, O_DTB:O_DTB + 2 * HEADS].rearrange("p (d h) -> p d h", d=2)
                dch = "p (d c h) -> p d c h"
                dve.tensor_tensor(ty[:, 0, :].rearrange(dch, d=2, c=CH),
                                  bank[4][:, 0:GW].rearrange("p (c d h) -> p d c h", c=CH, d=2),
                                  bias.unsqueeze(2).broadcast_to([P, 2, CH, HEADS]), ALU.add).then_inc(dt_v, 1)
                dve.wait_ge(nega_e, seen(L + 1))
                step(dve.tensor_scalar(nega[:, :], nega[:, :], -1.0, None, ALU.mult))
                dve.wait_ge(dt_e, seen(2 * L + 2))
                e = ty[:, 1, :]
                r_, s_, s2, q_ = (tmf[:, 0:GW], tmf[:, GW:2 * GW], E[:, 0, 0:2, :].rearrange("p a b -> p (a b)"),
                                  E[:, 0, 2:4, :].rearrange("p a b -> p (a b)"))
                step(dve.tensor_scalar(r_, e, 2.0, None, ALU.add))
                dve.wait_ge(dve_order, issued())
                step(dve.reciprocal(r_, r_))
                dve.wait_ge(dve_order, issued())
                step(dve.tensor_tensor(s_, e, r_, ALU.mult))
                dve.wait_ge(dve_order, issued())
                step(dve.tensor_tensor(s2, s_, s_, ALU.mult))
                dve.wait_ge(dve_order, issued())
                step(dve.tensor_scalar(q_, s2, 1.0 / (2 * LOG_TERMS + 1), None, ALU.mult))
                for n in range(LOG_TERMS - 1, 0, -1):
                    dve.wait_ge(dve_order, issued())
                    step(dve.scalar_tensor_tensor(out=q_, in0=q_, scalar=1.0 / (2 * n + 1), in1=s2, op0=ALU.add, op1=ALU.mult))
                dve.wait_ge(dve_order, issued())
                step(dve.scalar_tensor_tensor(out=q_, in0=q_, scalar=1.0, in1=s_, op0=ALU.add, op1=ALU.mult))
                step(dve.tensor_scalar(r_, ty[:, 0, :], 0.0, None, ALU.max))
                dve.wait_ge(dve_order, issued())
                step(dve.scalar_tensor_tensor(out=stepf[:, DTK, :], in0=q_, scalar=2.0, in1=r_, op0=ALU.mult, op1=ALU.add))
                dve.wait_ge(dve_order, issued())
                dve.tensor_tensor(steps[:, ADT], steps[:, DTK],
                                  nega[:, :].rearrange("p (d h) -> p d h", d=2).unsqueeze(2).broadcast_to([P, 2, CH, HEADS]),
                                  ALU.mult).then_inc(ad_ready, 1)
                dve.wait_ge(cum_exp, seen(2 * L + 2))
                step(dve.tensor_tensor(stepf[:, WDEC, :], stepf[:, WDEC, :], stepf[:, DTK, :], ALU.mult))
                restart()
                with dve.Fori(0, PAIRS) as j:
                    c0 = base + j * PAIR_CYCLES
                    G0 = L * GROUPS + j * 2
                    G1 = G0 + 1
                    group_params(0, G0, j * 2)
                    conv(0, G0, 0, [(c0, 0), (c0, 1)])
                    conv(0, G0, 2, [(c0, 2), (c0, 3)])
                    weighted_xs(0, G0, 0)
                    weighted_xs(0, G0, 1)
                    group_params(1, G1, j * 2 + 1)
                    mask_cb(G0)
                    conv(1, G1, 0, [(c0 + 1, 2), (c0 + 1, 3)])
                    weighted_xs(0, G0, 2)
                    mix(0, G0, 0)
                    mix(0, G0, 1)
                    entering(0, G0)
                    mix(0, G0, 2)
                    outputs(0, G0, 0)
                    mix(0, G0, 3)
                    outputs(0, G0, 1)
                    outputs(0, G0, 2)
                    outputs(0, G0, 3)
                    conv(1, G1, 2, [(c0 + 2, 0), (c0 + 2, 1)])
                    normalise_y(G0)
                    weighted_xs(1, G1, 0)
                    weighted_xs(1, G1, 1)
                    rest_of_y(0, G0)
                    mask_cb(G1)
                    mix(1, G1, 0)
                    dve.wait_ge(ua_ready, seen(KT * L + 2 * j))
                    glu(c0 + 3, 0, 0)
                    mix(1, G1, 1)
                    weighted_xs(1, G1, 2)
                    entering(1, G1)
                    mix(1, G1, 2)
                    outputs(1, G1, 0)
                    mix(1, G1, 3)
                    outputs(1, G1, 1)
                    outputs(1, G1, 2)
                    outputs(1, G1, 3)
                    glu(c0 + 3, 2, 1)
                    step(dve.tensor_copy(caw[:, :, :], par[:, bass.ds(O_CAW + j * (2 * CP), 2 * CP)]
                                         .rearrange("p (a b) -> p a b", a=2)))
                    normalise_y(G1)
                    rest_of_y(1, G1)

                    def add_mamba(n):
                        m = (n - 1) // 2
                        if n % 2 == 0 or m >= KT:
                            return
                        c, s = 4 + m // SLOTS, m % SLOTS
                        dve.wait_ge(used[s], seen(c0 + c + 1))
                        dve.tensor_tensor(zb[:, m, :], zb[:, m, :], bank[s][:, :], ALU.add).then_inc(evac[s], 1)

                    dve.wait_ge(zb_zero, seen(L + 1))
                    dve.wait_ge(evac[0], seen(c0 + 4))
                    dve.wait_ge(evac[2], seen(c0 + 4))
                    dve.wait_ge(dve_order, issued())
                    outs = [za[:, bass.ds(2 * j + r, 1), :].rearrange("p a t -> p (a t)") for r in range(2)]
                    taps(outs, [u[:, 0, :], u[:, 1, :]],
                         [caw[:, 0, :], caw[:, 1, :], caw[:, 0, CONV_A:CP], caw[:, 1, CONV_A:CP]], CONV_A, ua_ready,
                         add_mamba)
                    dve.wait_ge(ua_ready, seen(KT * L + 2 * j + 2))
                    restart()
                dve.wait_ge(evac[3], seen(base + C_GATE_A))
                norm(L, LN_A, za, aah, aal, al_done)
                restart()
                with dve.Fori(0, KT // SLOTS) as i:
                    for s in range(SLOTS):
                        m = bass.ds(SLOTS * i + s, 1)
                        dve.wait_ge(evac[s], seen(base + C_GATE_B + i + 1))
                        dve.tensor_tensor(zb[:, m, :], zb[:, m, :], sg[:, :].unsqueeze(1), ALU.mult).then_inc(gb_ready, 1)
                dve.wait_ge(gb_ready, seen(KT * (L + 1)))
                settle(dve)
                with dve.Fori(0, KT // SLOTS) as i:
                    for s in range(SLOTS):
                        n = KT * L + SLOTS * i + s
                        m = bass.ds(SLOTS * i + s, 1)
                        dve.wait_ge(used[s], seen(base + C_A_OUT + i + 1))
                        dve.tensor_tensor(ge[:, m, :], bank[s][:, :].unsqueeze(1), ge[:, m, :], ALU.mult).then_inc(evac[s], 1)
                        dve.wait_ge(evac[s], seen(base + C_A_OUT + i + 1))
                        dve.tensor_tensor(zb[:, m, :], zb[:, m, :], ge[:, m, :], ALU.add).then_inc(mg_ready, 1)
                        dve.wait_ge(bh_done, seen(n + 1))
                        rest(abl[:, m, :], zb[:, m, :], abh[:, m, :], bl_done)
                dve.wait_ge(al_done, seen(KT * (L + 1)))
                settle(dve)
                with dve.Fori(0, KT // SLOTS) as i:
                    for s in range(SLOTS):
                        m = bass.ds(SLOTS * i + s, 1)
                        dve.wait_ge(used[s], seen(base + C_O + i + 1))
                        dve.scalar_tensor_tensor(out=za[:, m, :], in0=xh[:, m, :].bitcast(F32), scalar=ALPHA,
                                                 in1=bank[s][:, :].unsqueeze(1), op0=ALU.mult, op1=ALU.add).then_inc(evac[s], 1)
                        dve.wait_ge(evac[s], seen(base + C_O + i + 1))
                        dve.scalar_tensor_tensor(out=za[:, m, :], in0=xl[:, m, :].bitcast(F32), scalar=ALPHA,
                                                 in1=za[:, m, :], op0=ALU.mult, op1=ALU.add).then_inc(z1_ready, 1)
                dve.wait_ge(z1_ready, seen(KT * (L + 1)))
                norm(L, LN_1, za, xh, xl, xl_done)

                def swiglu(c0, count, hi, lo, n0):
                    restart()
                    with dve.Fori(0, count // 2) as i:
                        for r in range(2):
                            dve.wait_ge(fl_done, seen(n0 + 2 * i))
                            dve.wait_ge(evac[2 * r], seen(c0 + i + 1))
                            dve.wait_ge(used[2 * r + 1], seen(c0 + i + 1))
                            dve.tensor_tensor(u[:, r, :], bank[2 * r + 1][:, :], sg[:, :], ALU.mult).then_inc(evac[2 * r + 1], 1)
                        for r in range(2):
                            dve.wait_ge(fh_done, seen(n0 + 2 * i + r + 1))
                            m = bass.ds(2 * i + r, 1)
                            rest(lo[:, m, :], u[:, r, :].unsqueeze(1), hi[:, m, :], fl_done)

                def down(c0, first):
                    with dve.Fori(0, KT // SLOTS) as i:
                        for s in range(SLOTS):
                            m = bass.ds(SLOTS * i + s, 1)
                            b = bank[s][:, :].unsqueeze(1)
                            dve.wait_ge(used[s], seen(c0 + i + 1))
                            dve.wait_ge(evac[s], seen(c0 + i))
                            if first:
                                r = dve.scalar_tensor_tensor(out=zb[:, m, :], in0=za[:, m, :], scalar=ALPHA, in1=b,
                                                             op0=ALU.mult, op1=ALU.add)
                            else:
                                r = dve.tensor_tensor(zb[:, m, :], zb[:, m, :], b, ALU.add)
                            r.then_inc(evac[s], 1)

                f = FT * L
                swiglu(base + C_UP0, KT, aah, aal, f)
                swiglu(base + C_UP1, KT, abh, abl, f + KT)
                down(base + C_DOWN0, True)
                swiglu(base + C_UP2, LAST, aah, aal, f + 2 * KT)
                down(base + C_DOWN1, False)
                down(base + C_DOWN2, False)
                for s in range(SLOTS):
                    dve.wait_ge(evac[s], seen(base + C_PLE))
                norm(L, LN_2, zb, xh, xl, xl_done)
                dve.wait_ge(estd_ready, seen(L + 1))
                step(dve.reciprocal(rstd[:, :], rstd[:, :]))
                dve.wait_ge(dve_order, issued())
                for m in range(KT):
                    dve.tensor_tensor(ge[:, m, :], ge[:, m, :], rstd[:, :], ALU.mult).then_inc(en_ready, 1)
                restart()
                with dve.Fori(0, KT // SLOTS) as i:
                    for s in range(SLOTS):
                        n = KT * L + SLOTS * i + s
                        m = bass.ds(SLOTS * i + s, 1)
                        dve.wait_ge(ef_ready, seen(n + 1))
                        dve.wait_ge(evac[s], seen(base + C_PLE + i + 1))
                        dve.tensor_tensor(ge[:, m, :], ge[:, m, :], sg[:, :].unsqueeze(1), ALU.mult).then_inc(pg_used, 1)
                        dve.wait_ge(pg_used, seen(n + 1))
                        dve.tensor_tensor(zb[:, m, :], zb[:, m, :], ge[:, m, :], ALU.add).then_inc(xn_ready, 1)
                dve.wait_ge(xn_ready, seen(KT * (L + 1)))


def layout(x, p, w_in, conv_a_w, conv_a_b, ln_a_g, ln_a_b, w_a_out, ssm_conv_w, ssm_conv_b, a_log, dt_bias,
           d_skip, ssm_norm_g, w_b_out, w_o, ln1_g, ln1_b, w_gate_up, w_down, ln2_g, ln2_b, w_ple, ple_norm_g,
           w_ple_gate):
    import numpy as np

    def cols(w, c, rows=slice(None)):
        t = w[rows, c:c + P].reshape(-1, P, P).transpose(1, 0, 2).reshape(P, -1)
        return np.concatenate([t, np.zeros((P, WT - t.shape[1]), t.dtype)], 1)

    Z0 = 2 * D + 2 * D
    XS0 = Z0 + INNER
    B0 = XS0 + INNER
    C0 = B0 + GROUPS * STATE
    DT0 = C0 + GROUPS * STATE
    stream, w_dt, par = [], [], []
    for i in range(LAYERS):
        wi = w_in[i]
        for j in range(PAIRS):
            for g in (2 * j, 2 * j + 1):
                stream += [cols(wi, XS0 + g * GW), cols(wi, XS0 + g * GW + P), cols(wi, B0 + g * STATE), cols(wi, C0 + g * STATE)]
                stream += [cols(wi, Z0 + g * GW), cols(wi, Z0 + g * GW + P)]
            for t in (2 * j, 2 * j + 1):
                stream += [cols(wi, t * P), cols(wi, D + t * P)]
            stream += [cols(w_b_out[i], m * P, slice(j * 2 * GW, (j + 1) * 2 * GW)) for m in range(KT)]
        stream += [cols(wi, 2 * D + m * P) for m in range(KT)]
        stream += [cols(wi, 3 * D + m * P) for m in range(KT)]
        stream += [cols(w_a_out[i], m * P) for m in range(KT)]
        stream += [cols(w_o[i], m * P) for m in range(KT)]

        def up(f):
            return [cols(w_gate_up[i], f * P), cols(w_gate_up[i], FFN + f * P)]

        def down(f, n):
            return [cols(w_down[i], m * P, slice(f * P, (f + n) * P)) for m in range(KT)]

        for f in range(2 * KT):
            stream += up(f)
        stream += down(0, KT)
        for f in range(2 * KT, FT):
            stream += up(f)
        stream += down(KT, KT) + down(2 * KT, LAST)
        stream += [cols(w_ple_gate[i], m * P) for m in range(KT)]
        back = lambda v: np.concatenate([v[HEADS:], v[:HEADS]])
        wd = np.concatenate([wi[:, DT0 + HEADS:DT0 + 2 * HEADS], wi[:, DT0:DT0 + HEADS]], 1)
        w_dt.append(wd.reshape(KT, P, 2 * HEADS).transpose(1, 0, 2).reshape(P, -1))
        tiled = lambda v: v.reshape(-1, P).T
        every = lambda v: np.broadcast_to(v[None, :], (P, v.shape[0]))
        cols_ = []
        for t in range(KT):
            cols_ += [conv_a_w[i][:, t * P:(t + 1) * P].T, tiled(conv_a_b[i])[:, t:t + 1]]
        for g in range(GROUPS):
            at = [g * GW, g * GW + P, INNER + g * STATE, INNER + GROUPS * STATE + g * STATE]
            cols_ += [ssm_conv_w[i][:, a:a + P].T for a in at] + [ssm_conv_b[i][a:a + P, None] for a in at]
            cols_ += [tiled(ssm_norm_g[i])[:, 2 * g:2 * g + 2]]
        for v in (ln_a_g, ln_a_b, ln1_g, ln1_b, ln2_g, ln2_b, ple_norm_g):
            cols_.append(tiled(v[i]))
        cols_ += [every(back(dt_bias[i].reshape(-1))), every(back(a_log[i].reshape(-1))), every(d_skip[i])]
        par.append(np.concatenate(cols_, 1))
    stream += [stream[0]] * SLOTS
    return {
        "x_in": x[0].T.reshape(KT, P, T).transpose(1, 0, 2),
        "p_in": p[:, 0].transpose(0, 2, 1).reshape(LAYERS, 2, P, T).transpose(0, 2, 1, 3),
        "w_stream": np.stack(stream).reshape(ALL_CYCLES, SLOTS, P, WT),
        "w_dt": np.stack(w_dt),
        "w_ple": w_ple.reshape(LAYERS, 2, P, D).transpose(0, 2, 1, 3),
        "par_in": np.stack(par),
    }


def kernel(**inputs):
    import numpy as np
    import concourse.bacc as bacc
    from concourse.bass_utils import run_bass_kernel_spmd

    nc = bacc.Bacc("TRN2", target_bir_lowering=False, num_devices=1)
    arrays = {k: np.ascontiguousarray(v) for k, v in layout(**{k: np.asarray(v) for k, v in inputs.items()}).items()}
    args = [nc.dram_tensor(k, v.shape, mybir.dt.from_np(v.dtype), kind="ExternalInput").ap() for k, v in arrays.items()]
    out = nc.dram_tensor("out", (P, KT, T), F32, kind="ExternalOutput").ap()
    build(nc, *args, out)
    r = run_bass_kernel_spmd(nc, [arrays], core_ids=[0])
    got = r.results[0]["out"]
    return np.ascontiguousarray(got.transpose(2, 1, 0).reshape(1, T, D))
```

```python
import concourse.bass as bass
from concourse import mybir
from contextlib import ExitStack
import math

F32 = mybir.dt.float32
F32R = mybir.dt.float32r
ALU = mybir.AluOpType
ACT = mybir.ActivationFunctionType

D, T, LAYERS, CONV_A, HEADS, GROUPS, STATE, HEAD = 1024, 512, 2, 31, 32, 8, 128, 64
INNER, FFN, PLE, TAPS = 2048, 2816, 256, 5
P = 128
KT = D // P
CH = T // P
HG = HEADS // GROUPS
GW = INNER // GROUPS
ALPHA = (2 * LAYERS) ** 0.25
LN_EPS, RMS_EPS = 1e-5, 1e-6
SLOTS = 4
WT = KT * P
HALF = WT // 2

PAIRS = GROUPS // 2
PAIR_CYCLES = 6
C_GATE_A = PAIRS * PAIR_CYCLES
C_GATE_B = C_GATE_A + KT // SLOTS
C_A_OUT = C_GATE_B + KT // SLOTS
C_O = C_A_OUT + KT // SLOTS
C_UP0 = C_O + KT // SLOTS
C_UP1 = C_UP0 + 2 * KT // SLOTS
C_DOWN0 = C_UP1 + 2 * KT // SLOTS
FT = FFN // P
LAST = FT - 2 * KT
C_UP2 = C_DOWN0 + KT // SLOTS
C_DOWN1 = C_UP2 + 2 * LAST // SLOTS
C_DOWN2 = C_DOWN1 + KT // SLOTS
C_PLE = C_DOWN2 + KT // SLOTS
CYCLES = C_PLE + KT // SLOTS
ALL_CYCLES = LAYERS * CYCLES

O_CAW = 0
CP = CONV_A + 1
GP = 4 * TAPS + 4 + 2
O_GRP = O_CAW + KT * CP
O_LNA = O_GRP + GROUPS * GP
O_LN1 = O_LNA + 2 * KT
O_LN2 = O_LN1 + 2 * KT
O_PLE = O_LN2 + 2 * KT
O_DTB = O_PLE + KT
O_ALOG = O_DTB + 2 * HEADS
O_DSK = O_ALOG + 2 * HEADS
NPAR = O_DSK + HEADS
DTK, ADT, WDEC, DOUT, TOT = range(5)
BWD, FWD = 0, 1
LN_A, LN_1, LN_2 = range(3)
NORMS = 3
CONSTS = 15
LOG_TERMS = 8
E_BANKS = (6, 7, 4)


def build(nc, x_in, p_in, w_stream, w_dt, w_ple, par_in, out):
    ctx = ExitStack()
    with ctx:
        def sb(name, shape, dtype=F32, where=None):
            return (where or ctx).enter_context(nc.sbuf_tensor(name, shape, dtype))

        def sem(name):
            return ctx.enter_context(nc.semaphore(name))

        xh = sb("x_hi", [P, KT, T], F32R)
        xl = sb("x_lo", [P, KT, T], F32R)
        raw = sb("w_raw", [P, 2, WT])
        whi = sb("w_hi", [P, SLOTS, WT], F32R)
        wlo = sb("w_lo", [P, SLOTS, WT], F32R)
        u = sb("glu_out", [P, 2, T])
        za = sb("z_a", [P, KT, T])
        zb = sb("z_b", [P, KT, T])
        sg = sb("sigmoids", [P, T])
        par = sb("params", [P, NPAR])
        steps = sb("steps", [P, 5, 2, CH, HEADS])
        gtab = sb("group_steps", [P, 2, 5 * 2 * CH, HG])
        gad = sb("group_steps_split", [P, 2, 2, 2 * CH, HG], F32R)
        gpar = sb("group_params", [P, 2, GP])
        gdsk = sb("group_skip", [P, 2, HG])
        nega = sb("neg_a", [P, 2 * HEADS])
        U = sb("tri_le", [P, P])
        LW = sb("tri_ge", [P, P])
        SL = sb("tri_gt", [P, P])
        SU = sb("tri_lt", [P, P])
        SLR = sb("tri_gt_r", [P, P], F32R)
        SUR = sb("tri_lt_r", [P, P], F32R)
        ones = sb("ones", [P, P])
        mean1 = sb("ones_over_d", [P, P])
        ident = sb("ident", [P, P])
        neghalf = sb("neg_half", [P, CH])
        ms = sb("mean_squares", [P, CH])
        mse = sb("mean_squares_eps", [P, CH])
        rst = sb("group_rstd", [P, CH])

        caw = sb("conv_a_params", [P, 2, CP])
        eps = sb("eps", [P, 2])
        spare = sb("spare", [P, 5])

        with ExitStack() as r:
            cin = sb("conv_in", [P, 4, T], F32, r)
            feat = sb("xs_b_c", [P, 4, T], F32, r)
            xtok = sb("x_tok", [P, CH, GW], F32, r)
            btok = sb("b_tok", [P, CH, STATE], F32, r)
            ztok = sb("z_tok", [P, 2, T], F32, r)
            E = sb("decay", [P, CH, HG, P], F32, r)
            rhs = sb("seg_rhs", [P, 2, 2, HG, P], F32R, r)
            cb = sb("cb_masked", [P, 2, CH, P], F32, r)
            xw = sb("x_weighted", [P, 2, 2, GW], F32, r)
            H = sb("states", [P, CH * 2, GW], F32, r)
            y = sb("y_tok", [P, CH, GW], F32, r)
            tm = sb("tmp_m", [P, HG, P], F32, r)
            ty = sb("tmp_y", [P, 2, GW], F32, r)
            junk = sb("squares", [P, GW], F32, r)
        with ExitStack() as r:
            with ExitStack() as r_a:
                aah = sb("act_a_hi", [P, KT, T], F32R, r_a)
                aal = sb("act_a_lo", [P, KT, T], F32R, r_a)
            with ExitStack() as r_a:
                pin = sb("ple_p", [P, 2, T], F32, r_a)
                wpl = sb("w_ple_in", [P, 2, D], F32, r_a)
            sb("act_a_place", [P, 2 * KT, T], F32, r)
            with ExitStack() as r_b:
                abh = sb("act_b_hi", [P, KT, T], F32R, r_b)
                abl = sb("act_b_lo", [P, KT, T], F32R, r_b)
            with ExitStack() as r_b:
                dwh = sb("w_dt_hi", [P, T], F32R, r_b)
                dwl = sb("w_dt_lo", [P, T], F32R, r_b)
                esq = sb("e_squares", [P, KT, T], F32, r_b)
                erms = sb("e_rstd", [P, T], F32, r_b)
            sb("act_b_place", [P, 2 * KT, T], F32, r)
            rstd = sb("rstd", [P, T], F32, r)
        sb("region_1", [P, 33 * T + GW])
        with ExitStack() as r:
            yh = sb("y_hi", [P, 4, T], F32R, r)
            yl = sb("y_lo", [P, 4, T], F32R, r)
        ge = sb("gate_or_e", [P, KT, T])
        stepf = steps[:, :, :, :, :].rearrange("p k d c h -> p k (d c h)")
        tmf = tm[:, :, :].rearrange("p a b -> p (a b)")
        tyf = ty[:, :, :].rearrange("p a b -> p (a b)")

        bank = [ctx.enter_context(nc.psum_tensor(f"bank{b}", [P, T], F32)) for b in range(8)]

        def halves(b):
            return b[:, :].rearrange("p (c e) -> p c e", c=2)

        def quarters(b):
            return b[:, :].rearrange("p (c e) -> p c e", c=4)

        raw_ready = [sem(f"raw_ready{s}") for s in range(SLOTS)]
        hi_done = [sem(f"hi_done{s}") for s in range(SLOTS)]
        lo_done = [sem(f"lo_done{s}") for s in range(SLOTS)]
        used = [sem(f"used{s}") for s in range(SLOTS)]
        evac = [sem(f"evac{s}") for s in range(SLOTS)]
        tri_ready = sem("tri_ready")
        consts = sem("consts")
        x_loaded = [sem(f"x_loaded{m}") for m in range(KT // 2)]
        par_loaded = sem("par_loaded")
        p_loaded = sem("p_loaded")
        ple_loaded = sem("ple_loaded")
        dtw_loaded = sem("dtw_loaded")
        out_stored = sem("out_stored")
        xh_done = sem("xh_done")
        xl_done = sem("xl_done")
        zb_zero = sem("zb_zero")
        dtw_hi = sem("dtw_hi")
        dtw_lo = sem("dtw_lo")
        dt_done = sem("dt_done")
        dt_evac = sem("dt_evac")
        dt_v = sem("dt_v")
        dt_e = sem("dt_e")
        ad_ready = sem("ad_ready")
        cum_done = sem("cum_done")
        cum_exp = sem("cum_exp")
        nega_e = sem("nega_e")
        grp_ready = sem("grp_ready")
        conv_done = sem("conv_done")
        silu_done = sem("silu_done")
        tr_done = sem("tr_done")
        tok_evac = sem("tok_evac")
        cb_done = sem("cb_done")
        xw_ready = sem("xw_ready")
        seg_done = sem("seg_done")
        rhs_ready = sem("rhs_ready")
        exp_done = sem("exp_done")
        st_done = sem("st_done")
        st_evac = sem("st_evac")
        h_ready = sem("h_ready")
        m_ready = sem("m_ready")
        yo_done = sem("yo_done")
        xd_ready = sem("xd_ready")
        yp_read = sem("yp_read")
        yg_ready = sem("yg_ready")
        ss_done = sem("ss_done")
        rms_done = sem("rms_done")
        yn_ready = sem("yn_ready")
        yt_done = sem("yt_done")
        yh_done = sem("yh_done")
        yl_done = sem("yl_done")
        ua_ready = sem("ua_ready")
        zsum_ready = sem("zsum_ready")
        mean_done = sem("mean_done")
        xc_ready = sem("xc_ready")
        sq_ready = sem("sq_ready")
        sq_used = sem("sq_used")
        sqa_used = sem("sqa_used")
        vara_done = sem("vara_done")
        table_near = sem("table_near")
        std_ready = sem("std_ready")
        zn_ready = sem("zn_ready")
        zf_ready = sem("zf_ready")
        zh_ready = sem("zh_ready")
        al_done = sem("al_done")
        bh_done = sem("bh_done")
        bl_done = sem("bl_done")
        gb_ready = sem("gb_ready")
        mg_ready = sem("mg_ready")
        z1_ready = sem("z1_ready")
        fh_done = sem("fh_done")
        fl_done = sem("fl_done")
        e_done = sem("e_done")
        e_evac = sem("e_evac")
        esq_ready = sem("esq_ready")
        esq_used = sem("esq_used")
        estd_ready = sem("estd_ready")
        en_ready = sem("en_ready")
        pg_used = sem("pg_used")
        xn_ready = sem("xn_ready")
        dve_order = sem("dve_order")
        settled = sem("settled")
        EARLY = 2

        def seen(n):
            return n + EARLY

        def settle(e):
            e.sem_inc(settled, 1)

        def open_(e, *ss):
            for s in ss:
                e.sem_inc(s, EARLY)

        block = ctx.enter_context(nc.Block())

        @block.sync
        def _(sp):
            def tile(cyc, s):
                sp.wait_ge(lo_done[(s + 2) % SLOTS], seen(cyc + (1 if s >= 2 else 0)))
                sp.dma_start(raw[:, s % 2, :], w_stream[cyc, s]).then_inc(raw_ready[s], 16)

            sp.dma_start(tmf, w_dt[0]).then_inc(dtw_loaded, 16)
            for m in range(0, KT, 2):
                sp.dma_start(zb[:, m:m + 2, :], x_in[:, m:m + 2, :]).then_inc(x_loaded[m // 2], 16)
            sp.dma_start(raw[:, 0, :], w_stream[0, 0]).then_inc(raw_ready[0], 16)
            sp.dma_start(raw[:, 1, :], w_stream[0, 1]).then_inc(raw_ready[1], 16)
            tile(0, 2)
            tile(0, 3)
            with sp.Fori(1, ALL_CYCLES) as cyc:
                for s in range(SLOTS):
                    tile(cyc, s)
            sp.wait_ge(xn_ready, seen((LAYERS + 1) * KT))
            sp.dma_start(out, zb[:, :, :]).then_inc(out_stored, 16)
            sp.wait_ge(out_stored, 16)

        @block.gpsimd
        def _(gp):
            open_(gp, rhs_ready, xd_ready, rms_done, zb_zero, *lo_done)

            def lo(cyc, *slots, n=WT):
                for s in slots:
                    gp.wait_ge(hi_done[s], seen(cyc + 1))
                    gp.tensor_tensor(wlo[:, s, 0:n], raw[:, s % 2, 0:n], whi[:, s, 0:n].bitcast(F32),
                                     ALU.subtract).then_inc(lo_done[s], 1)

            def masked_steps(q, G, c):
                gp.wait_ge(seg_done, seen(CH * G + c))
                for d, m in ((FWD, U), (BWD, LW)):
                    for part in range(2):
                        ad = gad[:, q, part, d * CH + c, :].bitcast(F32).unsqueeze(2).broadcast_to([P, HG, P])
                        i = gp.tensor_tensor(rhs[:, d, part], ad, m[:, :].unsqueeze(1).broadcast_to([P, HG, P]), ALU.mult)
                i.then_inc(rhs_ready, 1)

            def skip(q, G):
                gp.wait_ge(tok_evac, seen(3 * G + 2))
                gp.wait_ge(yt_done, seen(2 * G))
                d = gdsk[:, q, :].unsqueeze(1).unsqueeze(3).broadcast_to([P, CH, HG, HEAD])
                v = "p c (h e) -> p c h e"
                gp.tensor_tensor(y[:, :, :].rearrange(v, h=HG), xtok[:, :, :].rearrange(v, h=HG), d,
                                 ALU.mult).then_inc(xd_ready, 1)

            def group_rms(G, part):
                c = slice(0, CH - 1) if part == 0 else slice(CH - 1, CH)
                gp.wait_ge(ss_done, seen(CH * G + c.stop))
                gp.wait_ge(yn_ready, seen(2 * G))
                settle(gp)
                gp.tensor_scalar(mse[:, c], ms[:, c], RMS_EPS, None, ALU.add).then_inc(rms_done, 1)
                gp.wait_ge(rms_done, seen(4 * G + 2 * part + 1))
                gp.tensor_tensor(rst[:, c], mse[:, c], neghalf[:, c], ALU.pow).then_inc(rms_done, 1)

            n = [0]

            def fill(dst, pattern=None, value=1.0):
                gp.memset(dst, value).then_inc(consts, 1)
                n[0] += 1
                if pattern:
                    gp.wait_ge(consts, n[0])
                    base, mult, step, op = pattern
                    gp.affine_select(out=dst, in_=dst, compare_op=op, fill=0.0, base=base,
                                     pattern=[[step, P]], channel_multiplier=mult).then_inc(consts, 1)
                    n[0] += 1

            fill(ones[:, :])
            fill(eps[:, 0:1], value=LN_EPS)
            fill(eps[:, 1:2], value=RMS_EPS)
            fill(mean1[:, :], value=1.0 / D)
            fill(neghalf[:, :], value=-0.5)
            fill(U[:, :], (0, -1, 1, ALU.is_ge))
            fill(LW[:, :], (0, 1, -1, ALU.is_ge))
            fill(SL[:, :], (0, 1, -1, ALU.is_gt))
            fill(SU[:, :], (0, -1, 1, ALU.is_gt))
            fill(ident[:, :], (0, 1, -1, ALU.is_equal))
            assert n[0] == CONSTS
            with gp.Fori(0, LAYERS) as L:
                base = L * CYCLES
                lo(base, 0, 1, 2, 3)
                gp.wait_ge(xl_done, seen(NORMS * KT * L + KT))
                settle(gp)
                gp.memset(zb[:, :, :], 0.0).then_inc(zb_zero, 1)
                with gp.Fori(0, PAIRS) as j:
                    c0 = base + j * PAIR_CYCLES
                    G0 = L * GROUPS + j * 2
                    lo(c0 + 1, 0, 1, 2, 3)
                    gp.wait_ge(grp_ready, seen(G0 + 1))
                    masked_steps(0, G0, 0)
                    lo(c0 + 2, 0, 1)
                    masked_steps(0, G0, 1)
                    lo(c0 + 2, 2)
                    masked_steps(0, G0, 2)
                    lo(c0 + 2, 3)
                    masked_steps(0, G0, 3)
                    skip(0, G0)
                    lo(c0 + 3, 0, 1)
                    gp.wait_ge(grp_ready, seen(G0 + 2))
                    masked_steps(1, G0 + 1, 0)
                    group_rms(G0, 0)
                    group_rms(G0, 1)
                    masked_steps(1, G0 + 1, 1)
                    lo(c0 + 3, 2, 3)
                    masked_steps(1, G0 + 1, 2)
                    masked_steps(1, G0 + 1, 3)
                    skip(1, G0 + 1)
                    lo(c0 + 4, 0, 1, 2, n=HALF)
                    lo(c0 + 4, 3, n=HALF)
                    group_rms(G0 + 1, 0)
                    group_rms(G0 + 1, 1)
                    lo(c0 + 5, 0, 1, 2, 3, n=HALF)
                    lo(c0 + 6, 0, 1, 2, 3)
                with gp.Fori(C_GATE_A, CYCLES - 1) as c:
                    lo(base + c + 1, 0, 1, 2, 3)

        @block.scalar
        def _(act):
            open_(act, xh_done, silu_done, tok_evac, exp_done, st_evac, ss_done, yh_done,
                  sq_ready, std_ready, zf_ready, zh_ready, bh_done, fh_done,
                  e_evac, esq_ready, estd_ready, dt_evac, dt_e, cum_exp, nega_e,
                  dtw_hi, *hi_done)

            def hi(cyc, *slots, n=WT):
                for s in slots:
                    act.wait_ge(raw_ready[s], (cyc + 1) * 16)
                    act.wait_ge(used[s], seen(cyc))
                    act.activation(whi[:, s, 0:n], raw[:, s % 2, 0:n], ACT.Copy).then_inc(hi_done[s], 1)

            def take(cyc, s, dst, func=ACT.Copy):
                act.wait_ge(used[s], seen(cyc + 1))
                act.activation(dst, bank[s][:, :], func).then_inc(evac[s], 1)

            def conv_input(G, c, cyc, s):
                take(cyc, s, cin[:, c, :])
                hi(cyc + 1, s)

            def z_gates(G, cyc, slots):
                act.wait_ge(yg_ready, seen(CH * G))
                for i, s in enumerate(slots):
                    take(cyc, s, ztok[:, i, :], ACT.Silu)
                    hi(cyc + 1, s)

            def silu(G, c):
                act.wait_ge(conv_done, seen(4 * G + c + 1))
                act.activation(feat[:, c, :], feat[:, c, :], ACT.Silu).then_inc(silu_done, 1)

            def xs_tokens(G, i):
                act.wait_ge(xd_ready, seen(G))
                act.wait_ge(yo_done, seen(CH * G))
                act.wait_ge(tr_done, seen(4 * G + i + 1))
                act.activation(xtok[:, 2 * i:2 * i + 2, :], halves(bank[6 + i]), ACT.Copy).then_inc(tok_evac, 1)

            def b_tokens(G):
                act.wait_ge(tr_done, seen(4 * G + 3))
                act.activation(btok[:, :, :], quarters(bank[6]), ACT.Copy).then_inc(tok_evac, 1)

            def decay(G, c):
                act.wait_ge(seg_done, seen(CH * G + c + 1))
                act.activation(E[:, c], quarters(bank[4 + c % 2]), ACT.Exp).then_inc(exp_done, 1)

            def state(G, n):
                act.wait_ge(st_done, seen(3 * G + n + 1))
                dst = (H[:, 3:5, :], H[:, 0:6:5, :], H[:, 2:8:5, :])[n]
                act.activation(dst, halves(bank[6 + n % 2]), ACT.Copy).then_inc(st_evac, 1)

            def square(G, c):
                act.wait_ge(ss_done, seen(CH * G + c))
                act.wait_ge(yg_ready, seen(CH * G + c + 1))
                act.activation(junk[:, :], y[:, c, :], ACT.Square, scale=GW ** -0.5,
                               accum_out=ms[:, c:c + 1]).then_inc(ss_done, 1)

            def round_y(q, G, i):
                act.wait_ge(yt_done, seen(2 * G + i + 1))
                act.activation(yh[:, 2 * q + i, :], bank[4 + i][:, :], ACT.Copy,
                               scale=gpar[:, q, 24 + i:25 + i]).then_inc(yh_done, 1)

            def norm_stats(k, z, summed, n):
                for m in range(KT):
                    act.wait_ge(xc_ready, seen(k * KT + m + 1))
                    if m >= 2:
                        act.wait_ge(summed, seen(n + m - 1))
                    act.activation(u[:, m % 2, :], z[:, m, :], ACT.Square).then_inc(sq_ready, 1)

            def want(n, func):
                act.activation(spare[:, n:n + 1], eps[:, 0:1], func).then_inc(table_near, 1)

            def norm_std():
                act.activation(rstd[:, :], bank[5][:, :], ACT.Sqrt, bias=eps[:, 0:1]).then_inc(std_ready, 1)

            def norm_round(k, m, z, off):
                act.wait_ge(zn_ready, seen(k * KT + m + 1))
                act.activation(xh[:, m, :], z[:, m, :], ACT.Identity,
                               bias=par[:, off + KT + m:off + KT + m + 1]).then_inc(zh_ready, 1)

            act.wait_ge(dtw_loaded, 16)
            act.activation(dwh[:, :], tmf, ACT.Copy).then_inc(dtw_hi, 1)
            act.wait_ge(consts, CONSTS)
            settle(act)
            with act.Fori(0, LAYERS) as L:
                base = L * CYCLES
                want(4, ACT.Exp)
                act.wait_ge(used[3], seen(base))
                for m in range(KT):
                    if m % 2 == 0:
                        act.wait_ge(x_loaded[m // 2], 16)
                    act.wait_ge(xn_ready, seen(KT * L + m + 1))
                    act.activation(xh[:, m, :], zb[:, m, :], ACT.Copy).then_inc(xh_done, 1)
                act.dma_start(par[:, :], par_in[L]).then_inc(par_loaded, 16)
                hi(base, 0, 1)
                act.wait_ge(dt_done, seen(2 * L + 1))
                act.activation(sg[0:2 * HEADS, :], bank[4][0:2 * HEADS, :], ACT.Copy).then_inc(dt_evac, 1)
                act.wait_ge(par_loaded, 16 * (L + 1))
                act.activation(nega[:, :], par[:, O_ALOG:O_ALOG + 2 * HEADS], ACT.Exp).then_inc(nega_e, 1)
                hi(base, 2)
                act.wait_ge(dt_v, seen(L + 1))
                act.activation(ty[:, 1, :], ty[:, 0, :], ACT.Abs).then_inc(dt_e, 1)
                act.wait_ge(dt_e, seen(2 * L + 1))
                act.activation(ty[:, 1, :], ty[:, 1, :], ACT.Exp, scale=-1.0).then_inc(dt_e, 1)
                hi(base, 3)
                act.wait_ge(cum_done, seen(L + 1))
                act.activation(stepf[:, WDEC:DOUT + 1, :], halves(bank[5]), ACT.Exp).then_inc(cum_exp, 1)
                act.activation(stepf[:, TOT, :], bank[6][:, 0:GW], ACT.Exp).then_inc(cum_exp, 1)
                with act.Fori(0, PAIRS) as j:
                    c0 = base + j * PAIR_CYCLES
                    G0 = L * GROUPS + j * 2
                    G1 = G0 + 1
                    act.wait_ge(conv_done, seen(4 * G0))
                    for c in range(4):
                        conv_input(G0, c, c0, c)
                    z_gates(G0, c0 + 1, (0, 1))
                    silu(G0, 0)
                    silu(G0, 1)
                    act.wait_ge(conv_done, seen(4 * G0 + 2))
                    conv_input(G1, 0, c0 + 1, 2)
                    xs_tokens(G0, 0)
                    xs_tokens(G0, 1)
                    silu(G0, 2)
                    silu(G0, 3)
                    decay(G0, 0)
                    conv_input(G1, 1, c0 + 1, 3)
                    decay(G0, 1)
                    b_tokens(G0)
                    act.wait_ge(conv_done, seen(4 * G0 + 4))
                    conv_input(G1, 2, c0 + 2, 0)
                    decay(G0, 2)
                    state(G0, 0)
                    silu(G1, 0)
                    silu(G1, 1)
                    conv_input(G1, 3, c0 + 2, 1)
                    decay(G0, 3)
                    state(G0, 1)
                    state(G0, 2)
                    for c in range(CH):
                        square(G0, c)
                    z_gates(G1, c0 + 2, (2, 3))
                    decay(G1, 0)
                    want(2, ACT.Silu)
                    xs_tokens(G1, 0)
                    xs_tokens(G1, 1)
                    round_y(0, G0, 0)
                    round_y(0, G0, 1)
                    silu(G1, 2)
                    silu(G1, 3)
                    b_tokens(G1)
                    hi(c0 + 4, 0, n=HALF)
                    take(c0 + 3, 1, sg[:, :], ACT.Sigmoid)
                    decay(G1, 1)
                    state(G1, 0)
                    state(G1, 1)
                    decay(G1, 2)
                    state(G1, 2)
                    hi(c0 + 4, 1, n=HALF)
                    decay(G1, 3)
                    want(3, ACT.Sigmoid)
                    hi(c0 + 4, 2, n=HALF)
                    act.wait_ge(evac[0], seen(c0 + 4))
                    take(c0 + 3, 3, sg[:, :], ACT.Sigmoid)
                    hi(c0 + 4, 3, n=HALF)
                    for c in range(CH):
                        square(G1, c)
                    round_y(1, G1, 0)
                    round_y(1, G1, 1)
                    hi(c0 + 5, 0, 1, 2, 3, n=HALF)
                    hi(c0 + 6, 0, 1, 2, 3)
                act.wait_ge(yl_done, seen(2 * GROUPS * (L + 1)))
                settle(act)
                with act.Fori(0, KT // SLOTS) as i:
                    for s in range(SLOTS):
                        take(base + C_GATE_A + i, s, ge[:, SLOTS * i + s, :], ACT.Sigmoid)
                        hi(base + C_GATE_A + i + 1, s)
                k = NORMS * L + LN_A
                norm_stats(k, za, sqa_used, KT * L)

                def gate_b(i, s):
                    act.wait_ge(gb_ready, seen(KT * L + SLOTS * i + s))
                    take(base + C_GATE_B + i, s, sg[:, :], ACT.Sigmoid)

                act.wait_ge(vara_done, seen(L + 1))
                norm_std()
                for s in range(SLOTS):
                    gate_b(0, s)
                    hi(base + C_GATE_B + 1, s)
                for m in range(KT + 1):
                    if m < KT:
                        act.wait_ge(zn_ready, seen(k * KT + m + 1))
                        act.activation(za[:, m, :], za[:, m, :], ACT.Silu, scale=par[:, O_LNA + m:O_LNA + m + 1],
                                       bias=par[:, O_LNA + KT + m:O_LNA + KT + m + 1]).then_inc(zf_ready, 1)
                    if m >= 1:
                        act.wait_ge(zf_ready, seen(2 * KT * L + m))
                        act.activation(aah[:, m - 1, :], za[:, m - 1, :], ACT.Copy).then_inc(zh_ready, 1)
                    if m in (4, 6, 8):
                        hi(base + C_A_OUT, m // 2 - 2)
                for s in range(SLOTS):
                    gate_b(1, s)
                hi(base + C_A_OUT, 3)
                with act.Fori(0, KT // SLOTS) as i:
                    for s in range(SLOTS):
                        act.wait_ge(mg_ready, seen(KT * L + SLOTS * i + s + 1))
                        act.activation(abh[:, SLOTS * i + s, :], zb[:, SLOTS * i + s, :], ACT.Copy).then_inc(bh_done, 1)
                        hi(base + C_A_OUT + i + 1, s)
                act.wait_ge(used[3], seen(base + C_O))
                act.dma_start(pin[:, :, :], p_in[L]).then_inc(p_loaded, 16)
                act.dma_start(wpl[:, :, :], w_ple[L]).then_inc(ple_loaded, 16)
                with act.Fori(C_O, C_UP0) as c:
                    hi(base + c + 1, 0, 1, 2, 3)
                k = NORMS * L + LN_1
                want(0, ACT.Sqrt)
                norm_stats(k, za, sq_used, 2 * KT * L)
                act.wait_ge(sq_used, seen(2 * KT * L + KT))
                norm_std()

                def ple(m):
                    act.wait_ge(e_done, seen(KT * L + m + 1))
                    act.activation(ge[:, m, :], bank[E_BANKS[m % 3]][:, :], ACT.Copy).then_inc(e_evac, 1)

                ple(0)
                ple(1)
                for m in range(KT):
                    norm_round(k, m, za, O_LN1)
                    if m + 2 < KT:
                        ple(m + 2)
                for m in range(KT):
                    act.wait_ge(xl_done, seen(KT * k + m + 1))
                    act.activation(za[:, m, :], za[:, m, :], ACT.Identity,
                                   bias=par[:, O_LN1 + KT + m:O_LN1 + KT + m + 1]).then_inc(zf_ready, 1)

                def swiglu(c0, count, dst):
                    with act.Fori(0, count // 2) as i:
                        for r in range(2):
                            take(c0 + i, 2 * r, sg[:, :], ACT.Silu)
                            hi(c0 + i + 1, 2 * r)
                            act.wait_ge(evac[2 * r + 1], seen(c0 + i + 1))
                            act.activation(dst[:, 2 * i + r, :], u[:, r, :], ACT.Copy).then_inc(fh_done, 1)
                            hi(c0 + i + 1, 2 * r + 1)

                swiglu(base + C_UP0, KT, aah)
                swiglu(base + C_UP1, KT, abh)
                with act.Fori(C_DOWN0, C_UP2) as c:
                    hi(base + c + 1, 0, 1, 2, 3)
                swiglu(base + C_UP2, LAST, aah)
                with act.Fori(C_DOWN1, C_DOWN2) as c:
                    hi(base + c + 1, 0, 1, 2, 3)
                act.wait_ge(used[3], seen(base + C_DOWN2))
                act.dma_start(tmf, w_dt[L + 1]).then_inc(dtw_loaded, 16)
                for m in range(KT):
                    act.activation(esq[:, m, :], ge[:, m, :], ACT.Square).then_inc(esq_ready, 1)
                with act.Fori(C_DOWN2, C_PLE) as c:
                    hi(base + c + 1, 0, 1, 2, 3)
                k = NORMS * L + LN_2
                want(1, ACT.Sqrt)
                norm_stats(k, zb, sq_used, 2 * KT * L + KT)
                act.wait_ge(sq_used, seen(2 * KT * (L + 1)))
                norm_std()
                for m in range(KT):
                    norm_round(k, m, zb, O_LN2)
                act.wait_ge(esq_used, seen(L + 1))
                act.activation(erms[:, :], bank[6][:, :], ACT.Sqrt, bias=eps[:, 1:2]).then_inc(estd_ready, 1)
                act.wait_ge(dtw_loaded, 16 * (L + 2))
                act.activation(dwh[:, :], tmf, ACT.Copy).then_inc(dtw_hi, 1)
                for i in range(KT // SLOTS):
                    for s in range(SLOTS):
                        act.wait_ge(pg_used, seen(KT * L + SLOTS * i + s))
                        take(base + C_PLE + i, s, sg[:, :], ACT.Sigmoid)
                        if i == 0:
                            hi(base + C_PLE + 1, s)


        @block.tensor
        def _(pe):
            open_(pe, dt_done, cum_done, tr_done, seg_done, st_done, yo_done, yt_done,
                  mean_done, sq_used, vara_done, e_done, esq_used, *used)

            def three(dst, wh, wl, mh, ml, first, last):
                pe.matmul(dst, wh, mh, start=first, stop=False)
                pe.matmul(dst, wh, ml, start=False, stop=False)
                return pe.matmul(dst, wl, mh, start=False, stop=last)

            def slot_ready(cyc, s):
                pe.wait_ge(lo_done[s], seen(cyc + 1))
                pe.wait_ge(evac[s], seen(cyc))

            def dense(cyc, s, mh, ml, nk=KT, ks=None):
                ks = ks or range(nk)
                if ks[0] == 0:
                    slot_ready(cyc, s)
                for k in ks:
                    w = slice(k * P, (k + 1) * P)
                    i = three(bank[s][:, :], whi[:, s, w], wlo[:, s, w], mh[:, k, :], ml[:, k, :],
                              k == 0, k == nk - 1)
                if ks[-1] == nk - 1:
                    i.then_inc(used[s], 1)

            def z_tiles(cyc, s, chunks=range(CH)):
                if chunks[0] == 0:
                    slot_ready(cyc, s)
                    slot_ready(cyc, s + 1)
                for c in chunks:
                    dst = halves(bank[s + c // 2])[:, c % 2, :].rearrange("p (b e) -> p b e", b=2)
                    for k in range(KT):
                        t, w = slice(c * P, (c + 1) * P), slice(k * P, (k + 1) * P)
                        h, l, end = whi[:, s:s + 2, w], wlo[:, s:s + 2, w], k == KT - 1
                        pe.matmul(dst, xh[:, k, t], h, start=k == 0, stop=False)
                        pe.matmul(dst, xh[:, k, t], l, start=False, stop=False)
                        if c < CH - 1 or not end:
                            pe.matmul(dst, xl[:, k, t], h, start=False, stop=end)
                        else:
                            pe.matmul(dst[:, 0], xl[:, k, t], h[:, 0], start=False, stop=False).then_inc(used[s], 1)
                            pe.matmul(dst[:, 1], xl[:, k, t], h[:, 1], start=False, stop=end).then_inc(used[s + 1], 1)

            def xs_transpose(G):
                for i in range(2):
                    pe.wait_ge(silu_done, seen(4 * G + 2))
                    pe.wait_ge(yp_read, seen(CH * G))
                    for n in range(4):
                        c, t = 2 * i + n // 2, n % 2
                        q = pe.transpose(bank[6 + i][:, n * P:(n + 1) * P], feat[:, t, c * P:(c + 1) * P], ident[:, :])
                    q.then_inc(tr_done, 1)

            def b_transpose(G):
                pe.wait_ge(silu_done, seen(4 * G + 3))
                pe.wait_ge(tok_evac, seen(3 * G + 1))
                for c in range(CH):
                    q = pe.transpose(bank[6][:, c * P:(c + 1) * P], feat[:, 2, c * P:(c + 1) * P], ident[:, :])
                q.then_inc(tr_done, 1)

            def c_dot_b(G):
                pe.wait_ge(silu_done, seen(4 * G + 4))
                pe.wait_ge(tok_evac, seen(3 * G + 2))
                for c in range(CH):
                    t = slice(c * P, (c + 1) * P)
                    q = pe.matmul(bank[7][:, t], feat[:, 2, t], feat[:, 3, t], start=True, stop=True)
                q.then_inc(tr_done, 1)

            def exponent(G, c, first=False):
                pe.wait_ge(rhs_ready, seen(CH * G + c + 1))
                if c == 0:
                    pe.wait_ge(yp_read, seen(CH * G))
                elif c > 1:
                    pe.wait_ge(exp_done, seen(CH * G + c - 1))
                if c == 1 or first:
                    pe.wait_ge(yl_done, seen(2 * G))
                b = quarters(bank[4 + c % 2])
                pe.matmul(b, SLR[:, :], rhs[:, FWD, 0], start=True, stop=False)
                pe.matmul(b, SLR[:, :], rhs[:, FWD, 1], start=False, stop=False)
                pe.matmul(b, SUR[:, :], rhs[:, BWD, 0], start=False, stop=False)
                pe.matmul(b, SUR[:, :], rhs[:, BWD, 1], start=False, stop=True).then_inc(seg_done, 1)

            def state(G, n):
                pe.wait_ge(xw_ready, seen(3 * G + n + 1))
                if n == 0:
                    pe.wait_ge(tok_evac, seen(3 * G + 3))
                elif n == 1:
                    pe.wait_ge(cb_done, seen(G + 1))
                else:
                    pe.wait_ge(st_evac, seen(3 * G + 1))
                if n == 0:
                    pe.matmul(bank[6][:, 0:GW], btok[:, 0, :], xw[:, 0, 0, :], start=True, stop=True)
                    q = pe.matmul(bank[6][:, GW:], btok[:, CH - 1, :], xw[:, 0, 1, :], start=True, stop=True)
                else:
                    q = pe.matmul(halves(bank[6 + n % 2]), btok[:, n, :], xw[:, n % 2], start=True, stop=True)
                q.then_inc(st_done, 1)

            def y_chunk(G, c):
                pe.wait_ge(m_ready, seen(CH * G + c + 1))
                if c < 2:
                    pe.wait_ge(st_evac, seen(3 * G + 3 - c))
                else:
                    pe.wait_ge(yp_read, seen(CH * G + c - 1))
                for h in range(HG):
                    e = slice(h * HEAD, (h + 1) * HEAD)
                    pe.matmul(bank[6 + c % 2][:, e], E[:, c, h, :], xtok[:, c, e], start=True, stop=True)
                pe.wait_ge(h_ready, seen(G + 1))
                if c < 2:
                    pe.wait_ge(exp_done, seen(CH * G + c + 3))
                a, b = {0: (BWD, BWD + 1), CH - 1: (FWD, FWD + 1)}.get(c, (BWD, FWD + 1))
                pe.matmul(halves(bank[4 + c % 2])[:, a:b, :], feat[:, 3, c * P:(c + 1) * P],
                          H[:, 2 * c + a:2 * c + b, :], start=True, stop=True).then_inc(yo_done, 1)

            def y_transpose(G, ahead=0):
                pe.wait_ge(yn_ready, seen(2 * (G + 1)))
                pe.wait_ge(exp_done, seen(CH * (G + 1) + ahead))
                pe.wait_ge(yp_read, seen(CH * (G + 1)))
                for i in range(2):
                    for c in range(CH):
                        q = pe.transpose(bank[4 + i][:, c * P:(c + 1) * P], y[:, c, i * P:(i + 1) * P], ident[:, :])
                    q.then_inc(yt_done, 1)

            def mean(k):
                pe.wait_ge(zsum_ready, seen(k + 1))
                pe.matmul(bank[4][:, :], mean1[:, :], sg[:, :], start=True, stop=True).then_inc(mean_done, 1)

            def var(k):
                for m in range(KT):
                    pe.wait_ge(sq_ready, seen(k * KT + m + 1))
                    pe.matmul(bank[5][:, :], mean1[:, :], u[:, m % 2, :], start=m == 0,
                              stop=m == KT - 1).then_inc(sq_used, 1)

            def phase(base, first, end, mh, ml, nk=KT, ready=None):
                if ready:
                    slot_ready(base + first, 0)
                    for k in range(nk):
                        ready(k)
                        dense(base + first, 0, mh, ml, nk, ks=(k,))
                    for s in range(1, SLOTS):
                        dense(base + first, s, mh, ml, nk)
                    first += 1
                settle(pe)
                with pe.Fori(first, end) as c:
                    for s in range(SLOTS):
                        dense(base + c, s, mh, ml, nk)

            def cumulative(L):
                pe.wait_ge(ad_ready, seen(L + 1))
                a = stepf[:, ADT, :].rearrange("p (d e) -> p d e", d=2)
                for o, d, m in ((0, BWD, SU), (1, FWD, SL), (2, BWD, LW), (3, FWD, U)):
                    pe.matmul(quarters(bank[5])[:, o, :], m[:, :], a[:, d, :], start=True, stop=True)
                pe.matmul(bank[6][:, 0:GW], ones[:, :], stepf[:, ADT, :], start=True, stop=True).then_inc(cum_done, 1)

            def pair(L, base, j, first=False):
                c0 = base + j * PAIR_CYCLES
                G0 = L * GROUPS + j * 2
                G1 = G0 + 1
                low, high = range(KT // 2), range(KT // 2, KT)
                dense(c0, 0, xh, xl)
                dense(c0, 1, xh, xl)
                if first:
                    cumulative(L)
                dense(c0, 2, xh, xl)
                dense(c0, 3, xh, xl)
                z_tiles(c0 + 1, 0)
                dense(c0 + 1, 2, xh, xl)
                xs_transpose(G0)
                exponent(G0, 0, True)
                dense(c0 + 1, 3, xh, xl)
                b_transpose(G0)
                c_dot_b(G0)
                exponent(G0, 1)
                dense(c0 + 2, 0, xh, xl)
                exponent(G0, 2)
                state(G0, 0)
                dense(c0 + 2, 1, xh, xl)
                exponent(G0, 3)
                state(G0, 1)
                state(G0, 2)
                z_tiles(c0 + 2, 2, (0, 1))
                y_chunk(G0, 0)
                z_tiles(c0 + 2, 2, (2,))
                y_chunk(G0, 1)
                y_chunk(G0, 2)
                z_tiles(c0 + 2, 2, (3,))
                y_chunk(G0, 3)
                dense(c0 + 3, 0, xh, xl)
                exponent(G1, 0)
                xs_transpose(G1)
                dense(c0 + 3, 1, xh, xl, ks=low)
                y_transpose(G0, 1)
                dense(c0 + 3, 1, xh, xl, ks=high)
                b_transpose(G1)
                c_dot_b(G1)
                exponent(G1, 1)
                dense(c0 + 3, 2, xh, xl, ks=low)
                state(G1, 0)
                state(G1, 1)
                exponent(G1, 2)
                dense(c0 + 3, 2, xh, xl, ks=high)
                state(G1, 2)
                exponent(G1, 3)
                dense(c0 + 3, 3, xh, xl, ks=low)
                y_chunk(G1, 0)
                y_chunk(G1, 1)
                dense(c0 + 3, 3, xh, xl, ks=high)
                y_chunk(G1, 2)
                y_chunk(G1, 3)
                for s in (0, 1, 3):
                    dense(c0 + 4, s, yh, yl, 4, ks=(0, 1))
                y_transpose(G1)
                dense(c0 + 4, 2, yh, yl, 4, ks=(0, 1))
                pe.wait_ge(yl_done, seen(2 * (G0 + 2)))
                for s in range(SLOTS):
                    dense(c0 + 4, s, yh, yl, 4, ks=(2, 3))
                for s in range(SLOTS):
                    dense(c0 + 5, s, yh, yl, 4)

            pe.wait_ge(consts, CONSTS)
            pe.wait_ge(tri_ready, 1)
            settle(pe)
            with pe.Fori(0, LAYERS) as L:
                base = L * CYCLES
                pe.wait_ge(dtw_lo, seen(L + 1))
                for k in range(KT):
                    pe.wait_ge(xl_done, seen(NORMS * KT * L + k + 1))
                    w = slice(k * 2 * HEADS, (k + 1) * 2 * HEADS)
                    q = three(bank[4][0:2 * HEADS, :], dwh[:, w], dwl[:, w], xh[:, k, :], xl[:, k, :], k == 0, k == KT - 1)
                q.then_inc(dt_done, 1)
                pe.wait_ge(dt_evac, seen(L + 1))
                settle(pe)
                for c in range(CH):
                    q = pe.transpose(bank[6][:, c * 2 * HEADS:(c + 1) * 2 * HEADS], sg[0:2 * HEADS, c * P:(c + 1) * P],
                                     ident[0:2 * HEADS, 0:2 * HEADS])
                q.then_inc(dt_done, 1)
                pair(L, base, 0, True)
                with pe.Fori(1, PAIRS) as j:
                    pair(L, base, j)
                phase(base, C_GATE_A, C_GATE_B, xh, xl)
                k = NORMS * L
                mean(k)
                for s in range(SLOTS):
                    dense(base + C_GATE_B, s, xh, xl)
                    if s == 1:
                        pe.wait_ge(sqa_used, seen(KT * (L + 1)))
                        pe.matmul(bank[5][:, :], mean1[:, :], rstd[:, :], start=True, stop=True).then_inc(vara_done, 1)
                phase(base, C_GATE_B + 1, C_A_OUT, xh, xl)
                phase(base, C_A_OUT, C_O, aah, aal, ready=lambda m: pe.wait_ge(al_done, seen(KT * L + m + 1)))
                phase(base, C_O, C_UP0, abh, abl, ready=lambda m: pe.wait_ge(bl_done, seen(KT * L + m + 1)))

                def ple(m):
                    if m >= 3:
                        pe.wait_ge(e_evac, seen(KT * L + m - 2))
                    for h in range(2):
                        q = pe.matmul(bank[E_BANKS[m % 3]][:, :], wpl[:, h, m * P:(m + 1) * P], pin[:, h, :],
                                      start=h == 0, stop=h == 1)
                    q.then_inc(e_done, 1)

                pe.wait_ge(p_loaded, 16 * (L + 1))
                pe.wait_ge(ple_loaded, 16 * (L + 1))
                ple(0)
                mean(k + 1)
                ple(1)
                var(k + 1)
                for m in range(2, KT):
                    ple(m)
                phase(base, C_UP0, C_DOWN0, xh, xl, ready=lambda m: pe.wait_ge(xl_done, seen(KT * (k + 1) + m + 1)))
                pe.wait_ge(fl_done, seen(FT * L + KT))
                phase(base, C_DOWN0, C_UP2, aah, aal)
                phase(base, C_UP2, C_DOWN1, xh, xl)
                phase(base, C_DOWN1, C_DOWN2, abh, abl)
                pe.wait_ge(fl_done, seen(FT * (L + 1)))
                phase(base, C_DOWN2, C_PLE, aah, aal, LAST)

                def e_mean_square(tiles):
                    for m in tiles:
                        pe.wait_ge(esq_ready, seen(KT * L + m + 1))
                        q = pe.matmul(bank[6][:, :], mean1[:, :], esq[:, m, :], start=m == 0, stop=m == KT - 1)
                    if tiles[-1] == KT - 1:
                        q.then_inc(esq_used, 1)

                e_mean_square(range(2))
                mean(k + 2)
                e_mean_square(range(2, 4))
                var(k + 2)
                e_mean_square(range(4, KT))
                phase(base, C_PLE, CYCLES, xh, xl, ready=lambda m: pe.wait_ge(xl_done, seen(KT * (k + 2) + m + 1)))

        @block.vector
        def _(dve):
            open_(dve, xl_done, dtw_lo, dt_v, ad_ready, grp_ready, conv_done, cb_done,
                  xw_ready, h_ready, m_ready, yp_read, yg_ready, yn_ready, yl_done,
                  ua_ready, xc_ready, zsum_ready, sqa_used, zn_ready, al_done, bl_done, gb_ready, mg_ready,
                  z1_ready, fl_done, en_ready, pg_used, xn_ready, *evac)
            dve.sem_inc(xn_ready, KT)
            order = [0]

            def step(ins):
                ins.then_inc(dve_order, 1)
                order[0] += 1

            def issued(but=0):
                return order[0] - but

            def restart():
                if order[0]:
                    settle(dve)
                    dve.wait_ge(dve_order, issued())
                    dve.sem_clear(dve_order)
                    order[0] = 0

            def spread(t, shape):
                return t.unsqueeze(len(t.shape)).broadcast_to([P, *shape, HEAD])

            def heads(t):
                return t.rearrange("p (h e) -> p h e", h=HG)

            def group_params(q, G, j2):
                dve.wait_ge(xd_ready, seen(G - 1))
                dve.wait_ge(yl_done, seen(2 * (G - q)))
                g = j2
                src = stepf[:, :, :].rearrange("p k (a h) -> p (k a) h", h=HEADS)
                step(dve.tensor_copy(gpar[:, q, :], par[:, bass.ds(O_GRP + g * GP, GP)]))
                step(dve.tensor_copy(gdsk[:, q, :], par[:, bass.ds(O_DSK + g * HG, HG)]))
                step(dve.tensor_copy(gtab[:, q], src[:, :, bass.ds(g * HG, HG)]))
                dve.wait_ge(dve_order, issued())
                ad = gtab[:, q, ADT * 2 * CH:(ADT + 1) * 2 * CH, :]
                step(dve.tensor_copy(gad[:, q, 0], ad))
                dve.wait_ge(dve_order, issued())
                dve.tensor_tensor(gad[:, q, 1], ad, gad[:, q, 0].bitcast(F32), ALU.subtract).then_inc(grp_ready, 1)

            def taps(outs, ins, ws, count, finish, between=lambda n: None):
                mid = count // 2
                for n, k in enumerate([mid] + [k for k in range(count) if k != mid]):
                    for i in range(2):
                        w, o = ws[i], k - mid
                        a, b = max(0, -o), T - max(0, o)
                        if n == 0:
                            step(dve.tensor_scalar(outs[i], ins[i], w[:, k:k + 1], ws[2 + i], ALU.mult, ALU.add))
                            continue
                        dve.wait_ge(dve_order, issued(0 if n == count - 1 and i else 1))
                        q = dve.scalar_tensor_tensor(out=outs[i][:, a:b], in0=ins[i][:, a + o:b + o], scalar=w[:, k:k + 1],
                                                     in1=outs[i][:, a:b], op0=ALU.mult, op1=ALU.add)
                        if n == count - 1:
                            q.then_inc(finish, 1)
                        else:
                            step(q)
                    between(n)

            def conv(q, G, i, tiles):
                for cyc, s in tiles:
                    dve.wait_ge(evac[s], seen(cyc + 1))
                if i == 0:
                    dve.wait_ge(tr_done, seen(4 * G - 2 if q else 4 * G))
                else:
                    dve.wait_ge(tr_done, seen(4 * G))
                    dve.wait_ge(yo_done, seen(CH * G))
                taps([feat[:, i, :], feat[:, i + 1, :]], [cin[:, i, :], cin[:, i + 1, :]],
                     [gpar[:, q, (i + c) * TAPS:(i + c + 1) * TAPS] for c in range(2)]
                     + [gpar[:, q, 4 * TAPS + i + c:4 * TAPS + i + c + 1] for c in range(2)],
                     TAPS, conv_done)

            def weighted_xs(q, G, n):
                dve.wait_ge(st_done, seen(3 * G + n // 2))
                dve.wait_ge(tok_evac, seen(3 * G + 2))
                for part, c, d in (((0, 0, FWD), (1, CH - 1, BWD)), ((BWD, 1, BWD), (FWD, 1, FWD)),
                                   ((BWD, 2, BWD), (FWD, 2, FWD)))[n]:
                    w = gtab[:, q, :, :].rearrange("p (k d c) h -> p k d c h", k=5, d=2)[:, WDEC, d, c, :]
                    r = dve.tensor_tensor(heads(xw[:, n % 2, part, :]), heads(xtok[:, c, :]), spread(w, [HG]), ALU.mult)
                    if part == (0, BWD, BWD)[n]:
                        step(r)
                    else:
                        r.then_inc(xw_ready, 1)

            def mask_cb(G):
                dve.wait_ge(tr_done, seen(4 * G + 4))
                for d, m in ((FWD, U), (BWD, LW)):
                    r = dve.tensor_tensor(cb[:, d], quarters(bank[7]), m[:, :].unsqueeze(1).broadcast_to([P, CH, P]), ALU.mult)
                    if d == FWD:
                        step(r)
                    else:
                        r.then_inc(cb_done, 1)

            def entering(q, G):
                g = gtab[:, q, :, :].rearrange("p (k d c) h -> p k d c h", k=5, d=2)
                dve.wait_ge(st_evac, seen(3 * G + 2))

                def carry(n, src, d, c):
                    return dve.tensor_tensor(heads(ty[:, n, :]), heads(H[:, src, :]), spread(g[:, TOT, d, c, :], [HG]), ALU.mult)

                def gain(n, dst):
                    return dve.tensor_tensor(H[:, dst, :], H[:, dst, :], ty[:, n, :], ALU.add)

                dve.wait_ge(yp_read, seen(CH * G))
                dve.wait_ge(dve_order, issued())
                step(carry(0, 3, FWD, 1))
                step(carry(1, 4, BWD, 2))
                dve.wait_ge(dve_order, issued(1))
                step(gain(0, 5))
                dve.wait_ge(st_evac, seen(3 * G + 3))
                dve.wait_ge(dve_order, issued(1))
                step(gain(1, 2))
                dve.wait_ge(dve_order, issued(1))
                step(carry(0, 5, FWD, 2))
                dve.wait_ge(dve_order, issued(1))
                step(carry(1, 2, BWD, 1))
                dve.wait_ge(dve_order, issued(1))
                step(gain(0, 7))
                dve.wait_ge(dve_order, issued(1))
                gain(1, 0).then_inc(h_ready, 1)

            def mix(q, G, c):
                g = gtab[:, q, :, :].rearrange("p (k d c) h -> p k d c h", k=5, d=2)
                dve.wait_ge(cb_done, seen(G + 1))
                dve.wait_ge(m_ready, seen(CH * G + c))
                step(dve.tensor_tensor(tm[:, :, :], cb[:, BWD, c, :].unsqueeze(1).broadcast_to([P, HG, P]),
                                       g[:, DTK, BWD, c, :].unsqueeze(2).broadcast_to([P, HG, P]), ALU.mult))
                dve.wait_ge(dve_order, issued())
                for h in range(HG):
                    step(dve.scalar_tensor_tensor(out=tm[:, h, :], in0=cb[:, FWD, c, :], scalar=g[:, DTK, FWD, c, h:h + 1],
                                                  in1=tm[:, h, :], op0=ALU.mult, op1=ALU.add))
                dve.wait_ge(dve_order, issued())
                dve.wait_ge(exp_done, seen(CH * G + c + 1))
                dve.tensor_tensor(E[:, c], E[:, c], tm[:, :, :], ALU.mult).then_inc(m_ready, 1)

            def outputs(q, G, c):
                g = gtab[:, q, :, :].rearrange("p (k d c) h -> p k d c h", k=5, d=2)
                dve.wait_ge(yo_done, seen(CH * G + c + 1))
                if c == 0:
                    dve.wait_ge(xd_ready, seen(G + 1))
                    dve.wait_ge(h_ready, seen(G + 1))
                off, yd = bank[4 + c % 2], bank[6 + c % 2][:, 0:GW]
                if 0 < c < CH - 1:
                    step(dve.tensor_tensor(ty[:, :, :].rearrange("p d (h e) -> p d h e", h=HG),
                                           off[:, :].rearrange("p (d h e) -> p d h e", d=2, h=HG),
                                           spread(g[:, DOUT, :, c, :], [2, HG]), ALU.mult))
                    dve.wait_ge(dve_order, issued())
                    step(dve.tensor_tensor(ty[:, 0, :], ty[:, 0, :], ty[:, 1, :], ALU.add))
                else:
                    d = BWD if c == 0 else FWD
                    step(dve.tensor_tensor(heads(ty[:, 0, :]), heads(halves(off)[:, d, :]),
                                           spread(g[:, DOUT, d, c, :], [HG]), ALU.mult))
                dve.wait_ge(dve_order, issued())
                dve.tensor_tensor(ty[:, 0, :], ty[:, 0, :], yd, ALU.add).then_inc(yp_read, 1)
                dve.wait_ge(yp_read, seen(CH * G + c + 1))
                step(dve.tensor_tensor(y[:, c, :], y[:, c, :], ty[:, 0, :], ALU.add))
                dve.wait_ge(dve_order, issued())
                dve.tensor_tensor(y[:, c, :], y[:, c, :], ztok[:, c // 2, (c % 2) * GW:(c % 2 + 1) * GW],
                                  ALU.mult).then_inc(yg_ready, 1)

            def normalise_y(G):
                for part in range(2):
                    dve.wait_ge(rms_done, seen(4 * G + 2 * part + 2))
                    for c in ((0, 1, 2), (3,))[part]:
                        r = dve.tensor_scalar(y[:, c, :], y[:, c, :], rst[:, c:c + 1], None, ALU.mult)
                        if c < CH - 2:
                            step(r)
                        else:
                            r.then_inc(yn_ready, 1)

            def rest_of_y(q, G):
                for i in range(2):
                    dve.wait_ge(yh_done, seen(2 * G + i + 1))
                    dve.scalar_tensor_tensor(out=yl[:, 2 * q + i, :], in0=bank[4 + i][:, :], scalar=gpar[:, q, 24 + i:25 + i],
                                             in1=yh[:, 2 * q + i, :].bitcast(F32), op0=ALU.mult,
                                             op1=ALU.subtract).then_inc(yl_done, 1)

            def rest(dst, z, h, split):
                dve.tensor_tensor(dst, z, h.bitcast(F32), ALU.subtract).then_inc(split, 1)

            def glu(cyc, s, r):
                dve.wait_ge(evac[s + 1], seen(cyc + 1))
                dve.wait_ge(used[s], seen(cyc + 1))
                dve.tensor_tensor(u[:, r, :], bank[s][:, :], sg[:, :], ALU.mult).then_inc(evac[s], 1)

            def add_to_sum(m, z):
                if m == 0:
                    return
                dve.wait_ge(dve_order, issued())
                r = dve.tensor_tensor(sg[:, :], z[:, 0, :] if m == 1 else sg[:, :], z[:, m, :], ALU.add)
                if m == KT - 1:
                    r.then_inc(zsum_ready, 1)
                else:
                    step(r)

            def norm_centre(k, z):
                dve.wait_ge(mean_done, seen(k + 1))
                for m in range(KT):
                    dve.tensor_tensor(z[:, m, :], z[:, m, :], bank[4][:, :], ALU.subtract).then_inc(xc_ready, 1)

            def norm_apply(k, z, hi, lo, lo_sem, off=None):
                dve.wait_ge(std_ready, seen(k + 1))
                step(dve.reciprocal(rstd[:, :], rstd[:, :]))
                dve.wait_ge(dve_order, issued())
                for m in range(KT + 2):
                    if m < KT and off is None:
                        dve.tensor_tensor(z[:, m, :], z[:, m, :], rstd[:, :], ALU.mult).then_inc(zn_ready, 1)
                    elif m < KT:
                        dve.scalar_tensor_tensor(out=z[:, m, :], in0=z[:, m, :], scalar=par[:, off + m:off + m + 1],
                                                 in1=rstd[:, :], op0=ALU.mult, op1=ALU.mult).then_inc(zn_ready, 1)
                    if m >= 2:
                        dve.wait_ge(zh_ready, seen(KT * k + m - 1))
                        if off is None:
                            rest(lo[:, m - 2, :], z[:, m - 2, :], hi[:, m - 2, :], lo_sem)
                        else:
                            b = par[:, off + KT + m - 2:off + KT + m - 1]
                            dve.scalar_tensor_tensor(out=lo[:, m - 2, :], in0=z[:, m - 2, :], scalar=b,
                                                     in1=hi[:, m - 2, :].bitcast(F32), op0=ALU.add,
                                                     op1=ALU.subtract).then_inc(lo_sem, 1)

            dve.wait_ge(consts, CONSTS)
            step(dve.tensor_copy(SLR[:, :], SL[:, :]))
            dve.tensor_copy(SUR[:, :], SU[:, :]).then_inc(tri_ready, 1)
            dve.wait_ge(tri_ready, 1)
            dve.wait_ge(dtw_hi, seen(1))
            rest(dwl[:, :], tmf, dwh[:, :], dtw_lo)
            restart()
            with dve.Fori(0, LAYERS) as L:
                base = L * CYCLES
                for m in range(KT):
                    dve.wait_ge(xh_done, seen(KT * L + m + 1))
                    rest(xl[:, m, :], zb[:, m, :], xh[:, m, :], xl_done)
                dve.wait_ge(par_loaded, 16 * (L + 1))
                dve.wait_ge(dt_done, seen(2 * L + 2))
                bias = par[:, O_DTB:O_DTB + 2 * HEADS].rearrange("p (d h) -> p d h", d=2)
                dch = "p (d c h) -> p d c h"
                dve.tensor_tensor(ty[:, 0, :].rearrange(dch, d=2, c=CH),
                                  bank[6][:, 0:GW].rearrange("p (c d h) -> p d c h", c=CH, d=2),
                                  bias.unsqueeze(2).broadcast_to([P, 2, CH, HEADS]), ALU.add).then_inc(dt_v, 1)
                dve.wait_ge(nega_e, seen(L + 1))
                step(dve.tensor_scalar(nega[:, :], nega[:, :], -1.0, None, ALU.mult))
                dve.wait_ge(dt_e, seen(2 * L + 2))
                e = ty[:, 1, :]
                r_, s_, s2, q_ = (tmf[:, 0:GW], tmf[:, GW:2 * GW], E[:, 0, 0:2, :].rearrange("p a b -> p (a b)"),
                                  E[:, 0, 2:4, :].rearrange("p a b -> p (a b)"))
                step(dve.tensor_scalar(r_, e, 2.0, None, ALU.add))
                dve.wait_ge(dve_order, issued())
                step(dve.reciprocal(r_, r_))
                dve.wait_ge(dve_order, issued())
                step(dve.tensor_tensor(s_, e, r_, ALU.mult))
                dve.wait_ge(dve_order, issued())
                step(dve.tensor_tensor(s2, s_, s_, ALU.mult))
                dve.wait_ge(dve_order, issued())
                step(dve.tensor_scalar(q_, s2, 1.0 / (2 * LOG_TERMS + 1), None, ALU.mult))
                for n in range(LOG_TERMS - 1, 0, -1):
                    dve.wait_ge(dve_order, issued())
                    step(dve.scalar_tensor_tensor(out=q_, in0=q_, scalar=1.0 / (2 * n + 1), in1=s2, op0=ALU.add, op1=ALU.mult))
                dve.wait_ge(dve_order, issued())
                step(dve.scalar_tensor_tensor(out=q_, in0=q_, scalar=1.0, in1=s_, op0=ALU.add, op1=ALU.mult))
                step(dve.tensor_scalar(r_, ty[:, 0, :], 0.0, None, ALU.max))
                dve.wait_ge(dve_order, issued())
                step(dve.scalar_tensor_tensor(out=stepf[:, DTK, :], in0=q_, scalar=2.0, in1=r_, op0=ALU.mult, op1=ALU.add))
                dve.wait_ge(dve_order, issued())
                dve.tensor_tensor(steps[:, ADT], steps[:, DTK],
                                  nega[:, :].rearrange("p (d h) -> p d h", d=2).unsqueeze(2).broadcast_to([P, 2, CH, HEADS]),
                                  ALU.mult).then_inc(ad_ready, 1)
                dve.wait_ge(cum_exp, seen(2 * L + 2))
                step(dve.tensor_tensor(stepf[:, WDEC, :], stepf[:, WDEC, :], stepf[:, DTK, :], ALU.mult))
                restart()
                with dve.Fori(0, PAIRS) as j:
                    c0 = base + j * PAIR_CYCLES
                    G0 = L * GROUPS + j * 2
                    G1 = G0 + 1
                    group_params(0, G0, j * 2)
                    conv(0, G0, 0, [(c0, 0), (c0, 1)])
                    conv(0, G0, 2, [(c0, 2), (c0, 3)])
                    weighted_xs(0, G0, 0)
                    weighted_xs(0, G0, 1)
                    group_params(1, G1, j * 2 + 1)
                    mask_cb(G0)
                    conv(1, G1, 0, [(c0 + 1, 2), (c0 + 1, 3)])
                    weighted_xs(0, G0, 2)
                    mix(0, G0, 0)
                    mix(0, G0, 1)
                    entering(0, G0)
                    mix(0, G0, 2)
                    outputs(0, G0, 0)
                    mix(0, G0, 3)
                    outputs(0, G0, 1)
                    outputs(0, G0, 2)
                    outputs(0, G0, 3)
                    normalise_y(G0)
                    conv(1, G1, 2, [(c0 + 2, 0), (c0 + 2, 1)])
                    rest_of_y(0, G0)
                    weighted_xs(1, G1, 0)
                    weighted_xs(1, G1, 1)
                    mask_cb(G1)
                    mix(1, G1, 0)
                    dve.wait_ge(ua_ready, seen(KT * L + 2 * j))
                    glu(c0 + 3, 0, 0)
                    mix(1, G1, 1)
                    weighted_xs(1, G1, 2)
                    entering(1, G1)
                    mix(1, G1, 2)
                    outputs(1, G1, 0)
                    mix(1, G1, 3)
                    outputs(1, G1, 1)
                    outputs(1, G1, 2)
                    outputs(1, G1, 3)
                    glu(c0 + 3, 2, 1)
                    step(dve.tensor_copy(caw[:, :, :], par[:, bass.ds(O_CAW + j * (2 * CP), 2 * CP)]
                                         .rearrange("p (a b) -> p a b", a=2)))
                    normalise_y(G1)
                    rest_of_y(1, G1)

                    def add_mamba(n):
                        m = (n - 1) // 2
                        if n % 2 == 0 or m >= KT:
                            return
                        c, s = 4 + m // SLOTS, m % SLOTS
                        dve.wait_ge(used[s], seen(c0 + c + 1))
                        dve.tensor_tensor(zb[:, m, :], zb[:, m, :], bank[s][:, :], ALU.add).then_inc(evac[s], 1)

                    dve.wait_ge(zb_zero, seen(L + 1))
                    dve.wait_ge(evac[0], seen(c0 + 4))
                    dve.wait_ge(evac[2], seen(c0 + 4))
                    dve.wait_ge(dve_order, issued())
                    outs = [za[:, bass.ds(2 * j + r, 1), :].rearrange("p a t -> p (a t)") for r in range(2)]
                    taps(outs, [u[:, 0, :], u[:, 1, :]],
                         [caw[:, 0, :], caw[:, 1, :], caw[:, 0, CONV_A:CP], caw[:, 1, CONV_A:CP]], CONV_A, ua_ready,
                         add_mamba)
                    dve.wait_ge(ua_ready, seen(KT * L + 2 * j + 2))
                    restart()
                dve.wait_ge(evac[3], seen(base + C_GATE_A))
                for m in range(KT):
                    add_to_sum(m, za)
                dve.wait_ge(mean_done, seen(NORMS * L + 1))

                def add_square(m):
                    dve.wait_ge(sq_ready, seen(NORMS * KT * L + m + 1))
                    if m > 1:
                        dve.wait_ge(sqa_used, seen(KT * L + m))
                    if m > 0:
                        dve.tensor_tensor(rstd[:, :], u[:, 0, :] if m == 1 else rstd[:, :], u[:, m % 2, :],
                                          ALU.add).then_inc(sqa_used, 2 if m == 1 else 1)

                for m in range(KT + 1):
                    if m < KT:
                        dve.tensor_tensor(za[:, m, :], za[:, m, :], bank[4][:, :], ALU.subtract).then_inc(xc_ready, 1)
                    if m > 0:
                        add_square(m - 1)

                def gate_b(i, s):
                    m = SLOTS * i + s
                    dve.wait_ge(evac[s], seen(base + C_GATE_B + i + 1))
                    dve.tensor_tensor(zb[:, m, :], zb[:, m, :], sg[:, :], ALU.mult).then_inc(gb_ready, 1)

                for s in range(SLOTS):
                    gate_b(0, s)
                norm_apply(NORMS * L + LN_A, za, aah, aal, al_done)
                for s in range(SLOTS):
                    gate_b(1, s)
                restart()
                dve.wait_ge(gb_ready, seen(KT * (L + 1)))
                settle(dve)
                with dve.Fori(0, KT // SLOTS) as i:
                    for s in range(SLOTS):
                        n = KT * L + SLOTS * i + s
                        m = bass.ds(SLOTS * i + s, 1)
                        dve.wait_ge(used[s], seen(base + C_A_OUT + i + 1))
                        dve.tensor_tensor(ge[:, m, :], bank[s][:, :].unsqueeze(1), ge[:, m, :], ALU.mult).then_inc(evac[s], 1)
                        dve.wait_ge(evac[s], seen(base + C_A_OUT + i + 1))
                        dve.tensor_tensor(zb[:, m, :], zb[:, m, :], ge[:, m, :], ALU.add).then_inc(mg_ready, 1)
                        dve.wait_ge(bh_done, seen(n + 1))
                        rest(abl[:, m, :], zb[:, m, :], abh[:, m, :], bl_done)
                dve.wait_ge(al_done, seen(KT * (L + 1)))
                for m in range(KT):
                    s = m % SLOTS
                    dve.wait_ge(used[s], seen(base + C_O + m // SLOTS + 1))
                    dve.scalar_tensor_tensor(out=za[:, m, :], in0=xh[:, m, :].bitcast(F32), scalar=ALPHA,
                                             in1=bank[s][:, :], op0=ALU.mult, op1=ALU.add).then_inc(evac[s], 1)
                    dve.wait_ge(evac[s], seen(base + C_O + m // SLOTS + 1))
                    dve.scalar_tensor_tensor(out=za[:, m, :], in0=xl[:, m, :].bitcast(F32), scalar=ALPHA,
                                             in1=za[:, m, :], op0=ALU.mult, op1=ALU.add).then_inc(z1_ready, 1)
                    dve.wait_ge(z1_ready, seen(KT * L + m + 1))
                    add_to_sum(m, za)
                norm_centre(NORMS * L + LN_1, za)
                norm_apply(NORMS * L + LN_1, za, xh, xl, xl_done, O_LN1)

                def swiglu(c0, count, hi, lo, n0):
                    restart()
                    with dve.Fori(0, count // 2) as i:
                        for r in range(2):
                            dve.wait_ge(fl_done, seen(n0 + 2 * i))
                            dve.wait_ge(evac[2 * r], seen(c0 + i + 1))
                            dve.wait_ge(used[2 * r + 1], seen(c0 + i + 1))
                            dve.tensor_tensor(u[:, r, :], bank[2 * r + 1][:, :], sg[:, :], ALU.mult).then_inc(evac[2 * r + 1], 1)
                        for r in range(2):
                            dve.wait_ge(fh_done, seen(n0 + 2 * i + r + 1))
                            m = bass.ds(2 * i + r, 1)
                            rest(lo[:, m, :], u[:, r, :].unsqueeze(1), hi[:, m, :], fl_done)

                def down(c0, first):
                    with dve.Fori(0, KT // SLOTS) as i:
                        for s in range(SLOTS):
                            m = bass.ds(SLOTS * i + s, 1)
                            b = bank[s][:, :].unsqueeze(1)
                            dve.wait_ge(used[s], seen(c0 + i + 1))
                            dve.wait_ge(evac[s], seen(c0 + i))
                            if first:
                                r = dve.scalar_tensor_tensor(out=zb[:, m, :], in0=za[:, m, :], scalar=ALPHA, in1=b,
                                                             op0=ALU.mult, op1=ALU.add)
                            else:
                                r = dve.tensor_tensor(zb[:, m, :], zb[:, m, :], b, ALU.add)
                            r.then_inc(evac[s], 1)

                f = FT * L
                swiglu(base + C_UP0, KT, aah, aal, f)
                swiglu(base + C_UP1, KT, abh, abl, f + KT)
                dve.wait_ge(zf_ready, seen(2 * KT * (L + 1)))
                settle(dve)
                down(base + C_DOWN0, True)
                swiglu(base + C_UP2, LAST, aah, aal, f + 2 * KT)
                down(base + C_DOWN1, False)
                restart()
                for m in range(KT):
                    s, c = m % SLOTS, base + C_DOWN2 + m // SLOTS
                    dve.wait_ge(used[s], seen(c + 1))
                    dve.wait_ge(evac[s], seen(c))
                    dve.tensor_tensor(zb[:, m, :], zb[:, m, :], bank[s][:, :], ALU.add).then_inc(evac[s], 1)
                    dve.wait_ge(evac[s], seen(c + 1))
                    add_to_sum(m, zb)
                norm_centre(NORMS * L + LN_2, zb)
                norm_apply(NORMS * L + LN_2, zb, xh, xl, xl_done, O_LN2)
                dve.wait_ge(estd_ready, seen(L + 1))
                step(dve.reciprocal(erms[:, :], erms[:, :]))
                dve.wait_ge(dve_order, issued())
                for m in range(KT):
                    dve.scalar_tensor_tensor(out=ge[:, m, :], in0=ge[:, m, :], scalar=par[:, O_PLE + m:O_PLE + m + 1],
                                             in1=erms[:, :], op0=ALU.mult, op1=ALU.mult).then_inc(en_ready, 1)
                dve.wait_ge(dtw_hi, seen(L + 2))
                rest(dwl[:, :], tmf, dwh[:, :], dtw_lo)
                dve.wait_ge(en_ready, seen(KT * (L + 1)))
                restart()
                for m in range(KT):
                    s, n = m % SLOTS, KT * L + m
                    dve.wait_ge(evac[s], seen(base + C_PLE + m // SLOTS + 1))
                    dve.tensor_tensor(ge[:, m, :], ge[:, m, :], sg[:, :], ALU.mult).then_inc(pg_used, 1)
                    dve.wait_ge(pg_used, seen(n + 1))
                    dve.scalar_tensor_tensor(out=zb[:, m, :], in0=zb[:, m, :],
                                             scalar=par[:, O_LN2 + KT + m:O_LN2 + KT + m + 1],
                                             in1=ge[:, m, :], op0=ALU.add, op1=ALU.add).then_inc(xn_ready, 1)
                dve.wait_ge(xn_ready, seen(KT * (L + 2)))


def layout(x, p, w_in, conv_a_w, conv_a_b, ln_a_g, ln_a_b, w_a_out, ssm_conv_w, ssm_conv_b, a_log, dt_bias,
           d_skip, ssm_norm_g, w_b_out, w_o, ln1_g, ln1_b, w_gate_up, w_down, ln2_g, ln2_b, w_ple, ple_norm_g,
           w_ple_gate):
    import numpy as np

    def cols(w, c, rows=slice(None)):
        t = w[rows, c:c + P].reshape(-1, P, P).transpose(1, 0, 2).reshape(P, -1)
        return np.concatenate([t, np.zeros((P, WT - t.shape[1]), t.dtype)], 1)

    Z0 = 2 * D + 2 * D
    XS0 = Z0 + INNER
    B0 = XS0 + INNER
    C0 = B0 + GROUPS * STATE
    DT0 = C0 + GROUPS * STATE
    stream, w_dt, par = [], [], []
    for i in range(LAYERS):
        wi = w_in[i]
        for j in range(PAIRS):
            for g in (2 * j, 2 * j + 1):
                stream += [cols(wi, XS0 + g * GW), cols(wi, XS0 + g * GW + P), cols(wi, B0 + g * STATE), cols(wi, C0 + g * STATE)]
                stream += [cols(wi, Z0 + g * GW), cols(wi, Z0 + g * GW + P)]
            for t in (2 * j, 2 * j + 1):
                stream += [cols(wi, t * P), cols(wi, D + t * P)]
            stream += [cols(w_b_out[i], m * P, slice(j * 2 * GW, (j + 1) * 2 * GW)) for m in range(KT)]
        stream += [cols(wi, 2 * D + m * P) for m in range(KT)]
        stream += [cols(wi, 3 * D + m * P) for m in range(KT)]
        stream += [cols(w_a_out[i], m * P) for m in range(KT)]
        stream += [cols(w_o[i], m * P) for m in range(KT)]

        def up(f):
            return [cols(w_gate_up[i], f * P), cols(w_gate_up[i], FFN + f * P)]

        def down(f, n):
            return [cols(w_down[i], m * P, slice(f * P, (f + n) * P)) for m in range(KT)]

        for f in range(2 * KT):
            stream += up(f)
        stream += down(0, KT)
        for f in range(2 * KT, FT):
            stream += up(f)
        stream += down(KT, KT) + down(2 * KT, LAST)
        stream += [cols(w_ple_gate[i], m * P) for m in range(KT)]
        back = lambda v: np.concatenate([v[HEADS:], v[:HEADS]])
        wd = np.concatenate([wi[:, DT0 + HEADS:DT0 + 2 * HEADS], wi[:, DT0:DT0 + HEADS]], 1)
        w_dt.append(wd.reshape(KT, P, 2 * HEADS).transpose(1, 0, 2).reshape(P, -1))
        tiled = lambda v: v.reshape(-1, P).T
        every = lambda v: np.broadcast_to(v[None, :], (P, v.shape[0]))
        cols_ = []
        for t in range(KT):
            cols_ += [conv_a_w[i][:, t * P:(t + 1) * P].T, tiled(conv_a_b[i])[:, t:t + 1]]
        for g in range(GROUPS):
            at = [g * GW, g * GW + P, INNER + g * STATE, INNER + GROUPS * STATE + g * STATE]
            cols_ += [ssm_conv_w[i][:, a:a + P].T for a in at] + [ssm_conv_b[i][a:a + P, None] for a in at]
            cols_ += [tiled(ssm_norm_g[i])[:, 2 * g:2 * g + 2]]
        for v in (ln_a_g, ln_a_b, ln1_g, ln1_b, ln2_g, ln2_b, ple_norm_g):
            cols_.append(tiled(v[i]))
        cols_ += [every(back(dt_bias[i].reshape(-1))), every(back(a_log[i].reshape(-1))), every(d_skip[i])]
        par.append(np.concatenate(cols_, 1))
    return {
        "x_in": x[0].T.reshape(KT, P, T).transpose(1, 0, 2),
        "p_in": p[:, 0].transpose(0, 2, 1).reshape(LAYERS, 2, P, T).transpose(0, 2, 1, 3),
        "w_stream": np.stack(stream).reshape(ALL_CYCLES, SLOTS, P, WT),
        "w_dt": np.stack(w_dt + w_dt[:1]),
        "w_ple": w_ple.reshape(LAYERS, 2, P, D).transpose(0, 2, 1, 3),
        "par_in": np.stack(par),
    }


def kernel(**inputs):
    import numpy as np
    import concourse.bacc as bacc
    from concourse.bass_utils import run_bass_kernel_spmd

    nc = bacc.Bacc("TRN2", target_bir_lowering=False, num_devices=1)
    arrays = {k: np.ascontiguousarray(v) for k, v in layout(**{k: np.asarray(v) for k, v in inputs.items()}).items()}
    args = [nc.dram_tensor(k, v.shape, mybir.dt.from_np(v.dtype), kind="ExternalInput").ap() for k, v in arrays.items()]
    out = nc.dram_tensor("out", (P, KT, T), F32, kind="ExternalOutput").ap()
    build(nc, *args, out)
    r = run_bass_kernel_spmd(nc, [arrays], core_ids=[0])
    got = r.results[0]["out"]
    return np.ascontiguousarray(got.transpose(2, 1, 0).reshape(1, T, D))
```
